# Optimizing a Trainium2 kernel written in Bass

```python
import jax, jax.numpy as jnp
from jax import lax
import numpy as np

D_MODEL = 1024
BATCH = 1
SEQ = 256
DEPTH = 1
DEC_BATCH = 8
DEC_SEQ = 4
PAST_LEN = 1024
PAGE_SIZE = 128

NORM_EPS = 1e-5
RWKV_HEAD = 64
RWKV_HEADS = D_MODEL // RWKV_HEAD
DECAY_LORA = max(32, int(round(1.8 * D_MODEL ** 0.5 / 32)) * 32)
AAA_LORA = max(32, int(round(1.8 * D_MODEL ** 0.5 / 32)) * 32)
GATE_LORA = max(32, int(round(0.6 * D_MODEL ** 0.8 / 32)) * 32)
GN_EPS = 64e-5
C_RW = 3 * D_MODEL + DECAY_LORA + AAA_LORA + GATE_LORA
ATT_HEAD = 128
ATT_HEADS_PER_GROUP = 4
DILATION_GROUPS = ((128, 1), (512, 4), (2048, 16))
N_GROUPS = len(DILATION_GROUPS)
ATT_DIM = N_GROUPS * ATT_HEADS_PER_GROUP * ATT_HEAD
ATT_OUT = ATT_HEADS_PER_GROUP * ATT_HEAD
ROPE_THETA = 10000.0
P_TOTAL = C_RW + 3 * ATT_DIM + 2 * D_MODEL
N_EXPERTS = 32
TOP_K = 4
D_EXPERT = D_MODEL
SWIGLU_ALPHA = 1.702
SWIGLU_LIMIT = 7.0
MOE_BLOCK = 128

kernel_name = 'hybrid_rwkv7_dilated_swa_moe_step'

F32 = jnp.float32

def rms_norm(x, w, eps=NORM_EPS):
    x32 = x.astype(F32)
    y = x32 * lax.rsqrt(jnp.mean(x32 * x32, axis=-1, keepdims=True) + eps)
    return (y * w.astype(F32)).astype(x.dtype)

def rotary(x, pos):
    e = x.shape[-1]
    inv = ROPE_THETA ** (-jnp.arange(0, e, 2, dtype=F32) / e)
    ang = pos.astype(F32)[:, None] * inv[None, :]
    cos = jnp.cos(ang)[None, :, None, None, :]
    sin = jnp.sin(ang)[None, :, None, None, :]
    x32 = x.astype(F32)
    x1, x2 = x32[..., : e // 2], x32[..., e // 2:]
    return jnp.concatenate([x1 * cos - x2 * sin, x2 * cos + x1 * sin], axis=-1).astype(x.dtype)

def rwkv7_branch(p_rw, prev_rw, s0, mu, w0, w2, a0, a2, g2, k_k, k_a, r_k, lnx_w, lnx_b):
    b, t, _ = p_rw.shape
    h, n, d = RWKV_HEADS, RWKV_HEAD, D_MODEL
    shifted = jnp.concatenate([prev_rw[:, None], p_rw[:, :-1]], axis=1)
    ps = p_rw + (shifted - p_rw) * mu
    r, k, v, xw, xa, xg = jnp.split(ps, [d, 2 * d, 3 * d, 3 * d + DECAY_LORA, 3 * d + DECAY_LORA + AAA_LORA], axis=-1)
    w = -jax.nn.softplus(-(w0 + jnp.tanh(xw) @ w2)) - 0.5
    decay = jnp.exp(-jnp.exp(w.astype(F32)))
    a = jax.nn.sigmoid(a0 + xa @ a2)
    g = jax.nn.sigmoid(xg) @ g2
    kk = (k * k_k).astype(F32).reshape(b, t, h, n)
    kk = kk / jnp.maximum(jnp.sqrt(jnp.sum(kk * kk, axis=-1, keepdims=True)), 1e-12)
    k = k * (1 + (a - 1) * k_a)
    heads = lambda z: z.astype(F32).reshape(b, t, h, n)
    rh, kh, vh, ah, wh = heads(r), heads(k), heads(v), heads(a), heads(decay)
    xs = tuple(jnp.moveaxis(z, 1, 0) for z in (rh, wh, kh, vh, -kk, kk * ah))

    def step(s, inp):
        r_t, w_t, k_t, v_t, a_t, b_t = inp
        sa = jnp.einsum('bhvk,bhk->bhv', s, a_t)
        s = s * w_t[:, :, None, :] + sa[..., None] * b_t[:, :, None, :] + v_t[..., None] * k_t[:, :, None, :]
        return s, jnp.einsum('bhvk,bhk->bhv', s, r_t)

    s_fin, y = lax.scan(step, s0.astype(F32), xs)
    y = jnp.moveaxis(y, 0, 1)
    mean = jnp.mean(y, axis=-1, keepdims=True)
    var = jnp.mean(jnp.square(y - mean), axis=-1, keepdims=True)
    y = ((y - mean) * lax.rsqrt(var + GN_EPS)).reshape(b, t, d) * lnx_w.astype(F32) + lnx_b.astype(F32)
    bonus = jnp.sum(rh * kh * r_k.astype(F32), axis=-1, keepdims=True) * vh
    y = y + bonus.reshape(b, t, d)
    return (y * g.astype(F32)).astype(p_rw.dtype), s_fin

def band_dilated_attention(q, k, v, dil, nw):
    b, t, h, e = q.shape
    blk = nw
    unit = dil * blk
    tp = -(-t // unit) * unit
    nb = tp // unit
    pad = ((0, 0), (0, tp - t), (0, 0), (0, 0))

    def blocks(z):
        return jnp.pad(z, pad).reshape(b, nb, blk, dil, h, e)

    def with_prev(z):
        prev = jnp.pad(z[:, :-1], ((0, 0), (1, 0), (0, 0), (0, 0), (0, 0), (0, 0)))
        return jnp.concatenate([prev, z], axis=2)

    qb = blocks(q)
    kb, vb = with_prev(blocks(k)), with_prev(blocks(v))
    s = jnp.einsum('bnqrhe,bnkrhe->bnrhqk', qb, kb, preferred_element_type=F32) * (e ** -0.5)
    qi = jnp.arange(blk)[:, None]
    ki = jnp.arange(2 * blk)[None, :]
    off = qi + blk - ki
    valid = (off >= 0) & (off <= nw)
    has_rows = (jnp.arange(nb)[:, None, None] > 0) | (ki >= blk)[None]
    mask = valid[None] & has_rows
    s = jnp.where(mask[None, :, None, None], s, -jnp.inf)
    m = jnp.max(s, axis=-1, keepdims=True)
    p = jnp.exp(s - m)
    den = jnp.sum(p, axis=-1)
    o = jnp.einsum('bnrhqk,bnkrhe->bnrhqe', p, vb.astype(F32)) / den[..., None]
    lse = m[..., 0] + jnp.log(den)
    o = jnp.transpose(o, (0, 1, 4, 2, 3, 5)).reshape(b, tp, h, e)[:, :t]
    lse = jnp.transpose(lse, (0, 1, 4, 2, 3)).reshape(b, tp, h)[:, :t]
    return o, lse

def gather_dilated_attention(q, kv_all, dil, nw):
    b, t, h, e = q.shape
    past = kv_all.shape[1] - t
    idx = past + jnp.arange(t)[:, None] - dil * jnp.arange(nw + 1)[None, :]
    valid = idx >= 0
    g = jnp.take(kv_all, jnp.maximum(idx, 0), axis=1)
    s = jnp.einsum('bthe,btjhe->bthj', q, g[:, :, :, 0], preferred_element_type=F32) * (e ** -0.5)
    s = jnp.where(valid[None, :, None, :], s, -jnp.inf)
    m = jnp.max(s, axis=-1, keepdims=True)
    p = jnp.exp(s - m)
    den = jnp.sum(p, axis=-1)
    o = jnp.einsum('bthj,btjhe->bthe', p, g[:, :, :, 1].astype(F32)) / den[..., None]
    return o, m[..., 0] + jnp.log(den)

def clamped_swiglu(hdn):
    glu, lin = hdn[..., ::2], hdn[..., 1::2]
    glu = jnp.minimum(glu, SWIGLU_LIMIT)
    lin = jnp.clip(lin, -SWIGLU_LIMIT, SWIGLU_LIMIT)
    return glu * jax.nn.sigmoid(SWIGLU_ALPHA * glu) * (lin + 1)

def moe_ffn(xt, router_w, router_b, w1, b1, w2, b2):
    n, d = xt.shape
    logits = (xt @ router_w).astype(F32) + router_b.astype(F32)
    top_val, top_idx = lax.top_k(logits, TOP_K)
    gates = jax.nn.softmax(top_val, axis=-1)
    nk = n * TOP_K
    flat_e = top_idx.reshape(nk)
    flat_tok = jnp.repeat(jnp.arange(n, dtype=jnp.int32), TOP_K)
    flat_g = gates.reshape(nk)
    order = jnp.argsort(flat_e)
    se, stok, sg = flat_e[order], flat_tok[order], flat_g[order]
    counts = jnp.bincount(flat_e, length=N_EXPERTS)
    starts = jnp.cumsum(counts) - counts
    blocks_e = (counts + MOE_BLOCK - 1) // MOE_BLOCK
    block_end = jnp.cumsum(blocks_e)
    row_start = (block_end - blocks_e) * MOE_BLOCK
    dest = row_start[se] + jnp.arange(nk, dtype=jnp.int32) - starts[se]
    n_blocks = -(-nk // MOE_BLOCK) + N_EXPERTS
    rows = n_blocks * MOE_BLOCK
    tok_buf = jnp.zeros((rows,), jnp.int32).at[dest].set(stok)
    gate_buf = jnp.zeros((rows,), F32).at[dest].set(sg)
    blk_expert = jnp.minimum(jnp.searchsorted(block_end, jnp.arange(n_blocks), side='right'), N_EXPERTS - 1)
    xb = xt[tok_buf].reshape(n_blocks, MOE_BLOCK, d)

    def expert_block(args):
        xblk, e = args
        return clamped_swiglu(xblk @ w1[e] + b1[e]) @ w2[e] + b2[e]

    yb = lax.map(expert_block, (xb, blk_expert))
    contrib = yb.reshape(rows, d).astype(F32) * gate_buf[:, None]
    return jnp.zeros((n, d), F32).at[tok_buf].add(contrib)

def layer_forward(x, pos, shift_prev, wkv0, kv_caches, lw):
    b, t, _ = x.shape
    xn = rms_norm(x, lw['attn_norm_w'])
    w_in = lw['w_in']
    proj = xn @ w_in
    prev_rw = shift_prev.astype(x.dtype) @ w_in[:, :C_RW]
    p_rw = proj[..., :C_RW]
    p_att = proj[..., C_RW:C_RW + 3 * ATT_DIM]
    p_gate = proj[..., C_RW + 3 * ATT_DIM:]

    y_rw, s_fin = rwkv7_branch(p_rw, prev_rw, wkv0, lw['rw_mu'], lw['rw_w0'], lw['rw_w2'], lw['rw_a0'],
                               lw['rw_a2'], lw['rw_g2'], lw['rw_kk'], lw['rw_ka'], lw['rw_rk'],
                               lw['rw_lnx_w'], lw['rw_lnx_b'])

    q, k, v = jnp.split(p_att, 3, axis=-1)
    hshape = (b, t, N_GROUPS, ATT_HEADS_PER_GROUP, ATT_HEAD)
    q = rotary(rms_norm(q.reshape(hshape), lw['q_norm_w']), pos)
    k = rotary(rms_norm(k.reshape(hshape), lw['k_norm_w']), pos)
    v = v.reshape(hshape)
    outs, lses, new_kv = [], [], []
    for gi, (window, dil) in enumerate(DILATION_GROUPS):
        nw = window // dil
        kv_new = jnp.stack([k[:, :, gi], v[:, :, gi]], axis=2)
        if kv_caches is None:
            o, lse = band_dilated_attention(q[:, :, gi], k[:, :, gi], v[:, :, gi], dil, nw)
            new_kv.append(kv_new[:, t - min(window, t):])
        else:
            buf_len = kv_caches[gi].shape[1]
            kv_all = jnp.concatenate([kv_caches[gi].astype(x.dtype), kv_new], axis=1)
            o, lse = gather_dilated_attention(q[:, :, gi], kv_all, dil, nw)
            new_kv.append(kv_all[:, kv_all.shape[1] - buf_len:])
        outs.append(o)
        lses.append(lse)
    alpha = jax.nn.softmax(jnp.stack(lses, axis=0), axis=0)
    o_att = jnp.sum(alpha[..., None] * jnp.stack(outs, axis=0), axis=0).reshape(b, t, ATT_OUT).astype(x.dtype)

    gate_a, gate_b = jnp.split(jax.nn.sigmoid(p_gate), 2, axis=-1)
    w_br = lw['w_br']
    merged = gate_a * (y_rw @ w_br[:D_MODEL]) + gate_b * (o_att @ w_br[D_MODEL:])
    h = x + merged @ lw['w_out']
    hn = rms_norm(h, lw['ffn_norm_w'])
    ffn = moe_ffn(hn.reshape(b * t, D_MODEL), lw['router_w'], lw['router_b'], lw['moe_w1'], lw['moe_b1'],
                  lw['moe_w2'], lw['moe_b2'])
    y = (h.astype(F32) + ffn.reshape(b, t, D_MODEL)).astype(x.dtype)
    return y, xn[:, -1], s_fin.astype(x.dtype), new_kv

def setup_inputs(seed: int = 0) -> dict:
    key = jax.random.key(seed)
    ks = jax.random.split(key, 32)
    nrm = lambda kk, shape, s: s * jax.random.normal(kk, shape, F32)
    hg, hd = ATT_HEADS_PER_GROUP, ATT_HEAD
    w1_w, w2_w, w3_w = (DILATION_GROUPS[0][0], DILATION_GROUPS[1][0], DILATION_GROUPS[2][0])
    return {
        'x_prompt': nrm(ks[0], (BATCH, SEQ, D_MODEL), 1.0),
        'x_sample': nrm(ks[1], (DEC_BATCH, DEC_SEQ, D_MODEL), 1.0),
        'state_wkv': nrm(ks[2], (DEPTH, DEC_BATCH, RWKV_HEADS, RWKV_HEAD, RWKV_HEAD), 0.3),
        'state_shift': nrm(ks[3], (DEPTH, DEC_BATCH, D_MODEL), 1.0),
        'cache_kv_w128': nrm(ks[4], (DEPTH, DEC_BATCH, min(w1_w, PAST_LEN), 2, hg, hd), 1.0),
        'cache_kv_w512': nrm(ks[5], (DEPTH, DEC_BATCH, min(w2_w, PAST_LEN), 2, hg, hd), 1.0),
        'cache_kv_w2048': nrm(ks[6], (DEPTH, DEC_BATCH, min(w3_w, PAST_LEN), 2, hg, hd), 1.0),
        'attn_norm_w': 1.0 + nrm(ks[7], (DEPTH, D_MODEL), 0.02),
        'w_in': nrm(ks[8], (DEPTH, D_MODEL, P_TOTAL), D_MODEL ** -0.5),
        'rw_mu': jax.random.uniform(ks[9], (DEPTH, C_RW), F32, 0.0, 1.0),
        'rw_w0': jax.random.uniform(ks[10], (DEPTH, D_MODEL), F32, -6.0, -0.5),
        'rw_w2': nrm(ks[11], (DEPTH, DECAY_LORA, D_MODEL), 0.1),
        'rw_a0': nrm(ks[12], (DEPTH, D_MODEL), 0.1),
        'rw_a2': nrm(ks[13], (DEPTH, AAA_LORA, D_MODEL), 0.1),
        'rw_g2': nrm(ks[14], (DEPTH, GATE_LORA, D_MODEL), GATE_LORA ** -0.5),
        'rw_kk': 0.85 + nrm(ks[15], (DEPTH, D_MODEL), 0.05),
        'rw_ka': 1.0 + nrm(ks[16], (DEPTH, D_MODEL), 0.05),
        'rw_rk': nrm(ks[17], (DEPTH, RWKV_HEADS, RWKV_HEAD), 0.1),
        'rw_lnx_w': 1.0 + nrm(ks[18], (DEPTH, D_MODEL), 0.02),
        'rw_lnx_b': nrm(ks[19], (DEPTH, D_MODEL), 0.02),
        'q_norm_w': 1.0 + nrm(ks[20], (DEPTH, ATT_HEAD), 0.02),
        'k_norm_w': 1.0 + nrm(ks[21], (DEPTH, ATT_HEAD), 0.02),
        'w_br': nrm(ks[22], (DEPTH, D_MODEL + ATT_OUT, D_MODEL), (D_MODEL + ATT_OUT) ** -0.5),
        'w_out': nrm(ks[23], (DEPTH, D_MODEL, D_MODEL), D_MODEL ** -0.5),
        'ffn_norm_w': 1.0 + nrm(ks[24], (DEPTH, D_MODEL), 0.02),
        'router_w': nrm(ks[25], (DEPTH, D_MODEL, N_EXPERTS), D_MODEL ** -0.5),
        'router_b': nrm(ks[26], (DEPTH, N_EXPERTS), 0.01),
        'moe_w1': nrm(ks[27], (DEPTH, N_EXPERTS, D_MODEL, 2 * D_EXPERT), D_MODEL ** -0.5),
        'moe_b1': nrm(ks[28], (DEPTH, N_EXPERTS, 2 * D_EXPERT), 0.01),
        'moe_w2': nrm(ks[29], (DEPTH, N_EXPERTS, D_EXPERT, D_MODEL), D_EXPERT ** -0.5),
        'moe_b2': nrm(ks[30], (DEPTH, N_EXPERTS, D_MODEL), 0.01),
    }

def reference(x_prompt, x_sample, state_wkv, state_shift, cache_kv_w128, cache_kv_w512, cache_kv_w2048,
              attn_norm_w, w_in, rw_mu, rw_w0, rw_w2, rw_a0, rw_a2, rw_g2, rw_kk, rw_ka, rw_rk,
              rw_lnx_w, rw_lnx_b, q_norm_w, k_norm_w, w_br, w_out, ffn_norm_w, router_w, router_b,
              moe_w1, moe_b1, moe_w2, moe_b2):
    bp, tp, _ = x_prompt.shape
    ts = x_sample.shape[1]
    pos_p = jnp.arange(tp, dtype=jnp.int32)
    pos_s = PAST_LEN + jnp.arange(ts, dtype=jnp.int32)
    hp, hs = x_prompt, x_sample
    p_wkv, p_shift, s_wkv, s_shift = [], [], [], []
    p_kv = [[] for _ in DILATION_GROUPS]
    s_kv = [[] for _ in DILATION_GROUPS]
    for l in range(DEPTH):
        lw = {'attn_norm_w': attn_norm_w[l], 'w_in': w_in[l], 'rw_mu': rw_mu[l], 'rw_w0': rw_w0[l],
              'rw_w2': rw_w2[l], 'rw_a0': rw_a0[l], 'rw_a2': rw_a2[l], 'rw_g2': rw_g2[l], 'rw_kk': rw_kk[l],
              'rw_ka': rw_ka[l], 'rw_rk': rw_rk[l], 'rw_lnx_w': rw_lnx_w[l], 'rw_lnx_b': rw_lnx_b[l],
              'q_norm_w': q_norm_w[l], 'k_norm_w': k_norm_w[l], 'w_br': w_br[l], 'w_out': w_out[l],
              'ffn_norm_w': ffn_norm_w[l], 'router_w': router_w[l], 'router_b': router_b[l],
              'moe_w1': moe_w1[l], 'moe_b1': moe_b1[l], 'moe_w2': moe_w2[l], 'moe_b2': moe_b2[l]}
        zero_shift = jnp.zeros((bp, D_MODEL), x_prompt.dtype)
        zero_wkv = jnp.zeros((bp, RWKV_HEADS, RWKV_HEAD, RWKV_HEAD), F32)
        hp, sh_p, wkv_p, kv_p = layer_forward(hp, pos_p, zero_shift, zero_wkv, None, lw)
        hs, sh_s, wkv_s, kv_s = layer_forward(hs, pos_s, state_shift[l], state_wkv[l],
                                              (cache_kv_w128[l], cache_kv_w512[l], cache_kv_w2048[l]), lw)
        p_wkv.append(wkv_p)
        p_shift.append(sh_p)
        s_wkv.append(wkv_s)
        s_shift.append(sh_s)
        for gi in range(N_GROUPS):
            p_kv[gi].append(kv_p[gi])
            s_kv[gi].append(kv_s[gi])
    return (hp, hs,
            jnp.stack(p_wkv), jnp.stack(p_shift), jnp.stack(p_kv[0]), jnp.stack(p_kv[1]), jnp.stack(p_kv[2]),
            jnp.stack(s_wkv), jnp.stack(s_shift), jnp.stack(s_kv[0]), jnp.stack(s_kv[1]), jnp.stack(s_kv[2]))


_drawn_inputs = setup_inputs


def setup_inputs(seed=0):
    import zlib

    import numpy as np

    out = dict(_drawn_inputs(seed))
    spreads = {}
    factors = {'q_norm_w': 5.575,
     'k_norm_w': 3.961,
     'moe_b1': 8.0,
     'moe_b2': 8.0,
     'rw_lnx_b': 2.683,
     'rw_lnx_w': 2.864}
    for name, (base, spread) in spreads.items():
        noise = np.random.default_rng([zlib.crc32(name.encode()), seed]).standard_normal(out[name].shape)
        drawn = base * np.exp(spread * noise) if base else spread * noise
        out[name] = __import__('jax').numpy.asarray(drawn.astype(out[name].dtype))
    for name, factor in factors.items():
        out[name] = (out[name] * factor).astype(out[name].dtype)
    return out
```

```python
from contextlib import ExitStack

import concourse.bass as bass
from concourse import mybir

F32 = mybir.dt.float32
I32 = mybir.dt.int32
U32 = mybir.dt.uint32
ALU = mybir.AluOpType
ACT = mybir.ActivationFunctionType
AX = mybir.AxisListType

D = 1024
SEQ = 256
NB = 8
TS = 4
NSMP = NB * TS
NTOK = SEQ + NSMP
KC = D // 128
XC = 1 + SEQ + NB * (TS + 1)
SMP0 = 1 + SEQ
HR, NR = 16, 64
LORA = 64
GLORA = 160
C_RW = 3 * D + 2 * LORA + GLORA
NM_RW = -(-C_RW // 128)
NG, HG, E = 3, 4, 128
GW = HG * E
ATT = NG * GW
WIN = ((128, 1), (512, 4), (2048, 16))
CACHE = (128, 512, 1024)
P_TOTAL = C_RW + 3 * ATT + 2 * D
NEXP = 32
CAP = 64
LEVELS = -(-NTOK // CAP)
NEG = -1.0e30
TILES = ((0, 128), (128, 128), (256, 32))
L = 64
NCH = SEQ // L
KAPPA = 0.6065306597126334

_off, _n = {}, 0
for _name, _w in (("ident", 128), ("blockones", 128), ("prefix", 128), ("ones", 128),
                  ("cos", 3 * 64), ("sin", 3 * 64), ("pm0", 384), ("pm1", 768), ("sm", 480),
                  ("tri2", 128), ("tril", 64), ("eye2", 64), ("iota64", 128), ("iota32", 32), ("keep", 512), ("eps", 4)):
    _off[_name] = (_n, _n + _w)
    _n += _w
NCONST = _n
COFF = _off


def host_constants():
    import numpy as np
    c = np.zeros((128, NCONST), np.float32)

    def put(name, a):
        o = COFF[name]
        c[:a.shape[0], o[0]:o[1]] = a.reshape(a.shape[0], -1)

    p = np.arange(128)
    put("ident", np.eye(128))
    put("blockones", (p[:, None] // 64 == p[None] // 64) * 1.0)
    put("prefix", (p[:, None] <= p[None]) * 1.0)
    put("ones", np.ones((128, 128)))
    pos = np.zeros(3 * 128, np.float32)
    pos[:SEQ] = np.arange(SEQ)
    pos[SEQ:NTOK] = 1024 + np.arange(NSMP) % TS
    inv = (np.float32(10000.0) ** (-np.arange(0, E, 2, dtype=np.float32) / E)).astype(np.float32)
    ang = (pos[:, None] * inv[None]).astype(np.float32)
    put("cos", np.cos(ang).reshape(3, 128, 64).transpose(1, 0, 2))
    put("sin", np.sin(ang).reshape(3, 128, 64).transpose(1, 0, 2))

    def band(q, k, window, dil):
        off = q[:, None] - k[None]
        return np.where((off >= 0) & (off <= window) & (off % dil == 0), 0.0, NEG)

    put("pm0", np.concatenate([band(p, p, *w) for w in WIN], 1))
    put("pm1", np.concatenate([band(p + 128, np.arange(256), *w) for w in WIN], 1))
    b, t = (p % 32) // TS, p % TS
    sm = np.zeros((128, 480), np.float32)
    sm[:, 0:128] = np.where(p[None] >= t[:, None], 0.0, NEG)
    sm[:, 256:384] = np.where(p[None] // 64 == t[:, None] % 2, 0.0, NEG)
    kb, kt = np.arange(NSMP) // TS, np.arange(NSMP) % TS
    for g, (window, dil) in enumerate(WIN):
        off = t[:, None] - kt[None]
        ok = (b[:, None] == kb[None]) & (off >= 0) & (off % dil == 0)
        sm[:, 384 + 32 * g:416 + 32 * g] = np.where(ok, 0.0, NEG)
    put("sm", sm)
    i, tt = p % 64, np.arange(64)
    put("tri2", np.concatenate([(i[:, None] < tt[None]) * 1.0, (i[:, None] <= tt[None]) * 1.0], 1))
    put("iota64", np.broadcast_to(np.arange(128) % 64, (128, 128)))
    put("iota32", np.broadcast_to(np.arange(32), (128, 32)))
    put("tril", (tt[None] < i[:, None]) * 1.0)
    put("eye2", (tt[None] == i[:, None]) * 1.0)
    put("keep", np.broadcast_to((np.arange(512) % L != 0) * 1.0, (128, 512)))
    put("eps", np.broadcast_to(np.array([1e-5, 64e-5, 1.0, 0.0]), (128, 4)))
    return c


INS = ["x_prompt", "x_sample", "state_wkv", "state_shift", "cache_kv_w128", "cache_kv_w512",
       "cache_kv_w2048", "attn_norm_w", "w_in", "rw_mu", "rw_w0", "rw_w2", "rw_a0", "rw_a2", "rw_g2",
       "rw_kk", "rw_ka", "rw_rk", "rw_lnx_w", "rw_lnx_b", "q_norm_w", "k_norm_w", "w_br", "w_out",
       "ffn_norm_w", "router_w", "router_b", "moe_w1", "moe_b1", "moe_w2", "moe_b2"]
OUTS = [(1, SEQ, D), (NB, TS, D), (1, 1, HR, NR, NR), (1, 1, D),
        (1, 1, 128, 2, HG, E), (1, 1, SEQ, 2, HG, E), (1, 1, SEQ, 2, HG, E),
        (1, NB, HR, NR, NR), (1, NB, D),
        (1, NB, 128, 2, HG, E), (1, NB, 512, 2, HG, E), (1, NB, 1024, 2, HG, E)]


def build(nc, A, consts, O):
    ctx = ExitStack()
    with ctx:
        def sb(name, shape, dt=F32):
            return ctx.enter_context(nc.sbuf_tensor(name, shape, dt))

        def sem(name):
            return ctx.enter_context(nc.semaphore(name))

        def row(ap, parts):
            n = ap.shape[-1]
            return bass.AP(tensor=ap.tensor, offset=ap.offset, ap=[[0, parts], [1, n]])

        B = [ctx.enter_context(nc.psum_tensor(f"bank{i}", [128, 512], F32)) for i in range(8)]

        NSLOT, SLOT = 6, 2048 
        ring = sb("ring", [128, NSLOT, SLOT])
        C = sb("C", [128, NCONST])

        def const(name, rows=128):
            return C[0:rows, COFF[name][0]:COFF[name][1]]

        ident, blockones, ones = const("ident"), const("blockones"), const("ones")
        xT = sb("xT", [128, KC, XC])
        xTs = sb("xTs", [128, KC, NSMP])

        small = sb("small", [128, 64])
        POOL = 33500
        pool = sb("pool", [128, POOL])

        def span(at, *shape):
            n = 1
            for s in shape:
                n *= s
            assert at + n <= POOL, (at, n)
            v = pool[:, at:at + n]
            if len(shape) == 2:
                v = v.rearrange("p (a b) -> p a b", a=shape[0])
            if len(shape) == 3:
                v = v.rearrange("p (a b c) -> p a b c", a=shape[0], b=shape[1])
            return v

        x_sb = span(0, 3, D)
        xsh = span(3072, D)
        nw = span(4096, D)
        sqx = span(5120, D)
        qT = span(0, NG * HG, NTOK)
        kT = span(3456, NG * HG, NTOK)
        v_sb = span(6912, 3, ATT)
        raw = span(11520, 2, GW)
        roped = span(12544, 2, GW)
        rt1 = span(13568, GW)
        rt2 = span(14080, GW)
        tabs = span(14592, 2, 3, 256)
        wqk = span(16128, 2, E)
        sqh = span(16384, HG, E)
        pP = (span(11520, 384), span(11904, 768))
        pPT = (span(12672, 3, 128), span(13056, 6, 128))
        kTb = span(13824, 2, 7, 128)
        sP, sPT = span(15616, 480), span(16096, 3, 128)
        sPTn = span(11520, 3, 128)
        zb = span(31584, 2, HG, 7 * 32)
        osm = span(16480, 128)
        amax = small[:, 32:34]
        anmx, aden, arden = small[:, 34:36], small[:, 36:38], small[:, 38:40]
        tokS = span(0, 6, D)
        vec = span(6144, 6 * TS, NR)
        Sh = span(0, 32, NR)
        stA, stP = span(2048, 32, NR), span(4096, 32, NR)
        ysm = span(7680, TS, NR)
        tokY = span(0, D)
        sa_ = small[:, 0:32]
        H2 = 2 * NR
        AR = span(7936, KC, H2)
        bh, kh = span(8960, KC, NR), span(9472, KC, NR)
        MQ, KQ = span(9984, KC, H2), span(11008, KC, H2)
        Nn = span(12032, KC, NR)
        tA, tB, tC, tD, tE = [span(12544 + 512 * i, KC, NR) for i in range(5)]
        Rr, Uu, ST = [span(15104 + 512 * i, KC, NR) for i in range(3)]
        bTm, kTm, vTm = [span(31584 + 512 * i, KC, NR) for i in range(3)]
        tF = C[:, COFF["pm1"][0]:COFF["pm1"][0] + 512].rearrange("p (a b) -> p a b", a=KC)
        wl = sb("wl", [128, KC])
        gT = span(0, 2 * KC, NTOK)
        gsq, grs, gpr = [span(4608 + i * 2304, KC, NTOK) for i in range(3)]
        g2w = span(11520, 2, D)
        mT = span(13568, KC, NTOK)
        acc = span(23808, 3, D)
        fw = span(26880, D)
        rwt = span(27904, KC, NEXP)
        rb = span(28160, NEXP)
        hn = span(16896, 3, D)
        hnT = span(0, KC, NTOK)
        t0 = 31584
        lg, mk, gsel, posm = span(t0, 3, NEXP), span(t0 + 96, 3, NEXP), span(t0 + 192, 3, NEXP), span(t0 + 288, 3, NEXP + 1)
        m8, idxf, g4 = span(t0 + 400, 3, 8), span(t0 + 424, 3, 8), span(t0 + 448, 3, 4)
        idx = span(t0 + 464, 3, 8).bitcast(U32)
        most = span(t0 + 488, 8)
        most_i = span(t0 + 496, 8).bitcast(I32)
        nm8 = span(t0 + 504, 8)
        m0 = 2304
        selT, selG = span(m0, 3, 128), span(m0 + 384, 3, 128)
        selGT = span(m0 + 768, 384)
        xe, xeT = span(m0 + 1152, 512), span(m0 + 1664, 4, 2, CAP)
        glu, lin, sgm, act_ = [span(m0 + 2176 + 512 * i, 512) for i in range(4)]
        actT = span(m0 + 4224, 4, 2, CAP)
        ysb = span(m0 + 4736, 512)
        b1r = span(m0 + 5248, 2, 512)
        b2w = span(m0 + 6272, D)
        gselT = span(t0 + 512, NTOK)
        R0 = 16896
        NA = KC * NTOK
        rT, kR, vR, sW, aR, kkn = [span(R0 + i * NA, KC, NTOK) for i in range(6)]
        lo = span(R0 + 6 * NA, 3, NTOK)
        praw = span(R0 + 6 * NA + 864, 2, XC)
        pdiff = span(R0 + 6 * NA + 864 + 2 * XC, XC)
        w2a2 = span(R0 + 6 * NA + 864 + 3 * XC, D)
        sqk = span(6912, KC, NTOK)
        knb = span(6912 + NA, KC, NTOK)
        prm = span(14592, 128)
        NPRM = NM_RW + 7 * KC
        prmT = sb("prmT", [128, NPRM + KC])
        MU, W0, A0, PKK, PKA, PRK, LNW, LNB = 0, *[NM_RW + KC * i for i in range(7)]
        ONEKA = NPRM
        oT = sb("oT", [128, HG, NTOK])

        nsq, rms, rstd = small[:, 0:3], small[:, 3:6], small[:, 6:9]
        hss = small[:, 12:20].rearrange("p (i h) -> p i h", i=2)
        hms = small[:, 20:28].rearrange("p (i h) -> p i h", i=2)
        hrs = small[:, 28:32]
        eps5, eps64 = const("eps")[:, 0:1], const("eps")[:, 1:2]

        c_in = sem("c_in")
        x_in = sem("x_in")
        sh_in = sem("sh_in")
        nw_in = sem("nw_in")
        qkw_in = sem("qkw_in")
        slot_full = [sem(f"slot_full{i}") for i in range(NSLOT)]
        rw_psum = sem("rw_psum")
        gate_psum = sem("gate_psum")
        s_psum, s_read, s_exp, p_ready = sem("s_psum"), sem("s_read"), sem("s_exp"), sem("p_ready")
        pt_psum, pt_out, pv_psum, o_out = sem("pt_psum"), sem("pt_out"), sem("pv_psum"), sem("o_out")
        z_ready = sem("z_ready")
        kt_psum, kt_out_a, kt_out_v = sem("kt_psum"), sem("kt_out_a"), sem("kt_out_v")
        ss_head, ss_exp, ss_read = sem("ss_head"), sem("ss_exp"), sem("ss_read")
        spt_psum, spt_out, sv_psum = sem("spt_psum"), sem("spt_out"), sem("sv_psum")
        so_read, so_psum, so_out = sem("so_read"), sem("so_psum"), sem("so_out")
        v_stored = sem("v_stored")
        tk_psum, tk_out, tk_written, vec_in = sem("tk_psum"), sem("tk_out"), sem("tk_written"), sem("vec_in")
        sh_load, sh_saved = sem("sh_load"), sem("sh_saved")
        st_zero = sem("st_zero")
        st_a, st_p, st_done = sem("st_a"), sem("st_p"), sem("st_done")
        ys_written, ys_in, ys_psum, ys_out = sem("ys_written"), sem("ys_in"), sem("ys_psum"), sem("ys_out")
        cum_ready, exps_ready, ops_ready = sem("cum_ready"), sem("exps_ready"), sem("ops_ready")
        ch_psum, ch_act, ch_dve = sem("ch_psum"), sem("ch_act"), sem("ch_dve")
        pst_saved = sem("pst_saved")
        gate_out, gnm_psum, gn_centred = sem("gate_out"), sem("gnm_psum"), sem("gn_centred")
        gn_sq, gnv_psum, gn_rs = sem("gn_sq"), sem("gnv_psum"), sem("gn_rs")
        bon_ready, bon_psum, bon_out = sem("bon_ready"), sem("bon_psum"), sem("bon_out")
        gg_psum, y_ready, g2_in, rest_in = sem("gg_psum"), sem("y_ready"), sem("g2_in"), sem("rest_in")
        br_psum, merged = sem("br_psum"), sem("merged")
        wo_psum, h_ready, h_rms, hn_ready = sem("wo_psum"), sem("h_ready"), sem("h_rms"), sem("hn_ready")
        hnt_psum, hnt_out, lg_psum, lg_max, lg_exp = sem("hnt_psum"), sem("hnt_out"), sem("lg_psum"), sem("lg_max"), sem("lg_exp")
        mk_ready, pos_psum, routed = sem("mk_ready"), sem("pos_psum"), sem("routed")
        moe_used, b1_full, b2_in = sem("moe_used"), sem("b1_full"), sem("b2_in")
        gt_psum, gt_out, b2_psum, b2_added = sem("gt_psum"), sem("gt_out"), sem("b2_psum"), sem("b2_added")
        sel_ready, selg_ready, xe_psum, xe_out = sem("sel_ready"), sem("selg_ready"), sem("xe_psum"), sem("xe_out")
        xet_psum, xet_out, glu_min, sg_ready = sem("xet_psum"), sem("xet_out"), sem("glu_min"), sem("sg_ready")
        act_done, at_psum, at_out = sem("act_done"), sem("at_psum"), sem("at_out")
        sgt_psum, sgt_out, ye_psum, ye_out = sem("sgt_psum"), sem("sgt_out"), sem("ye_psum"), sem("ye_out")
        sc_psum, sc_added, y_done, y_saved = sem("sc_psum"), sem("sc_added"), sem("y_done"), sem("y_saved")
        sgt_zero = sem("sgt_zero")
        squares = sem("squares")
        xn_ready = sem("xn_ready")
        xn_stored = sem("xn_stored")
        xt_psum = sem("xt_psum")
        xt_ready = sem("xt_ready")
        zero_col = sem("zero_col")
        prm_zero, prm_in, prm_psum, prm_ready = sem("prm_zero"), sem("prm_in"), sem("prm_psum"), sem("prm_ready")
        w2a2_in = sem("w2a2_in")
        rw_raw, rw_mixed = sem("rw_raw"), sem("rw_mixed")
        lora_in, lora_psum, lora_out = sem("lora_in"), sem("lora_psum"), sem("lora_out")
        sqk_ready, sqk_psum, knorm = sem("sqk_ready"), sem("sqk_psum"), sem("knorm")
        rw_arrays = sem("rw_arrays")
        proj_psum = sem("proj_psum")
        proj_out = sem("proj_out")
        rope_done = sem("rope_done")
        qk_psum = sem("qk_psum")
        qk_out = sem("qk_out")
        k_stored = [sem("k_stored0"), sem("k_stored1")]
        out_dma = sem("out_dma")
        n_out = [0]

        def stored(dma):
            dma.then_inc(out_dma, 16)
            n_out[0] += 1

        w_in = A["w_in"][0].rearrange("(k p) n -> p k n", p=128)
        w_br = A["w_br"][0].rearrange("(k p) n -> p k n", p=128)
        w_out = A["w_out"][0].rearrange("(k p) n -> p k n", p=128)
        loads = []

        def slot(n, width=None):
            v = ring[:, n % NSLOT, :]
            return v if width is None else v.rearrange("p (k n) -> p k n", n=width)

        def add_load(parts, used):
            loads.append((parts, used))

        def w_in_cols(c0, width, used):
            for half in range(2):
                n = len(loads)
                add_load([(slot(n, GW)[:, :, 0:width], w_in[:, 4 * half:4 * half + 4, c0:c0 + width])], used)

        ATT0, GATE0 = C_RW, C_RW + 3 * ATT
        for c in range(7):
            w_in_cols(c * GW, min(GW, C_RW - c * GW), (rw_psum, min(4 * c + 4, NM_RW)))
        N_ATT = len(loads)
        for c in range(9):
            w_in_cols(ATT0 + c * GW, GW, (proj_psum, 3 * c + 3))
        N_KV = len(loads)

        def kv_views(n):
            v1 = slot(n, GW)
            v0, v2 = slot(n + 1)[:, 0:GW], slot(n + 1)[:, GW:3 * GW].rearrange("p (a n) -> p a n", a=2)
            return v0, v1, v2

        for kv in range(2):
            for b in range(NB):
                used = (kt_psum, 2 * HG * (b + 1)) if kv == 0 else (sv_psum, b + 1)
                v0, v1, v2 = kv_views(len(loads))
                c0, c1, c2 = [A[f"cache_kv_w{WIN[g][0]}"][0, b, :, kv].rearrange("w h e -> w (h e)") for g in range(3)]
                add_load([(v1, c1.rearrange("(j t) n -> j t n", t=TS))], used)
                c2 = c2.rearrange("(m u) n -> m u n", u=16)
                add_load([(v0, c0)] + [(v2[64 * t2:64 * t2 + 64], c2[:, t2:TS:2, :]) for t2 in range(2)], used)
        N_GATE = len(loads)
        for c in range(4):
            w_in_cols(GATE0 + c * GW, GW, (gate_psum, 4 * c + 4))
        N_BR = len(loads)
        for i in range(6):
            add_load([(slot(len(loads), D), w_br[:, 2 * i:2 * i + 2, :])], (br_psum, 2 * KC))
        N_OUT = len(loads)
        for i in range(4):
            add_load([(slot(len(loads), D), w_out[:, 2 * i:2 * i + 2, :])], (wo_psum, 6))
        N_BASE = len(loads)
        full = []
        per_slot = [0] * NSLOT
        for n, (parts, _) in enumerate(loads):
            per_slot[n % NSLOT] += 16 * len(parts)
            full.append(per_slot[n % NSLOT])

        NL = 12
        w1_v = A["moe_w1"][0].rearrange("e (k p) n -> p e k n", p=128)
        w2_v = A["moe_w2"][0].rearrange("e (k p) n -> p e k n", p=128)

        def moe_slot(s, width=None):
            return slot(N_BASE + s, width)

        def moe_full(it, s):
            i = (N_BASE + s) % NSLOT
            return slot_full[i], it * 32 + per_slot[i] + 16 * (1 + s // NSLOT)

        def levels(eng, body):
            body(0)
            eng.wait_ge(routed, 1)
            n = eng.value_load(most_i[0:1, 0:1], min_val=0, max_val=NTOK)
            with eng.Fori(1, LEVELS) as l:
                with eng.If(n > l * CAP):
                    body(l)

        CH_OPS = ["MQ", "N", "KQ", "M1", "N1", "vT", "P1", "M2", "N2", "bT", "P2", "M3", "N3", "kT", "P3",
                  "M4", "N4", "P4", "N5", "P5", "R", "U", "Y", "S"]
        CH_BANK = {"MQ": (0, 1), "N": (4,), "KQ": (2, 3), "vT": (5,), "bT": (6,), "kT": (7,), "R": (6,), "U": (7,),
                   "Y": (3,), "S": (4,)}
        for k in range(1, 6):
            o = 3 * ((k + 1) % 2)
            CH_BANK[f"M{k}"], CH_BANK[f"N{k}"], CH_BANK[f"P{k}"] = (o,), (o + 1,), (o + 2,)
        CH_ACT = [x for x in CH_OPS if x in ("vT", "bT", "kT", "R", "Y") or x[0] == "M" and x != "MQ"]
        CH_DVE = [x for x in CH_OPS if x not in CH_ACT]

        def made(c, op):
            return len(CH_OPS) * c + CH_OPS.index(op) + 1

        def taken(c, op):
            if op in CH_ACT:
                return ch_act, len(CH_ACT) * c + CH_ACT.index(op) + 1
            return ch_dve, len(CH_DVE) * c + CH_DVE.index(op) + 1

        def bank(op):
            return B[CH_BANK[op][0]][:, :].rearrange("p (a b) -> p a b", a=KC)

        MP = {0: MQ[:, :, 0:NR], 1: tA, 2: tB, 3: tA, 4: tB}
        NP = {0: Nn, 1: tC, 2: tD, 3: tC, 4: tD, 5: tC}
        PP = {0: tE, 1: tF, 2: tE, 3: tF, 4: tE, 5: tF}

        scr = nc.dram_tensor("scratch_vec", (NB, 6, TS, D), F32, kind="Internal").ap()
        scr_y = nc.dram_tensor("scratch_y", (NB, TS, HR, NR), F32, kind="Internal").ap()

        block = ctx.enter_context(nc.Block())

        @block.gpsimd
        def _(pool_e):
            pool_e.wait_ge(xn_ready, 3)
            pool_e.dma_start(O[3].rearrange("a b d -> (a b) d"), x_sb[127:128, 1, :]).then_inc(xn_stored, 16)
            pool_e.dma_start(O[8][0], x_sb[TS - 1:NSMP:TS, 2, :]).then_inc(xn_stored, 16)
            for j in range(9, 18):
                g, t = (j - 9) // 3, j % 3
                r0, rows = TILES[t]
                pool_e.wait_ge(rope_done, j + 1)
                src = roped[0:rows, j % 2, :].rearrange("p (h e) -> p h e", h=HG)
                if t < 2 and g == 0:
                    if t == 1:
                        pool_e.dma_start(O[4][0, 0, :, 0], src).then_inc(k_stored[j % 2], 16)
                elif t < 2:
                    pool_e.dma_start(O[4 + g][0, 0, r0:r0 + 128, 0], src).then_inc(k_stored[j % 2], 16)
                else:
                    pool_e.dma_start(O[9 + g][0, :, CACHE[g] - TS:CACHE[g], 0].rearrange("b t h e -> b t (h e)"),
                                     roped[0:rows, j % 2, :]).then_inc(k_stored[j % 2], 16)
            pool_e.wait_ge(proj_out, 27)
            for g in range(NG):
                for t in range(2):
                    src = v_sb[:, t, g * GW:(g + 1) * GW].rearrange("p (h e) -> p h e", h=HG)
                    if g == 0 and t == 0:
                        continue
                    dst = O[4][0, 0, :, 1] if g == 0 else O[4 + g][0, 0, 128 * t:128 * t + 128, 1]
                    pool_e.dma_start(dst, src).then_inc(v_stored, 16)
                pool_e.dma_start(O[9 + g][0, :, CACHE[g] - TS:CACHE[g], 1].rearrange("b t h e -> b t (h e)"),
                                 v_sb[0:NSMP, 2, g * GW:(g + 1) * GW]).then_inc(v_stored, 16)

            for n in range(2 * NB):
                b = n % NB
                z = zb[:, n % 2]
                if n < NB:
                    src = [qT[:, HG * g:HG * g + HG, SEQ + TS * b:SEQ + TS * b + TS] for g in range(NG)]
                else:
                    src = [sPT[:, g, :].rearrange("p (h k) -> p h k", h=HG)[:, :, TS * b:TS * b + TS] for g in range(NG)]
                if n == 0:
                    pool_e.wait_ge(qk_out, 9)
                    pool_e.wait_ge(rw_arrays, 1)
                elif n == NB:
                    pool_e.wait_ge(spt_out, 1)
                if 2 <= n <= NB:
                    pool_e.wait_ge(ss_head, HG * (n - 1))
                elif n == NB + 1:
                    pool_e.wait_ge(ss_head, HG * NB)
                elif n > NB + 1:
                    pool_e.wait_ge(sv_psum, n - NB - 1)
                pool_e.memset(z, 0.0)
                pool_e.drain()
                pool_e.tensor_copy(z[:, :, TS * b:TS * b + TS], src[0])
                lo1 = 32 + TS * b
                pool_e.tensor_copy(z[:, :, lo1:lo1 + 33 * 3 + 1:33], src[1])
                for tp in range(2):
                    lo2 = 32 * (5 + tp) + TS * b + 2 * tp
                    ins = pool_e.tensor_copy(z[:, :, lo2:lo2 + 2], src[2][:, :, 2 * tp:2 * tp + 2])
                ins.then_inc(z_ready, 1)
                pool_e.drain()
            for i in range(6):
                pool_e.wait_ge(tk_out, i + 1)
                pool_e.dma_start(scr[:, i], tokS[0:NSMP, i, :]).then_inc(tk_written, 16)
            pool_e.wait_ge(tk_written, 96)
            for b in range(NB):
                pool_e.dma_start(vec[HR * b:HR * b + HR],
                                 scr[b].rearrange("a t (h n) -> h (a t) n", n=NR)).then_inc(vec_in, 16)
            pool_e.wait_ge(vec_in, 16 * NB)
            for hf in range(2):
                if hf:
                    pool_e.wait_ge(sh_saved, 16)
                pool_e.dma_start(Sh, A["state_wkv"][0, :, :, 32 * hf:32 * hf + 32].rearrange("b h v k -> (b h) v k"))\
                      .then_inc(sh_load, 16)
                for t in range(TS):
                    n = TS * hf + t
                    pool_e.tensor_tensor(stP, vec[:, TS * 3 + t, 32 * hf:32 * hf + 32].unsqueeze(2).broadcast_to([128, 32, NR]),
                                         vec[:, TS * 2 + t, :].unsqueeze(1).broadcast_to([128, 32, NR]), ALU.mult)
                    pool_e.wait_ge(st_a, n + 1)
                    pool_e.tensor_tensor(Sh, Sh, vec[:, TS * 1 + t, :].unsqueeze(1).broadcast_to([128, 32, NR]), ALU.mult)
                    pool_e.drain()
                    pool_e.tensor_tensor(Sh, Sh, stP, ALU.add).then_inc(st_p, 1)
                    pool_e.drain()
                pool_e.wait_ge(st_done, TS * (hf + 1))
                pool_e.dma_start(O[7][0, :, :, 32 * hf:32 * hf + 32].rearrange("b h v k -> (b h) v k"), Sh).then_inc(sh_saved, 16)
            for b in range(NB):
                pool_e.dma_start(scr_y[b].rearrange("t h v -> h t v"), ysm[HR * b:HR * b + HR]).then_inc(ys_written, 16)
            pool_e.wait_ge(sh_saved, 32)
            pool_e.wait_ge(ys_written, 16 * NB)
            pool_e.dma_start(tokY[0:NSMP, :], scr_y.rearrange("b t h v -> (b t) (h v)")).then_inc(ys_in, 16)
            pool_e.wait_ge(ch_act, len(CH_ACT) * NCH + 1)
            for j in range(2):
                pool_e.dma_start(O[2][0, 0].rearrange("(c j) v k -> j v c k", j=2)[j], Rr[NR * j:NR * j + NR]).then_inc(pst_saved, 16)

        K_JOBS = [j for j in range(9, 18) if j != 9]

        def k_stores_before(j):
            return sum(1 for i in K_JOBS if i < j and i % 2 == j % 2)

        @block.scalar
        def _(act):
            for t, (r0, rows) in enumerate(TILES):
                act.wait_ge(x_in, 48)
                act.activation(sqx[0:rows, :], x_sb[0:rows, t, :], ACT.Square, accum_out=nsq[0:rows, t:t + 1])
                act.drain()
                if t == 0:
                    act.wait_ge(c_in, 16)
                act.activation(rms[0:rows, t:t + 1], nsq[0:rows, t:t + 1], ACT.Sqrt, scale=1.0 / D,
                               bias=eps5[0:rows, :]).then_inc(squares, 1)
            for t in range(2):
                act.wait_ge(xt_psum, t + 1)
                for kb in range(2):
                    ins = act.copy(xT[:, 4 * kb:4 * kb + 4, 1 + 128 * t:129 + 128 * t],
                                   B[2 * t + kb][:, :].rearrange("p (k n) -> p k n", k=4))
                ins.then_inc(xt_ready, 1)
            act.wait_ge(xt_psum, 3)
            smp = B[4][:, 0:KC * NSMP].rearrange("p (k n) -> p k n", k=KC)
            act.copy(xTs[:, :, :], smp)
            for b in range(NB):
                c0 = SMP0 + b * (TS + 1)
                act.copy(xT[:, :, c0 + 1:c0 + 1 + TS], smp[:, :, TS * b:TS * b + TS])
            act.wait_ge(xt_psum, 4)
            shp = B[5][:, 0:KC * NB].rearrange("p (k n) -> p k n", k=KC)
            act.copy(xT[:, :, SMP0:XC:TS + 1], shp).then_inc(xt_ready, 1)

            act.wait_ge(prm_psum, 1)
            act.copy(prmT[:, 0:NPRM], B[6][:, 0:NPRM]).then_inc(prm_ready, 1)
            for m in range(NM_RW):
                rows = min(128, C_RW - 128 * m)
                act.wait_ge(rw_psum, m + 1)
                if m >= 2:
                    act.wait_ge(rw_mixed, m - 1)
                act.copy(praw[0:rows, m % 2, :], B[m % 4][0:rows, 0:XC]).then_inc(rw_raw, 1)
            act.wait_ge(rw_mixed, NM_RW)
            act.activation(lo[0:LORA, 0, :], lo[0:LORA, 0, :], ACT.Tanh)
            act.activation(lo[:, 1, :], lo[:, 1, :], ACT.Sigmoid)
            act.activation(lo[0:32, 2, :], lo[0:32, 2, :], ACT.Sigmoid).then_inc(lora_in, 1)
            for hc in range(KC):
                for i, (dst, off) in enumerate(((sW, W0), (aR, A0))):
                    act.wait_ge(lora_psum, 2 * hc + i + 1)
                    act.activation(dst[:, hc, :], B[4 + i][:, 0:NTOK], ACT.Sigmoid,
                                   bias=prmT[:, off + hc:off + hc + 1]).then_inc(lora_out, 1)
            for hc in range(KC):
                act.wait_ge(sqk_psum, hc + 1)
                act.activation(knb[:, hc, :], B[6 + hc % 2][:, 0:NTOK], ACT.Sqrt).then_inc(knorm, 1)
            act.wait_ge(xn_stored, 32)
            def transposed(j):
                c, t = j // 3, j % 3
                r0, rows = TILES[t]
                dst = (qT, kT)[c // 3]
                act.wait_ge(qk_psum, j + 1)
                act.copy(dst[:, HG * (c % 3):HG * (c % 3) + HG, r0:r0 + rows],
                         B[4 + j % 2][:, 0:HG * rows].rearrange("p (h n) -> p h n", h=HG)).then_inc(qk_out, 1)

            for j in range(27 + 2):
                if j < 27:
                    c, t = j // 3, j % 3
                    rows = TILES[t][1]
                    act.wait_ge(proj_psum, j + 1)
                    if c < 6:
                        if j >= 2:
                            act.wait_ge(rope_done, j - 1)
                        act.copy(raw[0:rows, j % 2, :], B[j % 4][0:rows, :])
                        for h in range(HG):
                            act.activation(sqh[0:rows, h, :], B[j % 4][0:rows, h * E:(h + 1) * E], ACT.Square,
                                           accum_out=hss[0:rows, j % 2, h:h + 1])
                        act.drain()
                        act.activation(hms[0:rows, j % 2, :], hss[0:rows, j % 2, :], ACT.Sqrt, scale=1.0 / E,
                                       bias=eps5[0:rows, :]).then_inc(proj_out, 1)
                    else:
                        if j == 18:
                            act.wait_ge(rw_arrays, 1)
                        act.copy(v_sb[0:rows, t, (c - 6) * GW:(c - 5) * GW], B[j % 4][0:rows, :]).then_inc(proj_out, 1)
                if 2 <= j < 20:
                    transposed(j - 2)

            for u in range(2 * HG):
                h, i = u // 2, u % 2
                act.wait_ge(s_read, u + 1)
                w = NG * 128 * (i + 1)
                act.activation(pP[i][:, 0:w], pP[i][:, 0:w], ACT.Exp, bias=anmx[:, i:i + 1],
                               accum_out=aden[:, i:i + 1]).then_inc(s_exp, 1)
                act.wait_ge(pt_psum, u + 1)
                if i == 0:
                    act.copy(pPT[0], B[3][:, 0:384].rearrange("p (k n) -> p k n", k=3)).then_inc(pt_out, 1)
                else:
                    act.copy(pPT[1][:, 0:4], B[4][:, :].rearrange("p (k n) -> p k n", k=4))
                    act.copy(pPT[1][:, 4:6], B[5][:, 0:256].rearrange("p (k n) -> p k n", k=2)).then_inc(pt_out, 1)
                act.wait_ge(pv_psum, u + 1)
                act.copy(oT[:, h, 128 * i:128 * i + 128], B[6 + i][:, 0:128]).then_inc(o_out, 1)
            for w in range(NB * HG):
                act.wait_ge(kt_psum, 2 * w + 1)
                if w >= 2:
                    act.wait_ge(ss_head, w - 1)
                act.copy(kTb[:, w % 2, 1:5, :], B[2 * (w % 2)][:, :].rearrange("p (k n) -> p k n", k=4))\
                   .then_inc(kt_out_a, 1)
            act.wait_ge(ss_read, 1)
            act.activation(sP, sP, ACT.Exp, bias=anmx[:, 0:1], accum_out=aden[:, 0:1]).then_inc(ss_exp, 1)
            act.wait_ge(spt_psum, 1)
            act.copy(sPT, B[5][:, 0:384].rearrange("p (k n) -> p k n", k=3))
            act.copy(sPTn[0:NSMP], B[6][0:NSMP, 0:384].rearrange("p (k n) -> p k n", k=3)).then_inc(spt_out, 1)
            act.wait_ge(so_psum, 1)
            act.copy(oT[:, :, SEQ:NTOK], B[5][:, 0:128].rearrange("p (h n) -> p h n", h=HG)).then_inc(so_out, 1)

            act.wait_ge(v_stored, 128)
            for i in range(6):
                act.wait_ge(tk_psum, i + 1)
                if i == 0:
                    act.wait_ge(so_out, 1)
                for kb in range(2):
                    src, dst = B[2 * (i % 2) + kb][0:NSMP, :], tokS[0:NSMP, i, 512 * kb:512 * kb + 512]
                    if i == 1:
                        ins = act.activation(dst, src, ACT.Exp, scale=-KAPPA)
                    else:
                        ins = act.activation(dst, src, ACT.Copy, scale=-1.0 if i == 4 else 1.0)
                ins.then_inc(tk_out, 1)

            def exps(c):
                act.wait_ge(cum_ready, c + 1)
                act.activation(tC, tB, ACT.Exp, scale=-KAPPA)
                act.activation(tD, tB, ACT.Exp, scale=KAPPA)
                act.activation(tE, tA, ACT.Exp, scale=-KAPPA).then_inc(exps_ready, 1)

            exps(0)
            for c in range(NCH):
                for op in CH_ACT:
                    dst = {"vT": vTm, "bT": bTm, "kT": kTm, "R": Rr, "Y": kkn[:, :, L * c:L * c + L]}.get(op)
                    act.wait_ge(ch_psum, made(c, op))
                    act.copy(dst if dst is not None else MP[int(op[1])], bank(op)).then_inc(ch_act, 1)
                    if op == "R" and c + 1 < NCH:
                        exps(c + 1)
            act.wait_ge(ch_psum, len(CH_OPS) * NCH + 1)
            act.copy(Rr, B[5][:, :].rearrange("p (a b) -> p a b", a=KC)).then_inc(ch_act, 1)
            act.wait_ge(ys_psum, 1)
            act.copy(kkn[:, :, SEQ:NTOK], B[6][:, 0:KC * NSMP].rearrange("p (a b) -> p a b", a=KC)).then_inc(ys_out, 1)

            def gate(m):
                act.wait_ge(gate_psum, m + 1)
                act.activation(gT[:, m, 0:SEQ], B[m % 4][:, 1:SMP0], ACT.Sigmoid)
                act.activation(gT[:, m, SEQ:NTOK].rearrange("p (b t) -> p b t", b=NB),
                               B[m % 4][:, SMP0:XC].rearrange("p (b u) -> p b u", b=NB)[:, :, 1:TS + 1],
                               ACT.Sigmoid).then_inc(gate_out, 1)

            act.wait_ge(pst_saved, 32)
            for hc in range(KC):
                act.wait_ge(gn_centred, hc + 1)
                act.activation(gsq[:, hc, :], kkn[:, hc, :], ACT.Square).then_inc(gn_sq, 1)
            for m in range(KC):
                gate(m)
            for hc in range(KC):
                act.wait_ge(gnv_psum, hc + 1)
                act.activation(grs[:, hc, :], B[6 + hc % 2][:, 0:NTOK], ACT.Sqrt, scale=1.0 / NR,
                               bias=eps64).then_inc(gn_rs, 1)
            for m in range(KC, 2 * KC):
                gate(m)
            for t, (r0, rows) in enumerate(TILES):
                act.wait_ge(h_ready, 2 * t + 2)
                act.activation(hn[0:rows, t, :], acc[0:rows, t, :], ACT.Square, accum_out=nsq[0:rows, t:t + 1])
                act.drain()
                act.activation(rms[0:rows, t:t + 1], nsq[0:rows, t:t + 1], ACT.Sqrt, scale=1.0 / D,
                               bias=eps5[0:rows, :]).then_inc(h_rms, 1)
            for t, (r0, rows) in enumerate(TILES):
                act.wait_ge(hnt_psum, t + 1)
                for kb in range(2):
                    ins = act.copy(hnT[:, 4 * kb:4 * kb + 4, r0:r0 + rows],
                                   B[2 * t + kb][:, 0:4 * rows].rearrange("p (k n) -> p k n", k=4))
                ins.then_inc(hnt_out, 1)
            for t, (r0, rows) in enumerate(TILES):
                act.wait_ge(lg_max, t + 1)
                act.activation(g4[0:rows, t, :], m8[0:rows, t, 0:4], ACT.Exp, bias=nm8[0:rows, t:t + 1],
                               accum_out=nm8[0:rows, 4 + t:5 + t]).then_inc(lg_exp, 1)
            act.wait_ge(gt_psum, 1)
            act.copy(gselT[0:NEXP, :], B[4][0:NEXP, 0:NTOK]).then_inc(gt_out, 1)

            for x in (xe_out, xet_out, sg_ready, at_out, ye_out, sgt_out):
                act.sem_inc(x, 1)

            def act_gathered(q):
                act.wait_ge(xe_psum, q + 1)
                act.copy(xe, B[2][:, :]).then_inc(xe_out, 1)
                act.wait_ge(xet_psum, q + 1)
                act.copy(xeT.rearrange("p a b c -> p (a b c)"), B[3][:, :]).then_inc(xet_out, 1)

            def act_level(l):
                act_gathered(l * (NEXP + 1))
                with act.Fori(0, NEXP) as e:
                    it = l * NEXP + e
                    q = l * (NEXP + 1) + e
                    act.wait_ge(glu_min, it + 1)
                    act.activation(sgm, glu, ACT.Sigmoid, scale=1.702).then_inc(sg_ready, 1)
                    act_gathered(q + 1)
                    act.wait_ge(at_psum, it + 1)
                    act.copy(actT.rearrange("p a b c -> p (a b c)"), B[4][:, :]).then_inc(at_out, 1)
                    act.wait_ge(sc_psum, q * 3 + 3)
                    act.wait_ge(ye_psum, it + 1)
                    act.copy(ysb, B[5][:, :]).then_inc(ye_out, 1)
                    act.wait_ge(sgt_psum, it + 2)
                    act.copy(selGT[:, 0:NTOK], B[3][:, 0:NTOK]).then_inc(sgt_out, 1)

            levels(act, act_level)

        @block.tensor
        def _(pe):
            pe.wait_ge(c_in, 16)
            for t in range(2):
                pe.wait_ge(xn_ready, t + 1)
                for k in range(KC):
                    mm = pe.transpose(B[2 * t + k // 4][:, 128 * (k % 4):128 * (k % 4) + 128],
                                      x_sb[:, t, 128 * k:128 * k + 128], ident)
                mm.then_inc(xt_psum, 1)
            pe.wait_ge(xn_ready, 3)
            for k in range(KC):
                mm = pe.transpose(B[4][:, NSMP * k:NSMP * k + NSMP], x_sb[0:NSMP, 2, 128 * k:128 * k + 128],
                                  ident[0:NSMP, 0:NSMP])
            mm.then_inc(xt_psum, 1)
            pe.wait_ge(sh_in, 16)
            for k in range(KC):
                mm = pe.transpose(B[5][:, NB * k:NB * k + NB], xsh[0:NB, 128 * k:128 * k + 128],
                                  ident[0:NB, 0:NB])
            mm.then_inc(xt_psum, 1)

            def turn(j):
                rows = TILES[j % 3][1]
                pe.wait_ge(rope_done, j + 1)
                if j >= 2:
                    pe.wait_ge(qk_out, j - 1)
                for h in range(HG):
                    mm = pe.transpose(B[4 + j % 2][:, h * rows:(h + 1) * rows],
                                      roped[0:rows, j % 2, h * E:(h + 1) * E], ident[0:rows, 0:rows])
                mm.then_inc(qk_psum, 1)

            pe.wait_ge(prm_in, 16 * 9)
            pe.transpose(B[6][:, 0:NPRM], prm[0:NPRM, :], ident[0:NPRM, 0:NPRM]).then_inc(prm_psum, 1)
            pe.wait_ge(xt_ready, 3)
            pe.wait_ge(zero_col, 1)
            for m in range(NM_RW):
                rows = min(128, C_RW - 128 * m)
                if m >= 4:
                    pe.wait_ge(rw_raw, m - 3)
                for k in range(KC):
                    n = 2 * (m // 4) + k // 4
                    if m % 4 == 0 and k % 4 == 0:
                        pe.wait_ge(slot_full[n % NSLOT], full[n])
                    mm = pe.matmul(B[m % 4][0:rows, 0:XC],
                                   slot(n, GW)[:, k % 4, 128 * (m % 4):128 * (m % 4) + rows], xT[:, k, :],
                                   start=(k == 0), stop=(k == KC - 1))
                mm.then_inc(rw_psum, 1)
            pe.wait_ge(lora_in, 1)
            pe.wait_ge(w2a2_in, 32)
            for hc in range(KC):
                for i in range(2):
                    if hc:
                        pe.wait_ge(lora_out, 2 * hc - 1 + i)
                    p = slice(LORA * i, LORA * i + LORA)
                    pe.matmul(B[4 + i][:, 0:NTOK], w2a2[p, 128 * hc:128 * hc + 128], lo[p, 0, :],
                              start=True, stop=True).then_inc(lora_psum, 1)
            pe.wait_ge(prm_ready, 1)
            for hc in range(KC):
                if hc == 0:
                    pe.wait_ge(sqk_ready, 1)
                if hc >= 2:
                    pe.wait_ge(knorm, hc - 1)
                pe.matmul(B[6 + hc % 2][:, 0:NTOK], blockones, sqk[:, hc, :], start=True, stop=True)\
                  .then_inc(sqk_psum, 1)
            pe.wait_ge(rw_raw, NM_RW)
            for c in range(9):
                for t, (r0, rows) in enumerate(TILES):
                    j = 3 * c + t
                    if j >= 4:
                        pe.wait_ge(proj_out, j - 3)
                    for k in range(KC):
                        n = N_ATT + 2 * c + k // 4
                        if t == 0 and k % 4 == 0:
                            pe.wait_ge(slot_full[n % NSLOT], full[n])
                        lhs = xT[:, k, 1 + r0:1 + r0 + rows] if t < 2 else xTs[:, k, :]
                        mm = pe.matmul(B[j % 4][0:rows, :], lhs, slot(n, GW)[:, k % 4, :],
                                       start=(k == 0), stop=(k == KC - 1))
                    mm.then_inc(proj_psum, 1)
                    if 2 <= j < 20:
                        turn(j - 2)

            def scores(u):
                h, i = u // 2, u % 2
                if u >= 2:
                    pe.wait_ge(s_read, u - 1)
                for g in range(NG):
                    w = 128 * (i + 1)
                    out = B[0][:, 128 * g:128 * g + 128] if i == 0 else B[1 + g // 2][:, 256 * (g % 2):256 * (g % 2) + 256]
                    mm = pe.matmul(out, qT[:, HG * g + h, 128 * i:128 * i + 128], kT[:, HG * g + h, 0:w],
                                   start=True, stop=True)
                mm.then_inc(s_psum, 1)

            pe.wait_ge(proj_out, 27)
            pe.wait_ge(qk_out, 18)
            scores(0)
            scores(1)
            for u in range(2 * HG):
                h, i = u // 2, u % 2
                pe.wait_ge(p_ready, u + 1)
                if u >= 2:
                    pe.wait_ge(pt_out, u - 1)
                for n in range(NG * (i + 1)):
                    out = B[3] if i == 0 else B[4 + n // 4]
                    mm = pe.transpose(out[:, 128 * (n % 4):128 * (n % 4) + 128], pP[i][:, 128 * n:128 * n + 128], ident)
                mm.then_inc(pt_psum, 1)
                if u + 2 < 2 * HG:
                    scores(u + 2)
                pe.wait_ge(pt_out, u + 1)
                if u >= 2:
                    pe.wait_ge(o_out, u - 1)
                for n in range(NG * (i + 1)):
                    g, kt = n // (i + 1), n % (i + 1)
                    mm = pe.matmul(B[6 + i][:, 0:128], v_sb[:, kt, g * GW + h * E:g * GW + h * E + E], pPT[i][:, n, :],
                                   start=(n == 0), stop=(n == NG * (i + 1) - 1))
                mm.then_inc(pv_psum, 1)

            def rows_of(bank, h):
                return bank[32 * h:32 * h + 32]

            pe.wait_ge(s_read, 2 * HG)
            pe.wait_ge(o_out, 2 * HG)
            for h in range(HG):
                for g in range(NG):
                    pe.matmul(rows_of(B[4], h)[:, 384 + 32 * g:416 + 32 * g], qT[:, HG * g + h, SEQ:NTOK],
                              kT[:, HG * g + h, SEQ:NTOK], start=(g == 0), stop=False,
                              tile_position=(0, 32 * h), skip_group_check=True)

            def turn_keys(w):
                b, h = w // HG, w % HG
                n = N_KV + 2 * b
                v0, v1, v2 = kv_views(n)
                if h == 0:
                    pe.wait_ge(slot_full[n % NSLOT], full[n])
                    pe.wait_ge(slot_full[(n + 1) % NSLOT], full[n + 1])
                if w >= 2:
                    pe.wait_ge(kt_out_a, w - 1)
                    pe.wait_ge(kt_out_v, w - 1)
                hs = slice(h * E, h * E + E)
                for t in range(TS):
                    mm = pe.transpose(B[2 * (w % 2)][:, 128 * t:128 * t + 128], v1[:, t, hs], ident)
                mm.then_inc(kt_psum, 1)
                for i, blk in enumerate((v0[:, hs], v2[:, 0, hs], v2[:, 1, hs])):
                    mm = pe.transpose(B[2 * (w % 2) + 1][:, 128 * i:128 * i + 128], blk, ident)
                mm.then_inc(kt_psum, 1)

            def cached_scores(w):
                b, h = w // HG, w % HG
                pe.wait_ge(kt_out_a, w + 1)
                pe.wait_ge(kt_out_v, w + 1)
                if h == 0:
                    pe.wait_ge(z_ready, b + 1)
                for i in range(7):
                    col = (0, 128, 128, 128, 128, 256, 256)[i]
                    mm = pe.matmul(rows_of(B[4], h)[:, col:col + 128], zb[:, b % 2, h, 32 * i:32 * i + 32],
                                   kTb[:, w % 2, i, :], start=False, stop=(b == NB - 1),
                                   tile_position=(0, 32 * h), skip_group_check=True)
                mm.then_inc(ss_head, 1)

            turn_keys(0)
            for w in range(NB * HG):
                if w + 1 < NB * HG:
                    turn_keys(w + 1)
                cached_scores(w)
            pe.wait_ge(ss_exp, 1)
            for g in range(NG):
                pe.transpose(B[5][:, 128 * g:128 * g + 128], sP[:, 128 * g:128 * g + 128], ident)
            for g in range(NG):
                mm = pe.transpose(B[6][0:NSMP, 128 * g:128 * g + 128], sP[:, 384 + 32 * g:416 + 32 * g], ident)
            mm.then_inc(spt_psum, 1)
            pe.wait_ge(spt_out, 1)
            for h in range(HG):
                for g in range(NG):
                    pe.matmul(rows_of(B[7], h)[:, 0:E], sPTn[0:NSMP, g, 32 * h:32 * h + 32],
                              v_sb[0:NSMP, 2, g * GW + h * E:g * GW + h * E + E], start=(g == 0), stop=False,
                              tile_position=(0, 32 * h), skip_group_check=True)
            for b in range(NB):
                n = N_KV + 2 * (NB + b)
                v0, v1, v2 = kv_views(n)
                pe.wait_ge(slot_full[n % NSLOT], full[n])
                pe.wait_ge(slot_full[(n + 1) % NSLOT], full[n + 1])
                pe.wait_ge(z_ready, NB + b + 1)
                for i, blk in enumerate((v0, v1[:, 0], v1[:, 1], v1[:, 2], v1[:, 3], v2[:, 0], v2[:, 1])):
                    for h in range(HG):
                        mm = pe.matmul(rows_of(B[7], h)[:, 0:E], zb[:, b % 2, h, 32 * i:32 * i + 32],
                                       blk[:, h * E:h * E + E], start=False, stop=(b == NB - 1 and i == 6),
                                       tile_position=(0, 32 * h), skip_group_check=True)
                mm.then_inc(sv_psum, 1)
            pe.wait_ge(so_read, 1)
            pe.transpose(B[5][:, 0:128], osm, ident).then_inc(so_psum, 1)

            for i, x in enumerate((rT, sW, kR, vR, kkn, aR)):
                if i >= 2:
                    pe.wait_ge(tk_out, i - 1)
                for k in range(KC):
                    mm = pe.transpose(B[2 * (i % 2) + k // 4][0:NSMP, 128 * (k % 4):128 * (k % 4) + 128],
                                      x[:, k, SEQ:NTOK], ident)
                mm.then_inc(tk_psum, 1)

            def heads(op, lhs, rhs, more=(), n=NR):
                terms = [(lhs, rhs), *more]
                for hc in range(KC):
                    for j in range(2):
                        p = slice(NR * j, NR * j + NR)
                        if n == NR:
                            out = bank(op)[p, hc, :] if op in CH_BANK else B[5][p, NR * hc:NR * hc + NR]
                        else:
                            out = B[CH_BANK[op][hc // 4]][p, n * (hc % 4):n * (hc % 4) + n]
                        for i, (x, y) in enumerate(terms):
                            mm = pe.matmul(out, x(p, hc), y(p, hc), start=(i == 0), stop=(i == len(terms) - 1),
                                           tile_position=(NR * j, NR * j))
                mm.then_inc(ch_psum, 1)

            def of(t, lo_=0, n=NR):
                return lambda p, hc: t[p, hc, lo_:lo_ + n]

            eye = lambda p, hc: ident[p, p]
            pe.wait_ge(tk_out, 6)
            pe.wait_ge(so_out, 1)
            bank_free = {}
            for c in range(NCH):
                needs = {"MQ": [], "N": [], "KQ": [], "M1": [taken(c, "MQ"), taken(c, "N")], "vT": [], "bT": [], "kT": [],
                         "R": [taken(c, "KQ"), taken(c, "vT")] + ([taken(c - 1, "S")] if c else [(st_zero, 1)]),
                         "U": [taken(c, "R"), taken(c, "P5")], "Y": [taken(c, "U")], "S": [taken(c, "bT"), taken(c, "kT")]}
                for k in range(1, 6):
                    if k > 1:
                        needs[f"M{k}"] = [taken(c, f"M{k - 1}"), taken(c, f"N{k - 1}")]
                    needs[f"N{k}"] = [taken(c, f"M{k - 1}")] if k == 5 else []
                    needs[f"P{k}"] = [taken(c, f"N{k}")] + ([taken(c, f"P{k - 1}")] if k > 1 else [])
                needs["N5"] += [taken(c, "N4")]
                pe.wait_ge(ops_ready, c + 1)
                for op in CH_OPS:
                    for w in needs[op]:
                        pe.wait_ge(*w)
                    for bk in CH_BANK[op]:
                        if bk in bank_free:
                            pe.wait_ge(*bank_free[bk])
                        bank_free[bk] = taken(c, op)
                    if op == "MQ":
                        heads(op, of(bh), of(AR, 0, H2), n=H2)
                    elif op == "KQ":
                        heads(op, of(kh), of(AR, 0, H2), n=H2)
                    elif op == "N":
                        heads(op, of(AR), of(bh))
                    elif op == "vT":
                        heads(op, of(vR, L * c), eye)
                    elif op == "bT":
                        heads(op, of(bh), eye)
                    elif op == "kT":
                        heads(op, of(kh), eye)
                    elif op == "R":
                        heads(op, of(AR), of(ST), [(of(KQ), of(vTm))])
                    elif op == "U":
                        heads(op, of(PP[5]), of(Rr))
                    elif op == "Y":
                        heads(op, of(ST), of(AR, NR), [(of(Uu), of(MQ, NR)), (of(vTm), of(KQ, NR))])
                    elif op == "S":
                        heads(op, of(bTm), of(Uu), [(of(kTm), of(vTm))])
                    else:
                        k = int(op[1])
                        if op[0] == "M":
                            heads(op, of(NP[k - 1]), of(MP[k - 1]))
                        elif op[0] == "N":
                            heads(op, of(MP[k - 1]), of(NP[k - 1]))
                        else:
                            heads(op, of(NP[k]), of(PP[k - 1]))
            pe.wait_ge(*taken(NCH - 1, "S"))
            heads("OUT", of(ST), eye)
            pe.wait_ge(ys_in, 16)
            for k in range(KC):
                mm = pe.transpose(B[6][:, NSMP * k:NSMP * k + NSMP], tokY[0:NSMP, 128 * k:128 * k + 128],
                                  ident[0:NSMP, 0:NSMP])
            mm.then_inc(ys_psum, 1)

            def gates(m0_, m1_):
                for m in range(m0_, m1_):
                    if m >= 4:
                        pe.wait_ge(gate_out, m - 3)
                    for k in range(KC):
                        n = N_GATE + 2 * (m // 4) + k // 4
                        if m % 4 == 0 and k % 4 == 0:
                            pe.wait_ge(slot_full[n % NSLOT], full[n])
                        mm = pe.matmul(B[m % 4][:, 0:XC], slot(n, GW)[:, k % 4, 128 * (m % 4):128 * (m % 4) + 128],
                                       xT[:, k, :], start=(k == 0), stop=(k == KC - 1))
                    mm.then_inc(gate_psum, 1)

            def head_sums(x, banks, out_sem, free_sem, ready=None):
                for hc in range(KC):
                    if ready is not None:
                        pe.wait_ge(ready, hc + 1)
                    if hc >= 2:
                        pe.wait_ge(free_sem, hc - 1)
                    pe.matmul(B[banks + hc % 2][:, 0:NTOK], blockones, x[:, hc, :], start=True, stop=True)\
                      .then_inc(out_sem, 1)

            pe.wait_ge(ys_out, 1)
            pe.wait_ge(ch_act, len(CH_ACT) * NCH + 1)
            head_sums(kkn, 4, gnm_psum, gn_centred)
            gates(0, KC)
            head_sums(gsq, 6, gnv_psum, gn_rs, gn_sq)
            pe.wait_ge(bon_ready, 1)
            pe.wait_ge(gn_centred, KC)
            head_sums(gpr, 4, bon_psum, bon_out)
            gates(KC, 2 * KC)
            pe.wait_ge(g2_in, 32)
            pe.wait_ge(gn_rs, KC)
            for hc in range(KC):
                if hc >= 2:
                    pe.wait_ge(y_ready, hc - 1)
                pe.matmul(B[6 + hc % 2][:, 0:NTOK], g2w[:, 0, 128 * hc:128 * hc + 128], lo[:, 1, :],
                          start=True, stop=False)
                pe.matmul(B[6 + hc % 2][:, 0:NTOK], g2w[0:32, 1, 128 * hc:128 * hc + 128], lo[0:32, 2, :],
                          start=False, stop=True).then_inc(gg_psum, 1)

            pe.wait_ge(y_ready, KC)
            pe.wait_ge(gate_out, 2 * KC)
            for n in range(N_BR, N_BR + 6):
                pe.wait_ge(slot_full[n % NSLOT], full[n])
            for m in range(KC):
                if m >= 2:
                    pe.wait_ge(merged, m - 1)
                for br, (k0, kn, x) in enumerate(((0, KC, kkn), (KC, HG, oT))):
                    for k in range(kn):
                        w = slot(N_BR + (k0 + k) // 2, D)[:, (k0 + k) % 2, 128 * m:128 * m + 128]
                        mm = pe.matmul(B[2 * (m % 2) + br][:, 0:NTOK], w, x[:, k, :], start=(k == 0), stop=(k == kn - 1))
                    mm.then_inc(br_psum, 1)
            pe.wait_ge(merged, KC)
            for n in range(N_OUT, N_OUT + 4):
                pe.wait_ge(slot_full[n % NSLOT], full[n])
            for t, (r0, rows) in enumerate(TILES):
                for c in range(2):
                    j = 2 * t + c
                    if j >= 4:
                        pe.wait_ge(h_ready, j - 3)
                    for k in range(KC):
                        mm = pe.matmul(B[4 + j % 4][0:rows, :], mT[:, k, r0:r0 + rows],
                                       slot(N_OUT + k // 2, D)[:, k % 2, 512 * c:512 * c + 512],
                                       start=(k == 0), stop=(k == KC - 1))
                    mm.then_inc(wo_psum, 1)
            for t, (r0, rows) in enumerate(TILES):
                pe.wait_ge(hn_ready, t + 1)
                if t == 2:
                    pe.wait_ge(h_ready, 6)
                for k in range(KC):
                    mm = pe.transpose(B[2 * t + k // 4][:, rows * (k % 4):rows * (k % 4) + rows],
                                      hn[0:rows, t, 128 * k:128 * k + 128], ident[0:rows, 0:rows])
                mm.then_inc(hnt_psum, 1)
            for t, (r0, rows) in enumerate(TILES):
                pe.wait_ge(hnt_out, t + 1)
                for k in range(KC):
                    mm = pe.matmul(B[6][0:rows, 32 * t:32 * t + NEXP], hnT[:, k, r0:r0 + rows], rwt[:, k, :],
                                   start=(k == 0), stop=(k == KC - 1))
            mm.then_inc(lg_psum, 1)
            pe.wait_ge(mk_ready, 3)
            for t, (r0, rows) in enumerate(TILES):
                for u in range(t + 1):
                    urows = TILES[u][1]
                    lhs = (const("prefix", urows)[:, 0:rows] if u == t else ones[0:urows, 0:rows])
                    pe.matmul(B[7][0:rows, 32 * t:32 * t + NEXP], lhs, mk[0:urows, u, :], start=(u == 0), stop=(u == t))
            for u in range(3):
                urows = TILES[u][1]
                mm = pe.matmul(B[7][:, 96:96 + NEXP], ones[0:urows, :], mk[0:urows, u, :], start=(u == 0), stop=(u == 2))
            mm.then_inc(pos_psum, 1)
            for t, (r0, rows) in enumerate(TILES):
                mm = pe.transpose(B[4][0:NEXP, r0:r0 + rows], gsel[0:rows, t, :], ident[0:rows, 0:rows])
            mm.then_inc(gt_psum, 1)
            pe.wait_ge(gt_out, 1)
            pe.wait_ge(b2_in, 16)
            for t, (r0, rows) in enumerate(TILES):
                for c in range(2):
                    pe.matmul(B[2 * t + c][0:rows, :], gselT[0:NEXP, r0:r0 + rows], b2w[0:NEXP, 512 * c:512 * c + 512],
                              start=True, stop=True).then_inc(b2_psum, 1)
            pe.wait_ge(b2_added, 1)
            pe.sem_inc(sgt_psum, 1)

            def gather(q):
                pe.wait_ge(sel_ready, q + 1)
                pe.wait_ge(xe_out, q + 1)
                for t, (r0, rows) in enumerate(TILES):
                    for hh in range(2):
                        mm = pe.matmul(B[2][CAP * hh:CAP * hh + CAP, :], selT[0:rows, t, CAP * hh:CAP * hh + CAP],
                                       hn[0:rows, t, 512 * hh:512 * hh + 512], start=(t == 0), stop=(t == 2),
                                       tile_position=(0, CAP * hh), skip_group_check=True)
                mm.then_inc(xe_psum, 1)

            def turn_gathered(q, it):
                pe.wait_ge(xe_out, q + 2)
                pe.wait_ge(sgt_out, it + 1)
                for c in range(4):
                    mm = pe.transpose(B[3][:, 128 * c:128 * c + 128], xe[:, 128 * c:128 * c + 128], ident)
                mm.then_inc(xet_psum, 1)

            def scatter(q, t):
                r0, rows = TILES[t]
                pe.wait_ge(sc_added, q * 3 + t + 1)
                for hh in range(2):
                    p = slice(CAP * hh, CAP * hh + CAP)
                    mm = pe.matmul(B[6 + hh][:, :], selGT[p, r0:r0 + 128], ysb[p, :], start=True, stop=True,
                                   tile_position=(CAP * hh, 0))
                mm.then_inc(sc_psum, 1)

            def pe_level(l):
                q0 = l * (NEXP + 1)
                pe.wait_ge(sgt_zero, l + 1)
                gather(q0)
                turn_gathered(q0, l * NEXP)
                with pe.Fori(0, NEXP) as e:
                    it = l * NEXP + e
                    q = q0 + e
                    pe.wait_ge(b1_full, it * 32 + 32)
                    pe.wait_ge(act_done, it + 1)
                    for hh in range(2):
                        for j in range(2):
                            p = 64 * j
                            pe.matmul(B[j][CAP * hh:CAP * hh + CAP, :], ones[p:p + 1, 0:CAP],
                                      b1r[p:p + 1, hh, :], start=True, stop=False,
                                      tile_position=(p, CAP * hh), skip_group_check=True)
                    pe.wait_ge(xet_out, q + 2)
                    for k in range(KC):
                        pe.wait_ge(*moe_full(it, k))
                        w = moe_slot(k)
                        for j in range(2):
                            for hh in range(2):
                                mm = pe.matmul(B[j][CAP * hh:CAP * hh + CAP, :], xeT[:, k % 4, k // 4, :],
                                               w[:, D * hh + 512 * j:D * hh + 512 * j + 512], start=False,
                                               stop=(k == KC - 1), tile_position=(0, CAP * hh), skip_group_check=True)
                        mm.then_inc(moe_used, 1)
                    gather(q + 1)
                    pe.wait_ge(sgt_out, it + 1)
                    pe.wait_ge(ye_out, it + 1)
                    scatter(q, 0)
                    turn_gathered(q + 1, it)
                    pe.wait_ge(act_done, it + 2)
                    pe.wait_ge(at_out, it + 1)
                    for c in range(4):
                        mm = pe.transpose(B[4][:, 128 * c:128 * c + 128], act_[:, 128 * c:128 * c + 128], ident)
                    mm.then_inc(at_psum, 1)
                    scatter(q, 1)
                    pe.wait_ge(at_out, it + 2)
                    for k in range(KC):
                        if k % 2 == 0:
                            pe.wait_ge(*moe_full(it, KC + k // 2))
                        for hh in range(2):
                            mm = pe.matmul(B[5][CAP * hh:CAP * hh + CAP, :], actT[:, k % 4, k // 4, :],
                                           moe_slot(KC + k // 2, D)[:, k % 2, 512 * hh:512 * hh + 512], start=(k == 0),
                                           stop=(k == KC - 1), tile_position=(0, CAP * hh), skip_group_check=True)
                        if k % 2 == 1 and k < KC - 1:
                            mm.then_inc(moe_used, 1)
                    mm.then_inc(ye_psum, 1)
                    scatter(q, 2)
                    pe.wait_ge(selg_ready, it + 1)
                    pe.wait_ge(xet_out, q + 3)
                    for t, (r0, rows) in enumerate(TILES):
                        mm = pe.transpose(B[3][:, r0:r0 + rows], selG[0:rows, t, :], ident[0:rows, 0:rows])
                    mm.then_inc(sgt_psum, 1)
                pe.wait_ge(ye_out, l * NEXP + NEXP + 1)
                pe.wait_ge(sgt_out, l * NEXP + NEXP + 1)
                for t in range(3):
                    scatter(q0 + NEXP, t)

            levels(pe, pe_level)

        @block.vector
        def _(dve):
            dve.memset(xT[:, :, 0:1], 0.0).then_inc(zero_col, 1)
            dve.memset(prm[0:NPRM, :], 0.0).then_inc(prm_zero, 1)
            dve.wait_ge(nw_in, 16)
            for t, (r0, rows) in enumerate(TILES):
                dve.wait_ge(squares, t + 1)
                dve.reciprocal(rstd[0:rows, t:t + 1], rms[0:rows, t:t + 1])
                dve.drain()
                dve.scalar_tensor_tensor(out=x_sb[0:rows, t, :], in0=x_sb[0:rows, t, :],
                                         scalar=rstd[0:rows, t:t + 1], in1=nw[0:rows, :],
                                         op0=ALU.mult, op1=ALU.mult).then_inc(xn_ready, 1)
            dve.wait_ge(prm_ready, 1)
            dve.tensor_scalar(prmT[:, ONEKA:ONEKA + KC], prmT[:, PKA:PKA + KC], -1.0, 1.0, ALU.mult, ALU.add)
            for m in range(NM_RW):
                rows = min(128, C_RW - 128 * m)
                p = praw[0:rows, m % 2, :]
                dst = ((rT, kR, vR)[m // KC][:, m % KC, :] if m < 3 * KC else lo[:, m - 3 * KC, :])[0:rows, :]
                mu = prmT[0:rows, MU + m:MU + m + 1]
                dve.wait_ge(rw_raw, m + 1)
                dve.tensor_tensor(pdiff[0:rows, 1:XC], p[:, 0:XC - 1], p[:, 1:XC], ALU.subtract)
                dve.drain()
                dve.scalar_tensor_tensor(out=dst[:, 0:SEQ], in0=pdiff[0:rows, 1:SMP0], scalar=mu,
                                         in1=p[:, 1:SMP0], op0=ALU.mult, op1=ALU.add)
                smp = lambda v: v[:, SMP0:XC].rearrange("p (b u) -> p b u", b=NB)[:, :, 1:TS + 1]
                dve.scalar_tensor_tensor(out=dst[:, SEQ:NTOK].rearrange("p (b t) -> p b t", b=NB),
                                         in0=smp(pdiff[0:rows, :]), scalar=mu, in1=smp(p),
                                         op0=ALU.mult, op1=ALU.add).then_inc(rw_mixed, 1)
                dve.drain()

            def prmb(off, n=NTOK):
                return prmT[:, off:off + KC].unsqueeze(2).broadcast_to([128, KC, n])

            dve.tensor_tensor(kkn, kR, prmb(PKK), ALU.mult)
            dve.drain()
            dve.tensor_tensor(sqk, kkn, kkn, ALU.mult).then_inc(sqk_ready, 1)

            def rwkv_arrays():
                dve.wait_ge(knorm, KC)
                dve.wait_ge(lora_out, 2 * KC)
                dve.tensor_scalar(knb, knb, 1e-12, None, ALU.max)
                dve.tensor_tensor(sqk, aR, prmb(PKA), ALU.mult)
                dve.drain()
                dve.reciprocal(knb, knb)
                dve.tensor_tensor(sqk, sqk, prmb(ONEKA), ALU.add)
                dve.drain()
                dve.tensor_tensor(kkn, kkn, knb, ALU.mult)
                dve.tensor_tensor(kR, kR, sqk, ALU.mult)
                dve.drain()
                dve.tensor_tensor(aR, kkn, aR, ALU.mult).then_inc(rw_arrays, 1)

            dve.wait_ge(c_in, 16)
            dve.wait_ge(qkw_in, 32)
            cos = const("cos").rearrange("p (t n) -> p t n", t=3)
            sin = const("sin").rearrange("p (t n) -> p t n", t=3)
            for s in range(2):
                w_lo = wqk[:, s, 0:64].unsqueeze(1).broadcast_to([128, 3, 64])
                w_hi = wqk[:, s, 64:128].unsqueeze(1).broadcast_to([128, 3, 64])
                dve.tensor_tensor(tabs[:, s, :, 0:64], w_lo, cos, ALU.mult)
                dve.tensor_tensor(tabs[:, s, :, 64:128], w_hi, cos, ALU.mult)
                dve.scalar_tensor_tensor(out=tabs[:, s, :, 128:192], in0=w_hi, scalar=-1.0, in1=sin,
                                         op0=ALU.mult, op1=ALU.mult)
                dve.tensor_tensor(tabs[:, s, :, 192:256], w_lo, sin, ALU.mult)
            dve.drain()
            for j in range(18):
                c, t = j // 3, j % 3
                rows = TILES[t][1]
                x = raw[0:rows, j % 2, :].rearrange("p (h e) -> p h e", h=HG)
                y = roped[0:rows, j % 2, :].rearrange("p (h e) -> p h e", h=HG)
                t1 = rt1[0:rows, :].rearrange("p (h e) -> p h e", h=HG)
                t2 = rt2[0:rows, :].rearrange("p (h e) -> p h e", h=HG)
                tab = tabs[0:rows, c // 3, t, :]
                bc = lambda a, n: a.unsqueeze(1).broadcast_to([rows, HG, n])
                dve.wait_ge(proj_out, j + 1)
                dve.reciprocal(hrs[0:rows, :], hms[0:rows, j % 2, :])
                dve.drain()
                dve.tensor_tensor(t1, x, hrs[0:rows, :].unsqueeze(2).broadcast_to([rows, HG, E]), ALU.mult)
                dve.drain()
                dve.tensor_tensor(t2[:, :, 0:64], t1[:, :, 64:128], bc(tab[:, 128:192], 64), ALU.mult)
                dve.tensor_tensor(t2[:, :, 64:128], t1[:, :, 0:64], bc(tab[:, 192:256], 64), ALU.mult)
                dve.drain()
                dve.tensor_tensor(t1, t1, bc(tab[:, 0:128], 128), ALU.mult)
                dve.drain()
                if j >= 2:
                    dve.wait_ge(qk_psum, j - 1)
                if k_stores_before(j):
                    dve.wait_ge(k_stored[j % 2], 16 * k_stores_before(j))
                dve.tensor_tensor(y, t1, t2, ALU.add).then_inc(rope_done, 1)
                dve.drain()
                if j == 3:
                    rwkv_arrays()

            SCALE = float(E) ** -0.5

            def masked(out, bank, mask):
                return dve.scalar_tensor_tensor(out=out, in0=bank, scalar=SCALE, in1=mask, op0=ALU.mult, op1=ALU.add)

            def normalise(u):
                i = u % 2
                w = NG * 128 * (i + 1)
                dve.wait_ge(s_exp, u + 1)
                dve.reciprocal(arden[:, i:i + 1], aden[:, i:i + 1])
                dve.drain()
                dve.tensor_scalar(pP[i][:, 0:w], pP[i][:, 0:w], arden[:, i:i + 1], None, ALU.mult).then_inc(p_ready, 1)

            dve.wait_ge(k_stored[0], 64)
            dve.wait_ge(k_stored[1], 64)
            for u in range(2 * HG):
                h, i = u // 2, u % 2
                w = NG * 128 * (i + 1)
                dve.wait_ge(s_psum, u + 1)
                if u >= 2:
                    dve.wait_ge(pt_psum, u - 1)
                if i == 0:
                    masked(pP[0], B[0][:, 0:384], const("pm0"))
                else:
                    masked(pP[1][:, 0:512], B[1][:, :], const("pm1")[:, 0:512])
                    masked(pP[1][:, 512:768], B[2][:, 0:256], const("pm1")[:, 512:768])
                dve.drain()
                dve.tensor_reduce(amax[:, i:i + 1], pP[i][:, 0:w], AX.X, ALU.max)
                dve.drain()
                dve.tensor_scalar(anmx[:, i:i + 1], amax[:, i:i + 1], -1.0, None, ALU.mult).then_inc(s_read, 1)
                if u >= 1:
                    normalise(u - 1)
            normalise(2 * HG - 1)
            for w in range(NB * HG):
                dve.wait_ge(kt_psum, 2 * w + 2)
                if w >= 2:
                    dve.wait_ge(ss_head, w - 1)
                src = B[2 * (w % 2) + 1]
                dve.tensor_copy(kTb[:, w % 2, 0, :], src[:, 0:128])
                dve.tensor_copy(kTb[:, w % 2, 5:7, :], src[:, 128:384].rearrange("p (k n) -> p k n", k=2))\
                   .then_inc(kt_out_v, 1)
            dve.wait_ge(ss_head, NB * HG)
            masked(sP, B[4][:, 0:480], const("sm"))
            dve.drain()
            dve.tensor_reduce(amax[:, 0:1], sP, AX.X, ALU.max)
            dve.drain()
            dve.tensor_scalar(anmx[:, 0:1], amax[:, 0:1], -1.0, None, ALU.mult).then_inc(ss_read, 1)
            dve.wait_ge(ss_exp, 1)
            dve.reciprocal(arden[:, 0:1], aden[:, 0:1])
            dve.drain()
            dve.wait_ge(sv_psum, NB)
            dve.tensor_scalar(osm, B[7][:, 0:E], arden[:, 0:1], None, ALU.mult).then_inc(so_read, 1)

            def prepare(c):
                if c:
                    dve.wait_ge(ch_psum, made(c - 1, "P5"))
                dve.tensor_copy(tA, sW[:, :, L * c:L * c + L])
                dve.drain()
                flat = lambda v: v.rearrange("p a b -> p (a b)")
                dve.tensor_tensor_scan(flat(tB), const("keep"), flat(tA), 0.0, ALU.mult, ALU.add)
                dve.drain()
                dve.tensor_tensor(tA, tB, tA, ALU.subtract).then_inc(cum_ready, 1)

            def operands(c):
                cs = slice(L * c, L * c + L)
                if c:
                    dve.wait_ge(ch_psum, made(c - 1, "S"))
                dve.wait_ge(exps_ready, c + 1)
                dve.scalar_tensor_tensor(out=AR[:, :, 0:NR], in0=kkn[:, :, cs], scalar=-1.0, in1=tE,
                                         op0=ALU.mult, op1=ALU.mult)
                dve.tensor_tensor(AR[:, :, NR:H2], rT[:, :, cs], tC, ALU.mult)
                dve.tensor_tensor(bh, aR[:, :, cs], tD, ALU.mult)
                dve.tensor_tensor(kh, kR[:, :, cs], tD, ALU.mult)
                dve.tensor_copy(wl[:, :].unsqueeze(2), tC[:, :, L - 1:L]).then_inc(ops_ready, 1)
                dve.drain()

            def take(c, op):
                dve.wait_ge(ch_psum, made(c, op))
                if op in ("MQ", "KQ"):
                    dst = MQ if op == "MQ" else KQ
                    mask = const("tri2").unsqueeze(1).broadcast_to([128, 4, H2])
                    for i in range(2):
                        ins = dve.tensor_tensor(dst[:, 4 * i:4 * i + 4, :],
                                                B[CH_BANK[op][i]][:, :].rearrange("p (a b) -> p a b", a=4), mask, ALU.mult)
                    if op == "MQ":
                        dve.drain()
                        ins = dve.tensor_tensor(PP[0], MP[0], const("eye2").unsqueeze(1).broadcast_to([128, KC, NR]), ALU.add)
                elif op == "N":
                    ins = dve.tensor_tensor(Nn, bank(op), const("tril").unsqueeze(1).broadcast_to([128, KC, NR]), ALU.mult)
                elif op[0] == "N":
                    ins = dve.tensor_copy(NP[int(op[1])], bank(op))
                elif op[0] == "P":
                    k = int(op[1])
                    ins = dve.tensor_tensor(PP[k], PP[k - 1], bank(op), ALU.add)
                elif op == "U":
                    ins = dve.tensor_copy(Uu, bank(op))
                else:
                    dve.tensor_tensor(ST, ST, bank(op), ALU.add)
                    dve.drain()
                    ins = dve.tensor_tensor(ST, ST, wl[:, :].unsqueeze(2).broadcast_to([128, KC, NR]), ALU.mult)
                ins.then_inc(ch_dve, 1)
                dve.drain()

            def vec_k(a, t):
                return vec[:, TS * a + t, :].unsqueeze(1).broadcast_to([128, 32, NR])

            def sample_part(n, part):
                hf, t = n // TS, n % TS
                if part == 0:
                    if n == 0:
                        dve.wait_ge(vec_in, 16 * NB)
                    if t == 0:
                        dve.wait_ge(sh_load, 16 * (hf + 1))
                    dve.tensor_tensor(stA, Sh, vec_k(4, t), ALU.mult).then_inc(st_a, 1)
                elif part == 1:
                    dve.tensor_reduce(sa_, stA, AX.X, ALU.add)
                elif part == 2:
                    dve.tensor_tensor(stA, sa_.unsqueeze(2).broadcast_to([128, 32, NR]), vec_k(5, t), ALU.mult)
                elif part == 3:
                    dve.wait_ge(st_p, n + 1)
                    dve.tensor_tensor(Sh, Sh, stA, ALU.add)
                elif part == 4:
                    dve.tensor_tensor(stA, Sh, vec_k(0, t), ALU.mult)
                else:
                    dve.tensor_reduce(ysm[:, t, 32 * hf:32 * hf + 32], stA, AX.X, ALU.add).then_inc(st_done, 1)
                dve.drain()

            dve.wait_ge(so_out, 1)
            dve.wait_ge(v_stored, 128)
            dve.memset(ST, 0.0).then_inc(st_zero, 1)
            prepare(0)
            operands(0)
            for c in range(NCH):
                for i, op in enumerate(CH_DVE):
                    take(c, op)
                    if op == "P5" and c + 1 < NCH:
                        prepare(c + 1)
                    if 1 <= i <= 12:
                        sample_part(2 * c + (i - 1) // 6, (i - 1) % 6)
                if c + 1 < NCH:
                    operands(c + 1)

            dve.wait_ge(pst_saved, 32)
            dve.wait_ge(ys_out, 1)
            dve.tensor_tensor(gpr, rT, kR, ALU.mult)
            dve.drain()
            dve.tensor_tensor(gpr, gpr, prmb(PRK), ALU.mult).then_inc(bon_ready, 1)
            for hc in range(KC):
                dve.wait_ge(gnm_psum, hc + 1)
                dve.scalar_tensor_tensor(out=kkn[:, hc, :], in0=B[4 + hc % 2][:, 0:NTOK], scalar=-1.0 / NR,
                                         in1=kkn[:, hc, :], op0=ALU.mult, op1=ALU.add).then_inc(gn_centred, 1)
            dve.wait_ge(gn_rs, KC)
            dve.reciprocal(grs, grs)
            dve.drain()
            dve.tensor_tensor(kkn, kkn, grs, ALU.mult)
            dve.drain()
            dve.tensor_tensor(kkn, kkn, prmb(LNW), ALU.mult)
            dve.drain()
            dve.tensor_tensor(kkn, kkn, prmb(LNB), ALU.add)
            for hc in range(KC):
                dve.wait_ge(bon_psum, hc + 1)
                dve.tensor_tensor(gsq[:, hc, :], B[4 + hc % 2][:, 0:NTOK], vR[:, hc, :], ALU.mult).then_inc(bon_out, 1)
            dve.drain()
            dve.tensor_tensor(kkn, kkn, gsq, ALU.add)
            dve.drain()
            for hc in range(KC):
                dve.wait_ge(gg_psum, hc + 1)
                dve.tensor_tensor(kkn[:, hc, :], kkn[:, hc, :], B[6 + hc % 2][:, 0:NTOK], ALU.mult).then_inc(y_ready, 1)
            for m in range(KC):
                dve.wait_ge(br_psum, 2 * m + 2)
                dve.tensor_tensor(mT[:, m, :], gT[:, m, :], B[2 * (m % 2)][:, 0:NTOK], ALU.mult)
                dve.tensor_tensor(gT[:, KC + m, :], gT[:, KC + m, :], B[2 * (m % 2) + 1][:, 0:NTOK], ALU.mult)
                dve.drain()
                dve.tensor_tensor(mT[:, m, :], mT[:, m, :], gT[:, KC + m, :], ALU.add).then_inc(merged, 1)
            dve.wait_ge(rest_in, 16 * 6)
            for t, (r0, rows) in enumerate(TILES):
                for c in range(2):
                    j = 2 * t + c
                    cs = slice(512 * c, 512 * c + 512)
                    dve.wait_ge(wo_psum, j + 1)
                    dve.tensor_tensor(acc[0:rows, t, cs], acc[0:rows, t, cs], B[4 + j % 4][0:rows, :], ALU.add).then_inc(h_ready, 1)
            for t, (r0, rows) in enumerate(TILES):
                dve.wait_ge(h_rms, t + 1)
                dve.reciprocal(rstd[0:rows, t:t + 1], rms[0:rows, t:t + 1])
                dve.drain()
                dve.scalar_tensor_tensor(out=hn[0:rows, t, :], in0=acc[0:rows, t, :], scalar=rstd[0:rows, t:t + 1],
                                         in1=fw[0:rows, :], op0=ALU.mult, op1=ALU.mult).then_inc(hn_ready, 1)
            dve.memset(posm, -1.0)
            dve.wait_ge(lg_psum, 1)
            for t, (r0, rows) in enumerate(TILES):
                dve.tensor_tensor(lg[0:rows, t, :], B[6][0:rows, 32 * t:32 * t + NEXP], rb[0:rows, :], ALU.add)
            dve.drain()
            for t, (r0, rows) in enumerate(TILES):
                dve.max(m8[0:rows, t, :], lg[0:rows, t, :])
            dve.drain()
            for t, (r0, rows) in enumerate(TILES):
                dve.tensor_scalar(nm8[0:rows, t:t + 1], m8[0:rows, t, 0:1], -1.0, None, ALU.mult).then_inc(lg_max, 1)
                dve.max_index(idx[0:rows, t, :], m8[0:rows, t, :], lg[0:rows, t, :])
            dve.drain()
            for t, (r0, rows) in enumerate(TILES):
                dve.tensor_copy(idxf[0:rows, t, :], idx[0:rows, t, :])
            dve.wait_ge(lg_exp, 3)
            for t, (r0, rows) in enumerate(TILES):
                dve.reciprocal(nm8[0:rows, 4 + t:5 + t], nm8[0:rows, 4 + t:5 + t])
            dve.drain()
            for t, (r0, rows) in enumerate(TILES):
                dve.tensor_scalar(g4[0:rows, t, :], g4[0:rows, t, :], nm8[0:rows, 4 + t:5 + t], None, ALU.mult)
            dve.drain()
            io32 = const("iota32")
            for t, (r0, rows) in enumerate(TILES):
                for j in range(4):
                    i_ = idxf[0:rows, t, j:j + 1]
                    if j == 0:
                        dve.tensor_scalar(mk[0:rows, t, :], io32[0:rows, :], i_, None, ALU.is_equal)
                        ins = dve.tensor_scalar(gsel[0:rows, t, :], io32[0:rows, :], i_, g4[0:rows, t, 0:1], ALU.is_equal, ALU.mult)
                    else:
                        dve.scalar_tensor_tensor(out=mk[0:rows, t, :], in0=io32[0:rows, :], scalar=i_, in1=mk[0:rows, t, :],
                                                 op0=ALU.is_equal, op1=ALU.add)
                        dve.tensor_scalar(lg[0:rows, t, :], io32[0:rows, :], i_, g4[0:rows, t, j:j + 1], ALU.is_equal, ALU.mult)
                        dve.drain()
                        ins = dve.tensor_tensor(gsel[0:rows, t, :], gsel[0:rows, t, :], lg[0:rows, t, :], ALU.add)
                    dve.drain()
                dve.drain().then_inc(mk_ready, 1)
            dve.wait_ge(pos_psum, 1)
            for t, (r0, rows) in enumerate(TILES):
                dve.tensor_tensor(posm[0:rows, t, 0:NEXP], B[7][0:rows, 32 * t:32 * t + NEXP], mk[0:rows, t, :], ALU.mult)
            dve.tensor_reduce(most[:, 0:1], B[7][:, 96:96 + NEXP], AX.X, ALU.max)
            dve.drain()
            for t, (r0, rows) in enumerate(TILES):
                dve.tensor_scalar(posm[0:rows, t, 0:NEXP], posm[0:rows, t, 0:NEXP], -1.0, None, ALU.add)
            dve.tensor_copy(most_i[:, 0:1], most[:, 0:1]).then_inc(routed, 1)
            dve.drain()

            for t, (r0, rows) in enumerate(TILES):
                for c in range(2):
                    cs = slice(512 * c, 512 * c + 512)
                    dve.wait_ge(b2_psum, 2 * t + c + 1)
                    ins = dve.tensor_tensor(acc[0:rows, t, cs], acc[0:rows, t, cs], B[2 * t + c][0:rows, :], ALU.add)
            ins.then_inc(b2_added, 1)
            dve.drain()

            dve.sem_inc(act_done, 1)
            dve.sem_inc(sc_added, 1)
            iota64 = const("iota64")

            def select(q, e):
                for t, (r0, rows) in enumerate(TILES):
                    ins = dve.tensor_scalar(selT[0:rows, t, :], iota64[0:rows, :], posm[0:rows, t, e], None, ALU.is_equal)
                ins.then_inc(sel_ready, 1)

            def dve_level(l):
                q0 = l * (NEXP + 1)
                if not isinstance(l, int):
                    dve.wait_ge(xe_psum, q0)
                    for t, (r0, rows) in enumerate(TILES):
                        dve.tensor_scalar(posm[0:rows, t, :], posm[0:rows, t, :], -float(CAP), None, ALU.add)
                    dve.drain()
                    dve.wait_ge(sc_psum, q0 * 3)
                else:
                    dve.memset(ysb, 0.0)
                    dve.drain()
                dve.memset(selGT, 0.0).then_inc(sgt_zero, 1)
                select(q0, slice(0, 1))
                with dve.Fori(0, NEXP) as e:
                    it = l * NEXP + e
                    q = q0 + e
                    dve.wait_ge(xe_psum, q + 1)
                    select(q + 1, bass.ds(e + 1, 1))
                    dve.wait_ge(sgt_psum, it + 1)
                    for t, (r0, rows) in enumerate(TILES):
                        ins = dve.tensor_scalar(selG[0:rows, t, :], iota64[0:rows, :], posm[0:rows, t, bass.ds(e, 1)],
                                                gsel[0:rows, t, bass.ds(e, 1)], ALU.is_equal, ALU.mult)
                    ins.then_inc(selg_ready, 1)
                    dve.wait_ge(moe_used, it * (NL - 1) + KC)
                    for j in range(2):
                        pair = B[j][:, :].rearrange("p (n two) -> p n two", two=2)
                        cs = slice(256 * j, 256 * j + 256)
                        ins = dve.tensor_scalar(glu[:, cs].unsqueeze(2), pair[:, :, 0:1], 7.0, None, ALU.min)
                    ins.then_inc(glu_min, 1)
                    for j in range(2):
                        pair = B[j][:, :].rearrange("p (n two) -> p n two", two=2)
                        cs = slice(256 * j, 256 * j + 256)
                        dve.tensor_scalar(lin[:, cs].unsqueeze(2), pair[:, :, 1:2], 7.0, -7.0, ALU.min, ALU.max)
                    dve.drain()
                    dve.scalar_tensor_tensor(out=lin, in0=lin, scalar=1.0, in1=glu, op0=ALU.add, op1=ALU.mult)
                    dve.drain()
                    dve.wait_ge(sg_ready, it + 2)
                    dve.tensor_tensor(act_, lin, sgm, ALU.mult).then_inc(act_done, 1)
                    for t in range(3):
                        add(q, t)
                for t in range(3):
                    add(q0 + NEXP, t)

            def add(q, t):
                r0, rows = TILES[t]
                dve.wait_ge(sc_psum, q * 3 + t + 1)
                for hh in range(2):
                    cs = slice(512 * hh, 512 * hh + 512)
                    ins = dve.tensor_tensor(acc[0:rows, t, cs], acc[0:rows, t, cs], B[6 + hh][0:rows, :], ALU.add)
                ins.then_inc(sc_added, 1)

            levels(dve, dve_level)
            dve.drain().then_inc(y_done, 1)

        @block.sync
        def _(sp):
            sp.dma_start(x_sb[:, 0, :], A["x_prompt"][0, 0:128, :]).then_inc(x_in, 16)
            sp.dma_start(x_sb[:, 1, :], A["x_prompt"][0, 128:256, :]).then_inc(x_in, 16)
            sp.dma_start(x_sb[0:NSMP, 2, :], A["x_sample"].rearrange("b t d -> (b t) d")).then_inc(x_in, 16)
            sp.dma_start(nw, row(A["attn_norm_w"], 128)).then_inc(nw_in, 16)
            sp.dma_start(xsh[0:NB, :], A["state_shift"][0]).then_inc(sh_in, 16)
            sp.dma_start(C[:, :], consts).then_inc(c_in, 16)
            sp.dma_start(wqk[:, 0, :], row(A["q_norm_w"], 128)).then_inc(qkw_in, 16)
            sp.dma_start(wqk[:, 1, :], row(A["k_norm_w"], 128)).then_inc(qkw_in, 16)
            sp.wait_ge(prm_zero, 1)
            full_mu = C_RW // 128
            sp.dma_start(prm[0:full_mu, :], A["rw_mu"][0, 0:128 * full_mu].rearrange("(k n) -> k n", n=128)).then_inc(prm_in, 16)
            sp.dma_start(prm[full_mu:NM_RW, 0:C_RW - 128 * full_mu], A["rw_mu"][0:1, 128 * full_mu:C_RW]).then_inc(prm_in, 16)
            for i, name in enumerate(("rw_w0", "rw_a0", "rw_kk", "rw_ka", "rw_lnx_w", "rw_lnx_b")):
                at = (W0, A0, PKK, PKA, LNW, LNB)[i]
                sp.dma_start(prm[at:at + KC, :], A[name][0].rearrange("(k n) -> k n", n=128)).then_inc(prm_in, 16)
            sp.dma_start(prm[PRK:PRK + KC, :], A["rw_rk"][0].rearrange("(k a) n -> k (a n)", a=2)).then_inc(prm_in, 16)
            sp.dma_start(w2a2[0:LORA, :], A["rw_w2"][0]).then_inc(w2a2_in, 16)
            sp.dma_start(w2a2[LORA:2 * LORA, :], A["rw_a2"][0]).then_inc(w2a2_in, 16)
            def move_caches():
                sp.wait_ge(vec_in, 16 * NB)
                sp.wait_ge(sh_load, 16)
                for gi in range(NG):
                    src, dst, w = A[f"cache_kv_w{WIN[gi][0]}"], O[9 + gi], CACHE[gi]
                    for b in range(NB):
                        stored(sp.dma_start(dst[0, b:b + 1, 0:w - TS].rearrange("b w a h e -> b (w a h e)"),
                                            src[0, b:b + 1, TS:w].rearrange("b w a h e -> b (w a h e)")))

            def load_rest():
                sp.wait_ge(ch_act, len(CH_ACT) * NCH + 1)
                sp.wait_ge(ys_out, 1)
                sp.wait_ge(pst_saved, 32)
                sp.dma_start(g2w[:, 0, :], A["rw_g2"][0, 0:128, :]).then_inc(g2_in, 16)
                sp.dma_start(g2w[0:32, 1, :], A["rw_g2"][0, 128:GLORA, :]).then_inc(g2_in, 16)
                sp.dma_start(acc[:, 0, :], A["x_prompt"][0, 0:128, :]).then_inc(rest_in, 16)
                sp.dma_start(acc[:, 1, :], A["x_prompt"][0, 128:256, :]).then_inc(rest_in, 16)
                sp.dma_start(acc[0:NSMP, 2, :], A["x_sample"].rearrange("b t d -> (b t) d")).then_inc(rest_in, 16)
                sp.dma_start(fw, row(A["ffn_norm_w"], 128)).then_inc(rest_in, 16)
                sp.dma_start(rwt, A["router_w"][0].rearrange("(k p) n -> p k n", p=128)).then_inc(rest_in, 16)
                sp.dma_start(rb, row(A["router_b"], 128)).then_inc(rest_in, 16)

            for n, (parts, _) in enumerate(loads):
                if n == N_GATE + NSLOT:
                    move_caches()
                if n == N_BR + 2:
                    load_rest()
                if n >= NSLOT:
                    sp.wait_ge(*loads[n - NSLOT][1])
                for dst, src in parts:
                    sp.dma_start(dst, src).then_inc(slot_full[n % NSLOT], 16)
            def load_expert(e, s):
                src = w1_v[:, e, s, :] if s < KC else w2_v[:, e, 2 * (s - KC):2 * (s - KC) + 2, :]
                dst = moe_slot(s) if s < KC else moe_slot(s, D)
                sp.dma_start(dst.unsqueeze(1), src).then_inc(slot_full[(N_BASE + s) % NSLOT], 16)

            def load_b1(e):
                src = A["moe_b1"][0, e, :].rearrange("a (h j n) -> a j h n", h=2, j=2)
                for j in range(2):
                    sp.dma_start(b1r[64 * j:64 * j + 1], src[:, j]).then_inc(b1_full, 16)

            def reuse(it, s_):
                if s_ < NL - 1:
                    sp.wait_ge(moe_used, it * (NL - 1) + (s_ + 1))
                else:
                    sp.wait_ge(ye_psum, it + 1)

            def sp_level(l):
                i0 = l * NEXP
                for s_ in range(NSLOT):
                    if isinstance(l, int):
                        sp.wait_ge(*loads[N_BASE - NSLOT + s_][1])
                    else:
                        reuse(i0 - 1, NL - NSLOT + s_)
                    load_expert(slice(0, 1), s_)
                if isinstance(l, int):
                    sp.wait_ge(hnt_out, 3)
                    sp.dma_start(b2w[0:NEXP, :], A["moe_b2"][0]).then_inc(b2_in, 16)
                load_b1(slice(0, 1))
                with sp.Fori(0, NEXP - 1) as e:
                    it = i0 + e
                    for s_ in range(NSLOT, NL):
                        reuse(it, s_ - NSLOT)
                        load_expert(bass.ds(e, 1), s_)
                        if s_ == NSLOT:
                            load_b1(bass.ds(e + 1, 1))
                    for s_ in range(NSLOT):
                        reuse(it, s_ + NL - NSLOT)
                        load_expert(bass.ds(e + 1, 1), s_)
                for s_ in range(NSLOT, NL):
                    reuse(i0 + NEXP - 1, s_ - NSLOT)
                    load_expert(slice(NEXP - 1, NEXP), s_)

            levels(sp, sp_level)
            sp.wait_ge(y_done, 1)
            for t in range(2):
                sp.dma_start(O[0][0, 128 * t:128 * t + 128, :], acc[:, t, :]).then_inc(y_saved, 16)
            sp.dma_start(O[1].rearrange("b t d -> (b t) d"), acc[0:NSMP, 2, :]).then_inc(y_saved, 16)
            sp.wait_ge(y_saved, 48)
            sp.wait_ge(xn_stored, 32)
            sp.wait_ge(v_stored, 128)
            sp.wait_ge(sh_saved, 32)
            sp.wait_ge(pst_saved, 32)
            sp.wait_ge(out_dma, 16 * n_out[0])
            sp.wait_ge(k_stored[0], 16 * 4)
            sp.wait_ge(k_stored[1], 16 * 4)


def kernel(**inputs):
    import numpy as _np
    import concourse.bacc as _bacc
    from concourse.bass_utils import run_bass_kernel_spmd as _run

    nc = _bacc.Bacc("TRN2", target_bir_lowering=False, num_devices=1)
    arrays, A = {}, {}
    for name in INS:
        a = _np.ascontiguousarray(inputs[name])
        arrays[f"in_{name}"] = a
        A[name] = nc.dram_tensor(f"in_{name}", a.shape, F32, kind="ExternalInput").ap()
    c = host_constants()
    arrays["in_consts"] = c
    consts = nc.dram_tensor("in_consts", c.shape, F32, kind="ExternalInput").ap()
    O = [nc.dram_tensor(f"out_{i}", s, F32, kind="ExternalOutput").ap() for i, s in enumerate(OUTS)]
    build(nc, A, consts, O)
    r = _run(nc, [arrays], core_ids=[0])
    return tuple(r.results[0][f"out_{i}"] for i in range(len(OUTS)))
```

```python
from contextlib import ExitStack

import concourse.bass as bass
from concourse import mybir

F32 = mybir.dt.float32
I32 = mybir.dt.int32
U32 = mybir.dt.uint32
ALU = mybir.AluOpType
ACT = mybir.ActivationFunctionType
AX = mybir.AxisListType

D = 1024
SEQ = 256
NB = 8
TS = 4
NSMP = NB * TS
NTOK = SEQ + NSMP
KC = D // 128
XC = 1 + SEQ + NB * (TS + 1)
SMP0 = 1 + SEQ
HR, NR = 16, 64
LORA = 64
GLORA = 160
C_RW = 3 * D + 2 * LORA + GLORA
NM_RW = -(-C_RW // 128)
NG, HG, E = 3, 4, 128
GW = HG * E
ATT = NG * GW
WIN = ((128, 1), (512, 4), (2048, 16))
CACHE = (128, 512, 1024)
P_TOTAL = C_RW + 3 * ATT + 2 * D
NEXP = 32
CAP = 64
LEVELS = -(-NTOK // CAP)
NEG = -1.0e30
TILES = ((0, 128), (128, 128), (256, 32))
QK_TILES = ((128, 4), (128, 4), (128, 1))
L = 64
NCH = SEQ // L
KAPPA = 0.6065306597126334

_off, _n = {}, 0
for _name, _w in (("ident", 128), ("eps", 4), ("blockones", 128), ("prefix", 128), ("ones", 128),
                  ("cos", 3 * 64), ("sin", 3 * 64), ("pm0", 384), ("pm1", 768), ("sm", 480),
                  ("tri2", 128), ("tril", 64), ("eye2", 64), ("iota64", 128), ("iota32", 32), ("keep", 512)):
    _off[_name] = (_n, _n + _w)
    _n += _w
NCONST = _n
NFIRST = 128 + 4
COFF = _off


def host_constants():
    import numpy as np
    c = np.zeros((128, NCONST), np.float32)

    def put(name, a):
        o = COFF[name]
        c[:a.shape[0], o[0]:o[1]] = a.reshape(a.shape[0], -1)

    p = np.arange(128)
    put("ident", np.eye(128))
    put("blockones", (p[:, None] // 64 == p[None] // 64) * 1.0)
    put("prefix", (p[:, None] <= p[None]) * 1.0)
    put("ones", np.ones((128, 128)))
    pos = np.zeros(3 * 128, np.float32)
    pos[:SEQ] = np.arange(SEQ)
    pos[SEQ:] = 1024 + np.arange(128) % TS
    inv = (np.float32(10000.0) ** (-np.arange(0, E, 2, dtype=np.float32) / E)).astype(np.float32)
    ang = (pos[:, None] * inv[None]).astype(np.float32)
    put("cos", np.cos(ang).reshape(3, 128, 64).transpose(1, 0, 2))
    put("sin", np.sin(ang).reshape(3, 128, 64).transpose(1, 0, 2))

    def band(q, k, window, dil):
        off = q[:, None] - k[None]
        return np.where((off >= 0) & (off <= window) & (off % dil == 0), 0.0, NEG)

    put("pm0", np.concatenate([band(p, p, *w) for w in WIN], 1))
    put("pm1", np.concatenate([band(p + 128, np.arange(256), *w) for w in WIN], 1))
    b, t = (p % 32) // TS, p % TS
    sm = np.zeros((128, 480), np.float32)
    sm[:, 0:128] = np.where(p[None] >= t[:, None], 0.0, NEG)
    sm[:, 256:384] = np.where(p[None] // 64 == t[:, None] % 2, 0.0, NEG)
    kb, kt = np.arange(NSMP) // TS, np.arange(NSMP) % TS
    for g, (window, dil) in enumerate(WIN):
        off = t[:, None] - kt[None]
        ok = (b[:, None] == kb[None]) & (off >= 0) & (off % dil == 0)
        sm[:, 384 + 32 * g:416 + 32 * g] = np.where(ok, 0.0, NEG)
    put("sm", sm)
    i, tt = p % 64, np.arange(64)
    put("tri2", np.concatenate([(i[:, None] < tt[None]) * 1.0, (i[:, None] <= tt[None]) * 1.0], 1))
    put("iota64", np.broadcast_to(np.arange(128) % 64, (128, 128)))
    put("iota32", np.broadcast_to(np.arange(32), (128, 32)))
    put("tril", (tt[None] < i[:, None]) * 1.0)
    put("eye2", (tt[None] == i[:, None]) * 1.0)
    put("keep", np.broadcast_to((np.arange(512) % L != 0) * 1.0, (128, 512)))
    put("eps", np.broadcast_to(np.array([1e-5, 64e-5, 1.0, 0.0]), (128, 4)))
    return c


INS = ["x_prompt", "x_sample", "state_wkv", "state_shift", "cache_kv_w128", "cache_kv_w512",
       "cache_kv_w2048", "attn_norm_w", "w_in", "rw_mu", "rw_w0", "rw_w2", "rw_a0", "rw_a2", "rw_g2",
       "rw_kk", "rw_ka", "rw_rk", "rw_lnx_w", "rw_lnx_b", "q_norm_w", "k_norm_w", "w_br", "w_out",
       "ffn_norm_w", "router_w", "router_b", "moe_w1", "moe_b1", "moe_w2", "moe_b2"]
OUTS = [(1, SEQ, D), (NB, TS, D), (1, 1, HR, NR, NR), (1, 1, D),
        (1, 1, 128, 2, HG, E), (1, 1, SEQ, 2, HG, E), (1, 1, SEQ, 2, HG, E),
        (1, NB, HR, NR, NR), (1, NB, D),
        (1, NB, 128, 2, HG, E), (1, NB, 512, 2, HG, E), (1, NB, 1024, 2, HG, E)]


def build(nc, A, consts, O):
    ctx = ExitStack()
    with ctx:
        def sb(name, shape, dt=F32):
            return ctx.enter_context(nc.sbuf_tensor(name, shape, dt))

        def sem(name):
            return ctx.enter_context(nc.semaphore(name))

        def row(ap, parts):
            n = ap.shape[-1]
            return bass.AP(tensor=ap.tensor, offset=ap.offset, ap=[[0, parts], [1, n]])

        B = [ctx.enter_context(nc.psum_tensor(f"bank{i}", [128, 512], F32)) for i in range(8)]

        NSLOT, SLOT = 6, 2048
        ring = sb("ring", [128, NSLOT, SLOT])
        C = sb("C", [128, NCONST])

        def const(name, rows=128):
            return C[0:rows, COFF[name][0]:COFF[name][1]]

        ident, blockones, ones = const("ident"), const("blockones"), const("ones")
        xT = sb("xT", [128, KC, XC])
        xTs = sb("xTs", [128, KC, NSMP])

        small = sb("small", [128, 64])
        POOL = 33500
        pool = sb("pool", [128, POOL])

        def span(at, *shape):
            n = 1
            for s in shape:
                n *= s
            assert at + n <= POOL, (at, n)
            v = pool[:, at:at + n]
            if len(shape) == 2:
                v = v.rearrange("p (a b) -> p a b", a=shape[0])
            if len(shape) == 3:
                v = v.rearrange("p (a b c) -> p a b c", a=shape[0], b=shape[1])
            return v

        x_sb = span(0, 3, D)
        xsh = span(3072, D)
        nw = span(4096, D)
        sqx = span(5120, D)
        qT = span(0, NG * HG, NTOK)
        kT = span(3456, NG * HG, NTOK)
        v_sb = span(6912, 3, ATT)
        raw = span(11520, 2, GW)
        roped = span(12544, 2, GW)
        rt1 = span(13568, GW)
        rt2 = span(14080, GW)
        tabs = span(14592, 2, 3, 256)
        wqk = span(16128, 2, E)
        sqh = span(16384, HG, E)
        pP = (span(11520, 384), span(11904, 768))
        pPT = (span(12672, 3, 128), span(13056, 6, 128))
        kTb = span(13824, 2, 7, 128)
        sP, sPT = span(15616, 480), span(16096, 3, 128)
        sPTn = span(11520, 3, 128)
        zb = span(31584, 2, HG, 7 * 32)
        osm = span(16480, 128)
        amax = small[:, 32:34]
        anmx, aden, arden = small[:, 34:36], small[:, 36:38], small[:, 38:40]
        tokS = span(0, 6, D)
        vec = span(6144, 6 * TS, NR)
        Sh = span(0, 32, NR)
        stA, stP = span(2048, 32, NR), span(4096, 32, NR)
        ysm = span(7680, TS, NR)
        tokY = span(0, D)
        sa_ = small[:, 0:32]
        H2 = 2 * NR
        AR = span(7936, KC, H2)
        bh, kh = span(8960, KC, NR), span(9472, KC, NR)
        MQ, KQ = span(9984, KC, H2), span(11008, KC, H2)
        Nn = span(12032, KC, NR)
        tA, tB, tC, tD, tE = [span(12544 + 512 * i, KC, NR) for i in range(5)]
        Rr, Uu, ST = [span(15104 + 512 * i, KC, NR) for i in range(3)]
        bTm, kTm, vTm = [span(31584 + 512 * i, KC, NR) for i in range(3)]
        tF = C[:, COFF["pm1"][0]:COFF["pm1"][0] + 512].rearrange("p (a b) -> p a b", a=KC)
        wl = sb("wl", [128, KC])
        gT = span(0, 2 * KC, NTOK)
        gsq, grs, gpr = [span(4608 + i * 2304, KC, NTOK) for i in range(3)]
        g2w = span(11520, 2, D)
        w_o = [span(at, 2, D) for at in (4608, 6656, 8704, 19968)]
        mT = span(13568, KC, NTOK)
        acc = span(24064, 3, D)
        fw = span(27136, D)
        rwt = span(28160, KC, NEXP)
        hn = span(16896, 3, D)
        hnT = span(0, KC, NTOK)
        t0 = 31584
        lg, mk, gsel, posm = span(t0, 3, NEXP), span(t0 + 96, 3, NEXP), span(t0 + 192, 3, NEXP), span(t0 + 288, 3, NEXP + 1)
        m8, g4 = span(t0 + 400, 3, 8), span(t0 + 448, 3, 4)
        idx = span(t0 + 464, 3, 8).bitcast(U32)
        most = span(t0 + 488, 8)
        most_i = span(t0 + 496, 8).bitcast(I32)
        nm8 = span(t0 + 504, 8)
        idx4, rb = span(t0 + 800, 3, 4), span(t0 + 812, NEXP)
        yT = span(0, KC, NTOK)
        m0 = 2304
        selT, selG = span(m0, 3, 128), span(m0 + 384, 3, 128)
        selGT = span(m0 + 768, NTOK)
        xe, xeT = span(m0 + 1152, 512), span(m0 + 1664, 4, 2, CAP)
        glu, lin, sgm, act_ = [span(m0 + 2176 + 512 * i, 512) for i in range(4)]
        actT = span(m0 + 4224, 4, 2, CAP)
        ysb = span(m0 + 4736, 512)
        chosen, gated = span(m0 + 2176, 12, NEXP), span(m0 + 2688, 12, NEXP)
        MOE_AT = [11520, 22016, 28416, None, None, None, None, None, None, 13568, 9472, 19968]
        b1r = span(m0 + 5248, 2, 512)
        b2w = span(27136, D)
        gselT = span(t0 + 512, NTOK)
        R0 = 16896
        NA = KC * NTOK
        rT, kR, vR, sW, aR, kkn = [span(R0 + i * NA, KC, NTOK) for i in range(6)]
        lo = span(R0 + 6 * NA, 3, NTOK)
        praw = span(R0 + 6 * NA + 864, 2, XC)
        pdiff = span(R0 + 6 * NA + 864 + 2 * XC, XC)
        w2a2 = span(R0 + 6 * NA + 864 + 3 * XC, D)
        sqk = span(6912, KC, NTOK)
        knb = span(6912 + NA, KC, NTOK)
        prm = span(14592, 128)
        NPRM = NM_RW + 7 * KC
        prmT = sb("prmT", [128, NPRM + KC])
        MU, W0, A0, PKK, PKA, PRK, LNW, LNB = 0, *[NM_RW + KC * i for i in range(7)]
        ONEKA = NPRM
        oT = sb("oT", [128, HG, NTOK])

        nsq, rms, rstd = small[:, 0:3], small[:, 3:6], small[:, 6:9]
        hss = small[:, 12:20].rearrange("p (i h) -> p i h", i=2)
        hms = small[:, 20:28].rearrange("p (i h) -> p i h", i=2)
        hrs = small[:, 28:32]
        eps5, eps64 = const("eps")[:, 0:1], const("eps")[:, 1:2]

        c_in, tables_in = sem("c_in"), sem("tables_in")
        x_in = sem("x_in")
        sh_in = sem("sh_in")
        nw_in = sem("nw_in")
        qkw_in = sem("qkw_in")
        slot_full = [sem(f"slot_full{i}") for i in range(NSLOT)]
        rw_psum = sem("rw_psum")
        gate_psum = sem("gate_psum")
        s_psum, s_read, s_exp, p_ready = sem("s_psum"), sem("s_read"), sem("s_exp"), sem("p_ready")
        pt_psum, pt_out, pv_psum, o_out = sem("pt_psum"), sem("pt_out"), sem("pv_psum"), sem("o_out")
        z_ready = sem("z_ready")
        kt_psum, kt_out_a, kt_out_v = sem("kt_psum"), sem("kt_out_a"), sem("kt_out_v")
        ss_head, ss_exp, ss_read = sem("ss_head"), sem("ss_exp"), sem("ss_read")
        spt_psum, spt_out, sv_psum = sem("spt_psum"), sem("spt_out"), sem("sv_psum")
        so_read, so_psum, so_out = sem("so_read"), sem("so_psum"), sem("so_out")
        v_stored = sem("v_stored")
        tk_psum, tk_out, tk_written, vec_in = sem("tk_psum"), sem("tk_out"), sem("tk_written"), sem("vec_in")
        sh_load, sh_saved = sem("sh_load"), sem("sh_saved")
        st_zero = sem("st_zero")
        st_a, st_p, st_done = sem("st_a"), sem("st_p"), sem("st_done")
        ys_written, ys_in, ys_psum, ys_out = sem("ys_written"), sem("ys_in"), sem("ys_psum"), sem("ys_out")
        cum_ready, exps_ready, ops_ready = sem("cum_ready"), sem("exps_ready"), sem("ops_ready")
        ch_psum, ch_act, ch_dve = sem("ch_psum"), sem("ch_act"), sem("ch_dve")
        pst_saved = sem("pst_saved")
        gate_out, gnm_psum, gn_centred = sem("gate_out"), sem("gnm_psum"), sem("gn_centred")
        gn_sq, gnv_psum, gn_rs = sem("gn_sq"), sem("gnv_psum"), sem("gn_rs")
        bon_ready, bon_psum, bon_out = sem("bon_ready"), sem("bon_psum"), sem("bon_out")
        gg_psum, y_ready, g2_in, rest_in = sem("gg_psum"), sem("y_ready"), sem("g2_in"), sem("rest_in")
        w_full = [sem(f"w_full{i}") for i in range(12)]
        br_psum, merged, w_o_in = sem("br_psum"), sem("merged"), sem("w_o_in")
        wo_psum, h_ready, h_rms, hn_ready = sem("wo_psum"), sem("h_ready"), sem("h_rms"), sem("hn_ready")
        hnt_psum, hnt_out, lg_psum, lg_max, lg_exp = sem("hnt_psum"), sem("hnt_out"), sem("lg_psum"), sem("lg_max"), sem("lg_exp")
        mk_ready, pos_psum, routed = sem("mk_ready"), sem("pos_psum"), sem("routed")
        moe_used, b1_full, b2_in = sem("moe_used"), sem("b1_full"), sem("b2_in")
        gt_psum, gt_out, b2_psum, b2_out = sem("gt_psum"), sem("gt_out"), sem("b2_psum"), sem("b2_out")
        sel_ready, selg_ready, xe_psum, xe_out = sem("sel_ready"), sem("selg_ready"), sem("xe_psum"), sem("xe_out")
        xet_psum, xet_out, glu_min, sg_ready = sem("xet_psum"), sem("xet_out"), sem("glu_min"), sem("sg_ready")
        act_done, at_psum, at_out = sem("act_done"), sem("at_psum"), sem("at_out")
        sgt_psum, sgt_out, ye_psum, ye_out = sem("sgt_psum"), sem("sgt_out"), sem("ye_psum"), sem("ye_out")
        sc_psum, sc_added, y_done, y_saved = sem("sc_psum"), sem("sc_added"), sem("y_done"), sem("y_saved")
        sgt_zero = sem("sgt_zero")
        yt_ready, yt_psum = sem("yt_ready"), sem("yt_psum")
        squares = sem("squares")
        xn_ready = sem("xn_ready")
        xn_stored = sem("xn_stored")
        xt_psum = sem("xt_psum")
        xt_ready = sem("xt_ready")
        zero_col = sem("zero_col")
        prm_zero, prm_in, prm_psum, prm_ready = sem("prm_zero"), sem("prm_in"), sem("prm_psum"), sem("prm_ready")
        w2a2_in = sem("w2a2_in")
        rw_raw, rw_mixed = sem("rw_raw"), sem("rw_mixed")
        lora_in, lora_psum, lora_out = sem("lora_in"), sem("lora_psum"), sem("lora_out")
        sqk_ready, sqk_psum, knorm = sem("sqk_ready"), sem("sqk_psum"), sem("knorm")
        rw_arrays = sem("rw_arrays")
        proj_psum = sem("proj_psum")
        proj_out = sem("proj_out")
        rope_done = sem("rope_done")
        qk_psum = sem("qk_psum")
        qk_out = sem("qk_out")
        k_stored = [sem("k_stored0"), sem("k_stored1")]

        out_dma = sem("out_dma")
        n_out = [0]

        def stored(dma):
            dma.then_inc(out_dma, 16)
            n_out[0] += 1

        w_in = A["w_in"][0].rearrange("(k p) n -> p k n", p=128)
        w_br = A["w_br"][0].rearrange("(k p) n -> p k n", p=128)
        w_out = A["w_out"][0].rearrange("(k p) n -> p k n", p=128)
        loads = []

        def slot(n, width=None):
            v = ring[:, n % NSLOT, :]
            return v if width is None else v.rearrange("p (k n) -> p k n", n=width)

        def add_load(parts, used):
            loads.append((parts, used))

        def w_in_cols(c0, width, used):
            for half in range(2):
                n = len(loads)
                add_load([(slot(n, GW)[:, :, 0:width], w_in[:, 4 * half:4 * half + 4, c0:c0 + width])], used)

        ATT0, GATE0 = C_RW, C_RW + 3 * ATT
        for c in range(7):
            w_in_cols(c * GW, min(GW, C_RW - c * GW), (rw_psum, min(4 * c + 4, NM_RW)))
        N_ATT = len(loads)
        for c in range(9):
            w_in_cols(ATT0 + c * GW, GW, (proj_psum, 3 * c + 3))
        N_KV = len(loads)

        def kv_views(n):
            v1 = slot(n, GW)
            v0, v2 = slot(n + 1)[:, 0:GW], slot(n + 1)[:, GW:3 * GW].rearrange("p (a n) -> p a n", a=2)
            return v0, v1, v2

        for kv in range(2):
            for b in range(NB):
                used = (kt_psum, 2 * HG * (b + 1)) if kv == 0 else (sv_psum, b + 1)
                v0, v1, v2 = kv_views(len(loads))
                c0, c1, c2 = [A[f"cache_kv_w{WIN[g][0]}"][0, b, :, kv].rearrange("w h e -> w (h e)") for g in range(3)]
                add_load([(v1, c1.rearrange("(j t) n -> j t n", t=TS))], used)
                c2 = c2.rearrange("(m u) n -> m u n", u=16)
                add_load([(v0, c0)] + [(v2[64 * t2:64 * t2 + 64], c2[:, t2:TS:2, :]) for t2 in range(2)], used)
        N_GATE = len(loads)
        for c in range(4):
            w_in_cols(GATE0 + c * GW, GW, (gate_psum, 4 * c + 4))
        N_BR = len(loads)
        for i in range(6):
            add_load([(slot(len(loads), D), w_br[:, 2 * i:2 * i + 2, :])], (br_psum, 2 * KC))
        N_BASE = len(loads)
        full = []
        per_slot = [0] * NSLOT
        for n, (parts, _) in enumerate(loads):
            per_slot[n % NSLOT] += 16 * len(parts)
            full.append(per_slot[n % NSLOT])

        NL = 12
        B2_BANK = (0, 1, 2, 3, 5, 6, 0, 1)
        w1_v = A["moe_w1"][0].rearrange("e (k p) n -> p e k n", p=128)
        w2_v = A["moe_w2"][0].rearrange("e (k p) n -> p e k n", p=128)

        def moe_slot(s, width=None):
            if MOE_AT[s] is None:
                return slot(N_BASE + s - 3, width)
            return span(MOE_AT[s], 2 * D) if width is None else span(MOE_AT[s], 2, D)

        def moe_full(it, s):
            return w_full[s], it * 16 + 16

        def levels(eng, body):
            body(0)
            eng.wait_ge(routed, 1)
            n = eng.value_load(most_i[0:1, 0:1], min_val=0, max_val=NTOK)
            with eng.If(n > CAP):
                with eng.Fori(1, LEVELS) as l:
                    with eng.If(n > l * CAP):
                        body(l)

        CH_OPS = ["MQ", "N", "KQ", "M1", "N1", "vT", "P1", "M2", "N2", "bT", "P2", "M3", "N3", "kT", "P3",
                  "M4", "N4", "P4", "N5", "P5", "R", "U", "Y", "S"]
        CH_BANK = {"MQ": (0, 1), "N": (4,), "KQ": (2, 3), "vT": (5,), "bT": (6,), "kT": (7,), "R": (6,), "U": (7,),
                   "Y": (3,), "S": (4,)}
        for k in range(1, 6):
            o = 3 * ((k + 1) % 2)
            CH_BANK[f"M{k}"], CH_BANK[f"N{k}"], CH_BANK[f"P{k}"] = (o,), (o + 1,), (o + 2,)
        CH_ACT = [x for x in CH_OPS if x in ("vT", "bT", "kT", "R", "Y") or x[0] == "M" and x != "MQ"]
        CH_DVE = [x for x in CH_OPS if x not in CH_ACT]

        def made(c, op):
            return len(CH_OPS) * c + CH_OPS.index(op) + 1

        def taken(c, op):
            if op in CH_ACT:
                return ch_act, len(CH_ACT) * c + CH_ACT.index(op) + 1
            return ch_dve, len(CH_DVE) * c + CH_DVE.index(op) + 1

        def bank(op):
            return B[CH_BANK[op][0]][:, :].rearrange("p (a b) -> p a b", a=KC)

        MP = {0: MQ[:, :, 0:NR], 1: tA, 2: tB, 3: tA, 4: tB}
        NP = {0: Nn, 1: tC, 2: tD, 3: tC, 4: tD, 5: tC}
        PP = {0: tE, 1: tF, 2: tE, 3: tF, 4: tE, 5: tF}

        scr = nc.dram_tensor("scratch_vec", (NB, 6, TS, D), F32, kind="Internal").ap()
        scr_y = nc.dram_tensor("scratch_y", (NB, TS, HR, NR), F32, kind="Internal").ap()

        block = ctx.enter_context(nc.Block())

        @block.gpsimd
        def _(pool_e):
            pool_e.wait_ge(xn_ready, 3)
            pool_e.dma_start(O[3].rearrange("a b d -> (a b) d"), x_sb[127:128, 1, :]).then_inc(xn_stored, 16)
            pool_e.dma_start(O[8][0], x_sb[TS - 1:NSMP:TS, 2, :]).then_inc(xn_stored, 16)
            for j in range(9, 18):
                g, t = (j - 9) // 3, j % 3
                r0, rows = TILES[t]
                pool_e.wait_ge(rope_done, j + 1)
                src = roped[:, j % 2, :].rearrange("p (h e) -> p h e", h=HG)
                if t < 2 and g == 0:
                    if t == 1:
                        pool_e.dma_start(O[4][0, 0, :, 0], src).then_inc(k_stored[j % 2], 16)
                elif t < 2:
                    pool_e.dma_start(O[4 + g][0, 0, r0:r0 + 128, 0], src).then_inc(k_stored[j % 2], 16)
                else:
                    dst = O[9 + g][0, :, CACHE[g] - TS:CACHE[g], 0]
                    for h in range(HG):
                        pool_e.dma_start(dst[:, :, h, :], roped[NSMP * h:NSMP * h + NSMP, j % 2, 0:E])\
                              .then_inc(k_stored[j % 2], 16)
            pool_e.wait_ge(proj_out, 27)
            for g in range(NG):
                for t in range(2):
                    src = v_sb[:, t, g * GW:(g + 1) * GW].rearrange("p (h e) -> p h e", h=HG)
                    if g == 0 and t == 0:
                        continue
                    dst = O[4][0, 0, :, 1] if g == 0 else O[4 + g][0, 0, 128 * t:128 * t + 128, 1]
                    pool_e.dma_start(dst, src).then_inc(v_stored, 16)
                pool_e.dma_start(O[9 + g][0, :, CACHE[g] - TS:CACHE[g], 1].rearrange("b t h e -> b t (h e)"),
                                 v_sb[0:NSMP, 2, g * GW:(g + 1) * GW]).then_inc(v_stored, 16)

            for n in range(2 * NB):
                b = n % NB
                z = zb[:, n % 2]
                if n < NB:
                    src = [qT[:, HG * g:HG * g + HG, SEQ + TS * b:SEQ + TS * b + TS] for g in range(NG)]
                else:
                    src = [sPT[:, g, :].rearrange("p (h k) -> p h k", h=HG)[:, :, TS * b:TS * b + TS] for g in range(NG)]
                if n == 0:
                    pool_e.wait_ge(qk_out, 9)
                    pool_e.wait_ge(rw_arrays, 1)
                elif n == NB:
                    pool_e.wait_ge(spt_out, 1)
                if 2 <= n <= NB:
                    pool_e.wait_ge(ss_head, HG * (n - 1))
                elif n == NB + 1:
                    pool_e.wait_ge(ss_head, HG * NB)
                elif n > NB + 1:
                    pool_e.wait_ge(sv_psum, n - NB - 1)
                pool_e.memset(z, 0.0)
                pool_e.drain()
                pool_e.tensor_copy(z[:, :, TS * b:TS * b + TS], src[0])
                at1 = 32 + TS * b
                pool_e.tensor_copy(z[:, :, at1:at1 + 33 * 3 + 1:33], src[1])
                for tp in range(2):
                    at2 = 32 * (5 + tp) + TS * b + 2 * tp
                    ins = pool_e.tensor_copy(z[:, :, at2:at2 + 2], src[2][:, :, 2 * tp:2 * tp + 2])
                ins.then_inc(z_ready, 1)
                pool_e.drain()
            for i in range(6):
                pool_e.wait_ge(tk_out, i + 1)
                pool_e.dma_start(scr[:, i], tokS[0:NSMP, i, :]).then_inc(tk_written, 16)
            pool_e.wait_ge(tk_written, 96)
            for b in range(NB):
                pool_e.dma_start(vec[HR * b:HR * b + HR],
                                 scr[b].rearrange("a t (h n) -> h (a t) n", n=NR)).then_inc(vec_in, 16)
            pool_e.wait_ge(vec_in, 16 * NB)
            for hf in range(2):
                if hf:
                    pool_e.wait_ge(sh_saved, 16)
                pool_e.dma_start(Sh, A["state_wkv"][0, :, :, 32 * hf:32 * hf + 32].rearrange("b h v k -> (b h) v k"))\
                      .then_inc(sh_load, 16)
                for t in range(TS):
                    n = TS * hf + t
                    pool_e.tensor_tensor(stP, vec[:, TS * 3 + t, 32 * hf:32 * hf + 32].unsqueeze(2).broadcast_to([128, 32, NR]),
                                         vec[:, TS * 2 + t, :].unsqueeze(1).broadcast_to([128, 32, NR]), ALU.mult)
                    pool_e.wait_ge(st_a, n + 1)
                    pool_e.tensor_tensor(Sh, Sh, vec[:, TS * 1 + t, :].unsqueeze(1).broadcast_to([128, 32, NR]), ALU.mult)
                    pool_e.drain()
                    pool_e.tensor_tensor(Sh, Sh, stP, ALU.add).then_inc(st_p, 1)
                    pool_e.drain()
                pool_e.wait_ge(st_done, TS * (hf + 1))
                pool_e.dma_start(O[7][0, :, :, 32 * hf:32 * hf + 32].rearrange("b h v k -> (b h) v k"), Sh).then_inc(sh_saved, 16)
            for b in range(NB):
                pool_e.dma_start(scr_y[b].rearrange("t h v -> h t v"), ysm[HR * b:HR * b + HR]).then_inc(ys_written, 16)
            pool_e.wait_ge(sh_saved, 32)
            pool_e.wait_ge(ys_written, 16 * NB)
            pool_e.dma_start(tokY[0:NSMP, :], scr_y.rearrange("b t h v -> (b t) (h v)")).then_inc(ys_in, 16)
            pool_e.wait_ge(ch_act, len(CH_ACT) * NCH + 1)
            for j in range(2):
                pool_e.dma_start(O[2][0, 0].rearrange("(c j) v k -> j v c k", j=2)[j], Rr[NR * j:NR * j + NR]).then_inc(pst_saved, 16)

        K_JOBS = [j for j in range(9, 18) if j != 9]

        def k_stores_before(j):
            return sum(HG if i % 3 == 2 else 1 for i in K_JOBS if i < j and i % 2 == j % 2)

        @block.scalar
        def _(act):
            for t, (r0, rows) in enumerate(TILES):
                act.wait_ge(x_in, 48)
                act.activation(sqx[0:rows, :], x_sb[0:rows, t, :], ACT.Square, accum_out=nsq[0:rows, t:t + 1])
                act.drain()
                if t == 0:
                    act.wait_ge(c_in, 16)
                act.activation(rms[0:rows, t:t + 1], nsq[0:rows, t:t + 1], ACT.Sqrt, scale=1.0 / D,
                               bias=eps5[0:rows, :]).then_inc(squares, 1)
            for t in range(2):
                act.wait_ge(xt_psum, t + 1)
                for kb in range(2):
                    ins = act.copy(xT[:, 4 * kb:4 * kb + 4, 1 + 128 * t:129 + 128 * t],
                                   B[2 * t + kb][:, :].rearrange("p (k n) -> p k n", k=4))
                ins.then_inc(xt_ready, 1)
            act.wait_ge(xt_psum, 3)
            smp = B[4][:, 0:KC * NSMP].rearrange("p (k n) -> p k n", k=KC)
            act.copy(xTs[:, :, :], smp)
            for b in range(NB):
                c0 = SMP0 + b * (TS + 1)
                act.copy(xT[:, :, c0 + 1:c0 + 1 + TS], smp[:, :, TS * b:TS * b + TS])
            act.wait_ge(xt_psum, 4)
            shp = B[5][:, 0:KC * NB].rearrange("p (k n) -> p k n", k=KC)
            act.copy(xT[:, :, SMP0:XC:TS + 1], shp).then_inc(xt_ready, 1)

            act.wait_ge(prm_psum, 1)
            act.copy(prmT[:, 0:NPRM], B[6][:, 0:NPRM]).then_inc(prm_ready, 1)
            for m in range(NM_RW):
                rows = min(128, C_RW - 128 * m)
                act.wait_ge(rw_psum, m + 1)
                if m >= 2:
                    act.wait_ge(rw_mixed, m - 1)
                act.copy(praw[0:rows, m % 2, :], B[m % 4][0:rows, 0:XC]).then_inc(rw_raw, 1)
            act.wait_ge(rw_mixed, NM_RW)
            act.activation(lo[0:LORA, 0, :], lo[0:LORA, 0, :], ACT.Tanh)
            act.activation(lo[:, 1, :], lo[:, 1, :], ACT.Sigmoid)
            act.activation(lo[0:32, 2, :], lo[0:32, 2, :], ACT.Sigmoid).then_inc(lora_in, 1)
            for hc in range(KC):
                for i, (dst, off) in enumerate(((sW, W0), (aR, A0))):
                    act.wait_ge(lora_psum, 2 * hc + i + 1)
                    act.activation(dst[:, hc, :], B[4 + i][:, 0:NTOK], ACT.Sigmoid,
                                   bias=prmT[:, off + hc:off + hc + 1]).then_inc(lora_out, 1)
            for hc in range(KC):
                act.wait_ge(sqk_psum, hc + 1)
                act.activation(knb[:, hc, :], B[6 + hc % 2][:, 0:NTOK], ACT.Sqrt).then_inc(knorm, 1)
            act.wait_ge(xn_stored, 32)
            def transposed(j):
                c, t = j // 3, j % 3
                r0, rows = TILES[t]
                dst = (qT, kT)[c // 3]
                act.wait_ge(qk_psum, j + 1)
                act.copy(dst[:, HG * (c % 3):HG * (c % 3) + HG, r0:r0 + rows],
                         B[4 + j % 2][:, 0:HG * rows].rearrange("p (h n) -> p h n", h=HG)).then_inc(qk_out, 1)

            for j in range(27 + 2):
                if j < 27:
                    c, t = j // 3, j % 3
                    rows, nh = QK_TILES[t] if c < 6 else (TILES[t][1], HG)
                    act.wait_ge(proj_psum, j + 1)
                    if c < 6:
                        if j >= 2:
                            act.wait_ge(rope_done, j - 1)
                        act.copy(raw[:, j % 2, 0:nh * E], B[j % 4][:, 0:nh * E])
                        for h in range(nh):
                            act.activation(sqh[0:rows, h, :], B[j % 4][0:rows, h * E:(h + 1) * E], ACT.Square,
                                           accum_out=hss[0:rows, j % 2, h:h + 1])
                        act.drain()
                        act.activation(hms[:, j % 2, 0:nh], hss[:, j % 2, 0:nh], ACT.Sqrt, scale=1.0 / E,
                                       bias=eps5).then_inc(proj_out, 1)
                    else:
                        if j == 18:
                            act.wait_ge(rw_arrays, 1)
                        dst = v_sb[0:rows, t, (c - 6) * GW:(c - 5) * GW]
                        if t < 2:
                            ins = act.copy(dst, B[j % 4][:, :])
                        else:
                            for h in range(HG):
                                ins = act.copy(dst[:, h * E:(h + 1) * E], B[j % 4][NSMP * h:NSMP * h + NSMP, 0:E])
                        ins.then_inc(proj_out, 1)
                if 2 <= j < 20:
                    transposed(j - 2)

            for u in range(2 * HG):
                h, i = u // 2, u % 2
                act.wait_ge(s_read, u + 1)
                w = NG * 128 * (i + 1)
                act.activation(pP[i][:, 0:w], pP[i][:, 0:w], ACT.Exp, bias=anmx[:, i:i + 1],
                               accum_out=aden[:, i:i + 1]).then_inc(s_exp, 1)
                act.wait_ge(pt_psum, u + 1)
                if i == 0:
                    act.copy(pPT[0], B[3][:, 0:384].rearrange("p (k n) -> p k n", k=3)).then_inc(pt_out, 1)
                else:
                    act.copy(pPT[1][:, 0:4], B[4][:, :].rearrange("p (k n) -> p k n", k=4))
                    act.copy(pPT[1][:, 4:6], B[5][:, 0:256].rearrange("p (k n) -> p k n", k=2)).then_inc(pt_out, 1)
                act.wait_ge(pv_psum, u + 1)
                act.copy(oT[:, h, 128 * i:128 * i + 128], B[6 + i][:, 0:128]).then_inc(o_out, 1)
            for w in range(NB * HG):
                act.wait_ge(kt_psum, 2 * w + 1)
                if w >= 2:
                    act.wait_ge(ss_head, w - 1)
                act.copy(kTb[:, w % 2, 1:5, :], B[2 * (w % 2)][:, :].rearrange("p (k n) -> p k n", k=4))\
                   .then_inc(kt_out_a, 1)
            act.wait_ge(ss_read, 1)
            act.activation(sP, sP, ACT.Exp, bias=anmx[:, 0:1], accum_out=aden[:, 0:1]).then_inc(ss_exp, 1)
            act.wait_ge(spt_psum, 1)
            act.copy(sPT, B[5][:, 0:384].rearrange("p (k n) -> p k n", k=3))
            act.copy(sPTn[0:NSMP], B[6][0:NSMP, 0:384].rearrange("p (k n) -> p k n", k=3)).then_inc(spt_out, 1)
            act.wait_ge(so_psum, 1)
            act.copy(oT[:, :, SEQ:NTOK], B[5][:, 0:128].rearrange("p (h n) -> p h n", h=HG)).then_inc(so_out, 1)

            def exps(c):
                act.wait_ge(cum_ready, c + 1)
                act.activation(tC, tB, ACT.Exp, scale=-KAPPA)
                act.activation(tD, tB, ACT.Exp, scale=KAPPA)
                act.activation(tE, tA, ACT.Exp, scale=-KAPPA).then_inc(exps_ready, 1)

            act.wait_ge(v_stored, 128)
            for i in range(6):
                act.wait_ge(tk_psum, i + 1)
                if i == 0:
                    act.wait_ge(so_out, 1)
                if i == 2:
                    exps(0)
                for kb in range(2):
                    src, dst = B[2 * (i % 2) + kb][0:NSMP, :], tokS[0:NSMP, i, 512 * kb:512 * kb + 512]
                    if i == 1:
                        ins = act.activation(dst, src, ACT.Exp, scale=-KAPPA)
                    else:
                        ins = act.activation(dst, src, ACT.Copy, scale=-1.0 if i == 4 else 1.0)
                ins.then_inc(tk_out, 1)

            for c in range(NCH):
                for op in CH_ACT:
                    dst = {"vT": vTm, "bT": bTm, "kT": kTm, "R": Rr, "Y": kkn[:, :, L * c:L * c + L]}.get(op)
                    act.wait_ge(ch_psum, made(c, op))
                    act.copy(dst if dst is not None else MP[int(op[1])], bank(op)).then_inc(ch_act, 1)
                    if op == "R" and c + 1 < NCH:
                        exps(c + 1)
            act.wait_ge(ch_psum, len(CH_OPS) * NCH + 1)
            act.copy(Rr, B[5][:, :].rearrange("p (a b) -> p a b", a=KC)).then_inc(ch_act, 1)
            act.wait_ge(ys_psum, 1)
            act.copy(kkn[:, :, SEQ:NTOK], B[6][:, 0:KC * NSMP].rearrange("p (a b) -> p a b", a=KC)).then_inc(ys_out, 1)

            def gate(m):
                act.wait_ge(gate_psum, m + 1)
                act.activation(gT[:, m, 0:SEQ], B[m % 4][:, 1:SMP0], ACT.Sigmoid)
                act.activation(gT[:, m, SEQ:NTOK].rearrange("p (b t) -> p b t", b=NB),
                               B[m % 4][:, SMP0:XC].rearrange("p (b u) -> p b u", b=NB)[:, :, 1:TS + 1],
                               ACT.Sigmoid).then_inc(gate_out, 1)

            for m in range(4):
                gate(m)
            act.wait_ge(pst_saved, 32)
            for hc in range(KC):
                act.wait_ge(gn_centred, hc + 1)
                act.activation(gsq[:, hc, :], kkn[:, hc, :], ACT.Square).then_inc(gn_sq, 1)
            for m in range(4, KC):
                gate(m)
            for hc in range(KC):
                act.wait_ge(gnv_psum, hc + 1)
                act.activation(grs[:, hc, :], B[6 + hc % 2][:, 0:NTOK], ACT.Sqrt, scale=1.0 / NR,
                               bias=eps64).then_inc(gn_rs, 1)
            for m in range(KC, 2 * KC):
                gate(m)
            for t, (r0, rows) in enumerate(TILES):
                act.wait_ge(h_ready, min(2 * t + 2, 5))
                act.activation(hn[0:rows, t, :], acc[0:rows, t, :], ACT.Square, accum_out=nsq[0:rows, t:t + 1])
                act.drain()
                act.activation(rms[0:rows, t:t + 1], nsq[0:rows, t:t + 1], ACT.Sqrt, scale=1.0 / D,
                               bias=eps5[0:rows, :]).then_inc(h_rms, 1)
            for t, (r0, rows) in enumerate(TILES):
                act.wait_ge(hnt_psum, t + 1)
                for kb in range(2):
                    ins = act.copy(hnT[:, 4 * kb:4 * kb + 4, r0:r0 + rows],
                                   B[2 * t + kb][:, 0:4 * rows].rearrange("p (k n) -> p k n", k=4))
                ins.then_inc(hnt_out, 1)
            for t, (r0, rows) in enumerate(TILES):
                act.wait_ge(lg_max, t + 1)
                act.activation(g4[0:rows, t, :], m8[0:rows, t, 0:4], ACT.Exp, bias=nm8[0:rows, t:t + 1],
                               accum_out=nm8[0:rows, 4 + t:5 + t]).then_inc(lg_exp, 1)
            act.wait_ge(gt_psum, 1)
            act.copy(gselT[0:NEXP, :], B[4][0:NEXP, 0:NTOK]).then_inc(gt_out, 1)
            for c in range(KC):
                act.wait_ge(b2_psum, c + 1)
                act.copy(yT[:, c, :], B[B2_BANK[c]][:, 0:NTOK]).then_inc(b2_out, 1)

            for x in (xe_out, xet_out, sg_ready, at_out, ye_out, sgt_out):
                act.sem_inc(x, 1)

            def act_gathered(q):
                act.wait_ge(xe_psum, q + 1)
                act.copy(xe, B[2][:, :]).then_inc(xe_out, 1)
                act.wait_ge(xet_psum, q + 1)
                act.copy(xeT.rearrange("p a b c -> p (a b c)"), B[3][:, :]).then_inc(xet_out, 1)

            def act_level(l):
                act_gathered(l * (NEXP + 1))
                with act.Fori(0, NEXP) as e:
                    it = l * NEXP + e
                    q = l * (NEXP + 1) + e
                    act.wait_ge(glu_min, it + 1)
                    act.activation(sgm, glu, ACT.Sigmoid, scale=1.702).then_inc(sg_ready, 1)
                    act_gathered(q + 1)
                    act.wait_ge(at_psum, it + 1)
                    act.copy(actT.rearrange("p a b c -> p (a b c)"), B[4][:, :]).then_inc(at_out, 1)
                    act.wait_ge(sc_psum, q * KC + KC)
                    act.wait_ge(ye_psum, it + 1)
                    act.copy(ysb, B[5][:, :]).then_inc(ye_out, 1)
                    act.wait_ge(sgt_psum, it + 2)
                    act.copy(selGT[:, 0:NTOK], B[3][:, 0:NTOK]).then_inc(sgt_out, 1)

            levels(act, act_level)

        @block.tensor
        def _(pe):
            pe.wait_ge(c_in, 16)
            for t in range(2):
                pe.wait_ge(xn_ready, t + 1)
                for k in range(KC):
                    mm = pe.transpose(B[2 * t + k // 4][:, 128 * (k % 4):128 * (k % 4) + 128],
                                      x_sb[:, t, 128 * k:128 * k + 128], ident)
                mm.then_inc(xt_psum, 1)
            pe.wait_ge(xn_ready, 3)
            for k in range(KC):
                mm = pe.transpose(B[4][:, NSMP * k:NSMP * k + NSMP], x_sb[0:NSMP, 2, 128 * k:128 * k + 128],
                                  ident[0:NSMP, 0:NSMP])
            mm.then_inc(xt_psum, 1)
            pe.wait_ge(sh_in, 16)
            for k in range(KC):
                mm = pe.transpose(B[5][:, NB * k:NB * k + NB], xsh[0:NB, 128 * k:128 * k + 128],
                                  ident[0:NB, 0:NB])
            mm.then_inc(xt_psum, 1)

            def turn(j):
                rows, nh = QK_TILES[j % 3]
                pe.wait_ge(rope_done, j + 1)
                if j >= 2:
                    pe.wait_ge(qk_out, j - 1)
                for h in range(nh):
                    mm = pe.transpose(B[4 + j % 2][:, h * rows:(h + 1) * rows],
                                      roped[:, j % 2, h * E:(h + 1) * E], ident)
                mm.then_inc(qk_psum, 1)

            pe.wait_ge(prm_in, 16 * 9)
            pe.transpose(B[6][:, 0:NPRM], prm[0:NPRM, :], ident[0:NPRM, 0:NPRM]).then_inc(prm_psum, 1)
            pe.wait_ge(xt_ready, 3)
            pe.wait_ge(zero_col, 1)
            for m in range(NM_RW):
                rows = min(128, C_RW - 128 * m)
                if m >= 4:
                    pe.wait_ge(rw_raw, m - 3)
                for k in range(KC):
                    n = 2 * (m // 4) + k // 4
                    if m % 4 == 0 and k % 4 == 0:
                        pe.wait_ge(slot_full[n % NSLOT], full[n])
                    mm = pe.matmul(B[m % 4][0:rows, 0:XC],
                                   slot(n, GW)[:, k % 4, 128 * (m % 4):128 * (m % 4) + rows], xT[:, k, :],
                                   start=(k == 0), stop=(k == KC - 1))
                mm.then_inc(rw_psum, 1)
            def low_rank():
                pe.wait_ge(lora_in, 1)
                pe.wait_ge(w2a2_in, 32)
                for hc in range(KC):
                    for i in range(2):
                        if hc:
                            pe.wait_ge(lora_out, 2 * hc - 1 + i)
                        p = slice(LORA * i, LORA * i + LORA)
                        pe.matmul(B[4 + i][:, 0:NTOK], w2a2[p, 128 * hc:128 * hc + 128], lo[p, 0, :],
                                  start=True, stop=True).then_inc(lora_psum, 1)
                pe.wait_ge(tables_in, 16)
                pe.wait_ge(prm_ready, 1)
                for hc in range(KC):
                    if hc == 0:
                        pe.wait_ge(sqk_ready, 1)
                    if hc >= 2:
                        pe.wait_ge(knorm, hc - 1)
                    pe.matmul(B[6 + hc % 2][:, 0:NTOK], blockones, sqk[:, hc, :], start=True, stop=True)\
                      .then_inc(sqk_psum, 1)

            pe.wait_ge(rw_raw, NM_RW)
            for c in range(9):
                for t, (r0, rows) in enumerate(TILES):
                    j = 3 * c + t
                    if j >= 4:
                        pe.wait_ge(proj_out, j - 3)
                    for k in range(KC):
                        n = N_ATT + 2 * c + k // 4
                        if t == 0 and k % 4 == 0:
                            pe.wait_ge(slot_full[n % NSLOT], full[n])
                        w = slot(n, GW)[:, k % 4, :]
                        if t == 2:
                            for h in range(HG):
                                mm = pe.matmul(B[j % 4][NSMP * h:NSMP * h + NSMP, 0:E], xTs[:, k, :],
                                               w[:, h * E:(h + 1) * E], start=(k == 0), stop=(k == KC - 1),
                                               tile_position=(0, NSMP * h), skip_group_check=True)
                            continue
                        lhs = xT[:, k, 1 + r0:1 + r0 + rows] if t < 2 else xTs[:, k, :]
                        mm = pe.matmul(B[j % 4][0:rows, :], lhs, w, start=(k == 0), stop=(k == KC - 1))
                    mm.then_inc(proj_psum, 1)
                    if j == 1:
                        low_rank()
                    if 2 <= j < 20:
                        turn(j - 2)

            def scores(u):
                h, i = u // 2, u % 2
                if u >= 2:
                    pe.wait_ge(s_read, u - 1)
                for g in range(NG):
                    w = 128 * (i + 1)
                    out = B[0][:, 128 * g:128 * g + 128] if i == 0 else B[1 + g // 2][:, 256 * (g % 2):256 * (g % 2) + 256]
                    mm = pe.matmul(out, qT[:, HG * g + h, 128 * i:128 * i + 128], kT[:, HG * g + h, 0:w],
                                   start=True, stop=True)
                mm.then_inc(s_psum, 1)

            pe.wait_ge(proj_out, 27)
            pe.wait_ge(qk_out, 18)
            scores(0)
            scores(1)
            for u in range(2 * HG):
                h, i = u // 2, u % 2
                pe.wait_ge(p_ready, u + 1)
                if u >= 2:
                    pe.wait_ge(pt_out, u - 1)
                for n in range(NG * (i + 1)):
                    out = B[3] if i == 0 else B[4 + n // 4]
                    mm = pe.transpose(out[:, 128 * (n % 4):128 * (n % 4) + 128], pP[i][:, 128 * n:128 * n + 128], ident)
                mm.then_inc(pt_psum, 1)
                if u + 2 < 2 * HG:
                    scores(u + 2)
                pe.wait_ge(pt_out, u + 1)
                if u >= 2:
                    pe.wait_ge(o_out, u - 1)
                for n in range(NG * (i + 1)):
                    g, kt = n // (i + 1), n % (i + 1)
                    mm = pe.matmul(B[6 + i][:, 0:128], v_sb[:, kt, g * GW + h * E:g * GW + h * E + E], pPT[i][:, n, :],
                                   start=(n == 0), stop=(n == NG * (i + 1) - 1))
                mm.then_inc(pv_psum, 1)

            def rows_of(bank, h):
                return bank[32 * h:32 * h + 32]

            pe.wait_ge(s_read, 2 * HG)
            pe.wait_ge(o_out, 2 * HG)
            for h in range(HG):
                for g in range(NG):
                    pe.matmul(rows_of(B[4], h)[:, 384 + 32 * g:416 + 32 * g], qT[:, HG * g + h, SEQ:NTOK],
                              kT[:, HG * g + h, SEQ:NTOK], start=(g == 0), stop=False,
                              tile_position=(0, 32 * h), skip_group_check=True)

            def turn_keys(w):
                b, h = w // HG, w % HG
                n = N_KV + 2 * b
                v0, v1, v2 = kv_views(n)
                if h == 0:
                    pe.wait_ge(slot_full[n % NSLOT], full[n])
                    pe.wait_ge(slot_full[(n + 1) % NSLOT], full[n + 1])
                if w >= 2:
                    pe.wait_ge(kt_out_a, w - 1)
                    pe.wait_ge(kt_out_v, w - 1)
                hs = slice(h * E, h * E + E)
                for t in range(TS):
                    mm = pe.transpose(B[2 * (w % 2)][:, 128 * t:128 * t + 128], v1[:, t, hs], ident)
                mm.then_inc(kt_psum, 1)
                for i, blk in enumerate((v0[:, hs], v2[:, 0, hs], v2[:, 1, hs])):
                    mm = pe.transpose(B[2 * (w % 2) + 1][:, 128 * i:128 * i + 128], blk, ident)
                mm.then_inc(kt_psum, 1)

            def cached_scores(w):
                b, h = w // HG, w % HG
                pe.wait_ge(kt_out_a, w + 1)
                pe.wait_ge(kt_out_v, w + 1)
                if h == 0:
                    pe.wait_ge(z_ready, b + 1)
                for i in range(7):
                    col = (0, 128, 128, 128, 128, 256, 256)[i]
                    mm = pe.matmul(rows_of(B[4], h)[:, col:col + 128], zb[:, b % 2, h, 32 * i:32 * i + 32],
                                   kTb[:, w % 2, i, :], start=False, stop=(b == NB - 1),
                                   tile_position=(0, 32 * h), skip_group_check=True)
                mm.then_inc(ss_head, 1)

            turn_keys(0)
            for w in range(NB * HG):
                if w + 1 < NB * HG:
                    turn_keys(w + 1)
                cached_scores(w)
            pe.wait_ge(ss_exp, 1)
            for g in range(NG):
                pe.transpose(B[5][:, 128 * g:128 * g + 128], sP[:, 128 * g:128 * g + 128], ident)
            for g in range(NG):
                mm = pe.transpose(B[6][0:NSMP, 128 * g:128 * g + 128], sP[:, 384 + 32 * g:416 + 32 * g], ident)
            mm.then_inc(spt_psum, 1)
            pe.wait_ge(spt_out, 1)
            for h in range(HG):
                for g in range(NG):
                    pe.matmul(rows_of(B[7], h)[:, 0:E], sPTn[0:NSMP, g, 32 * h:32 * h + 32],
                              v_sb[0:NSMP, 2, g * GW + h * E:g * GW + h * E + E], start=(g == 0), stop=False,
                              tile_position=(0, 32 * h), skip_group_check=True)
            for b in range(NB):
                n = N_KV + 2 * (NB + b)
                v0, v1, v2 = kv_views(n)
                pe.wait_ge(slot_full[n % NSLOT], full[n])
                pe.wait_ge(slot_full[(n + 1) % NSLOT], full[n + 1])
                pe.wait_ge(z_ready, NB + b + 1)
                for i, blk in enumerate((v0, v1[:, 0], v1[:, 1], v1[:, 2], v1[:, 3], v2[:, 0], v2[:, 1])):
                    for h in range(HG):
                        mm = pe.matmul(rows_of(B[7], h)[:, 0:E], zb[:, b % 2, h, 32 * i:32 * i + 32],
                                       blk[:, h * E:h * E + E], start=False, stop=(b == NB - 1 and i == 6),
                                       tile_position=(0, 32 * h), skip_group_check=True)
                mm.then_inc(sv_psum, 1)
            pe.wait_ge(so_read, 1)
            pe.transpose(B[5][:, 0:128], osm, ident).then_inc(so_psum, 1)

            for i, x in enumerate((rT, sW, kR, vR, kkn, aR)):
                if i >= 2:
                    pe.wait_ge(tk_out, i - 1)
                for k in range(KC):
                    mm = pe.transpose(B[2 * (i % 2) + k // 4][0:NSMP, 128 * (k % 4):128 * (k % 4) + 128],
                                      x[:, k, SEQ:NTOK], ident)
                mm.then_inc(tk_psum, 1)

            def heads(op, lhs, rhs, more=(), n=NR):
                terms = [(lhs, rhs), *more]
                for hc in range(KC):
                    for j in range(2):
                        p = slice(NR * j, NR * j + NR)
                        if n == NR:
                            out = bank(op)[p, hc, :] if op in CH_BANK else B[5][p, NR * hc:NR * hc + NR]
                        else:
                            out = B[CH_BANK[op][hc // 4]][p, n * (hc % 4):n * (hc % 4) + n]
                        for i, (x, y) in enumerate(terms):
                            mm = pe.matmul(out, x(p, hc), y(p, hc), start=(i == 0), stop=(i == len(terms) - 1),
                                           tile_position=(NR * j, NR * j))
                mm.then_inc(ch_psum, 1)

            def of(t, first=0, n=NR):
                return lambda p, hc: t[p, hc, first:first + n]

            eye = lambda p, hc: ident[p, p]
            pe.wait_ge(tk_out, 6)
            pe.wait_ge(so_out, 1)
            def gates(first, end):
                for m in range(first, end):
                    if m >= 4:
                        pe.wait_ge(gate_out, m - 3)
                    for k in range(KC):
                        n = N_GATE + 2 * (m // 4) + k // 4
                        if m % 4 == 0 and k % 4 == 0:
                            pe.wait_ge(slot_full[n % NSLOT], full[n])
                        mm = pe.matmul(B[m % 4][:, 0:XC], slot(n, GW)[:, k % 4, 128 * (m % 4):128 * (m % 4) + 128],
                                       xT[:, k, :], start=(k == 0), stop=(k == KC - 1))
                    mm.then_inc(gate_psum, 1)

            bank_free = {}
            for c in range(NCH):
                needs = {"MQ": [], "N": [], "KQ": [], "M1": [taken(c, "MQ"), taken(c, "N")], "vT": [], "bT": [], "kT": [],
                         "R": [taken(c, "KQ"), taken(c, "vT")] + ([taken(c - 1, "S")] if c else [(st_zero, 1)]),
                         "U": [taken(c, "R"), taken(c, "P5")], "Y": [taken(c, "U")], "S": [taken(c, "bT"), taken(c, "kT")]}
                for k in range(1, 6):
                    if k > 1:
                        needs[f"M{k}"] = [taken(c, f"M{k - 1}"), taken(c, f"N{k - 1}")]
                    needs[f"N{k}"] = [taken(c, f"M{k - 1}")] if k == 5 else []
                    needs[f"P{k}"] = [taken(c, f"N{k}")] + ([taken(c, f"P{k - 1}")] if k > 1 else [])
                needs["N5"] += [taken(c, "N4")]
                pe.wait_ge(ops_ready, c + 1)
                for op in CH_OPS:
                    for w in needs[op]:
                        pe.wait_ge(*w)
                    for bk in CH_BANK[op]:
                        if bk in bank_free:
                            pe.wait_ge(*bank_free[bk])
                        bank_free[bk] = taken(c, op)
                    if op == "MQ":
                        heads(op, of(bh), of(AR, 0, H2), n=H2)
                    elif op == "KQ":
                        heads(op, of(kh), of(AR, 0, H2), n=H2)
                    elif op == "N":
                        heads(op, of(AR), of(bh))
                    elif op == "vT":
                        heads(op, of(vR, L * c), eye)
                    elif op == "bT":
                        heads(op, of(bh), eye)
                    elif op == "kT":
                        heads(op, of(kh), eye)
                    elif op == "R":
                        heads(op, of(AR), of(ST), [(of(KQ), of(vTm))])
                    elif op == "U":
                        heads(op, of(PP[5]), of(Rr))
                    elif op == "Y":
                        heads(op, of(ST), of(AR, NR), [(of(Uu), of(MQ, NR)), (of(vTm), of(KQ, NR))])
                    elif op == "S":
                        heads(op, of(bTm), of(Uu), [(of(kTm), of(vTm))])
                    else:
                        k = int(op[1])
                        if op[0] == "M":
                            heads(op, of(NP[k - 1]), of(MP[k - 1]))
                        elif op[0] == "N":
                            heads(op, of(MP[k - 1]), of(NP[k - 1]))
                        else:
                            heads(op, of(NP[k]), of(PP[k - 1]))
            pe.wait_ge(*taken(NCH - 1, "S"))
            heads("OUT", of(ST), eye)
            pe.wait_ge(*taken(NCH - 1, "Y"))
            gates(0, 4)
            pe.wait_ge(ys_in, 16)
            for k in range(KC):
                mm = pe.transpose(B[6][:, NSMP * k:NSMP * k + NSMP], tokY[0:NSMP, 128 * k:128 * k + 128],
                                  ident[0:NSMP, 0:NSMP])
            mm.then_inc(ys_psum, 1)

            def head_sums(x, banks, out_sem, free_sem, ready=None):
                for hc in range(KC):
                    if ready is not None:
                        pe.wait_ge(ready, hc + 1)
                    if hc >= 2:
                        pe.wait_ge(free_sem, hc - 1)
                    pe.matmul(B[banks + hc % 2][:, 0:NTOK], blockones, x[:, hc, :], start=True, stop=True)\
                      .then_inc(out_sem, 1)

            gates(4, 6)
            pe.wait_ge(ys_out, 1)
            pe.wait_ge(ch_act, len(CH_ACT) * NCH + 1)
            head_sums(kkn, 4, gnm_psum, gn_centred)
            gates(6, 8)
            head_sums(gsq, 6, gnv_psum, gn_rs, gn_sq)
            gates(8, 14)
            pe.wait_ge(bon_ready, 1)
            pe.wait_ge(gn_centred, KC)
            head_sums(gpr, 4, bon_psum, bon_out)
            gates(14, 16)
            pe.wait_ge(g2_in, 32)
            pe.wait_ge(gn_rs, KC)
            for hc in range(KC):
                if hc >= 2:
                    pe.wait_ge(y_ready, hc - 1)
                pe.matmul(B[6 + hc % 2][:, 0:NTOK], g2w[:, 0, 128 * hc:128 * hc + 128], lo[:, 1, :],
                          start=True, stop=False)
                pe.matmul(B[6 + hc % 2][:, 0:NTOK], g2w[0:32, 1, 128 * hc:128 * hc + 128], lo[0:32, 2, :],
                          start=False, stop=True).then_inc(gg_psum, 1)

            pe.wait_ge(y_ready, KC)
            pe.wait_ge(gate_out, 2 * KC)
            for n in range(N_BR, N_BR + 6):
                pe.wait_ge(slot_full[n % NSLOT], full[n])
            for m in range(KC):
                if m >= 2:
                    pe.wait_ge(merged, m - 1)
                for br, (k0, kn, x) in enumerate(((0, KC, kkn), (KC, HG, oT))):
                    for k in range(kn):
                        w = slot(N_BR + (k0 + k) // 2, D)[:, (k0 + k) % 2, 128 * m:128 * m + 128]
                        mm = pe.matmul(B[2 * (m % 2) + br][:, 0:NTOK], w, x[:, k, :], start=(k == 0), stop=(k == kn - 1))
                    mm.then_inc(br_psum, 1)
            pe.wait_ge(merged, KC)
            pe.wait_ge(w_o_in, 16 * 4)
            for j in range(4):
                t, c = j // 2, j % 2
                for k in range(KC):
                    mm = pe.matmul(B[4 + j][:, :], mT[:, k, 128 * t:128 * t + 128],
                                   w_o[k // 2][:, k % 2, 512 * c:512 * c + 512], start=(k == 0), stop=(k == KC - 1))
                mm.then_inc(wo_psum, 1)
            pe.wait_ge(h_ready, 1)
            for k in range(KC):
                for g in range(4):
                    mm = pe.matmul(B[4][NSMP * g:NSMP * g + NSMP, 0:256], mT[:, k, SEQ:NTOK],
                                   w_o[k // 2][:, k % 2, 256 * g:256 * g + 256], start=(k == 0), stop=(k == KC - 1),
                                   tile_position=(0, NSMP * g), skip_group_check=True)
            mm.then_inc(wo_psum, 1)
            for t, (r0, rows) in enumerate(TILES):
                pe.wait_ge(hn_ready, t + 1)
                if t == 2:
                    pe.wait_ge(h_ready, 5)
                for k in range(KC):
                    mm = pe.transpose(B[2 * t + k // 4][:, rows * (k % 4):rows * (k % 4) + rows],
                                      hn[0:rows, t, 128 * k:128 * k + 128], ident[0:rows, 0:rows])
                mm.then_inc(hnt_psum, 1)
            for t, (r0, rows) in enumerate(TILES):
                pe.wait_ge(hnt_out, t + 1)
                for k in range(KC):
                    mm = pe.matmul(B[6][0:rows, 32 * t:32 * t + NEXP], hnT[:, k, r0:r0 + rows], rwt[:, k, :],
                                   start=(k == 0), stop=(k == KC - 1))
            mm.then_inc(lg_psum, 1)
            pe.wait_ge(mk_ready, 1)
            for t, (r0, rows) in enumerate(TILES):
                for u in range(t + 1):
                    urows = TILES[u][1]
                    lhs = (const("prefix", urows)[:, 0:rows] if u == t else ones[0:urows, 0:rows])
                    pe.matmul(B[7][0:rows, 32 * t:32 * t + NEXP], lhs, mk[0:urows, u, :], start=(u == 0), stop=(u == t))
            for u in range(3):
                urows = TILES[u][1]
                mm = pe.matmul(B[7][:, 96:96 + NEXP], ones[0:urows, :], mk[0:urows, u, :], start=(u == 0), stop=(u == 2))
            mm.then_inc(pos_psum, 1)
            pe.wait_ge(mk_ready, 2)
            for t, (r0, rows) in enumerate(TILES):
                mm = pe.transpose(B[4][0:NEXP, r0:r0 + rows], gsel[0:rows, t, :], ident[0:rows, 0:rows])
            mm.then_inc(gt_psum, 1)
            pe.wait_ge(gt_out, 1)
            pe.wait_ge(b2_in, 16)
            for c in range(KC):
                if c >= 6:
                    pe.wait_ge(b2_out, c - 5)
                pe.matmul(B[B2_BANK[c]][:, 0:NTOK], b2w[0:NEXP, 128 * c:128 * c + 128], gselT[0:NEXP, :],
                          start=True, stop=True).then_inc(b2_psum, 1)
            pe.wait_ge(b2_out, KC)
            pe.sem_inc(sgt_psum, 1)

            def gather(q):
                pe.wait_ge(sel_ready, q + 1)
                pe.wait_ge(xe_out, q + 1)
                for t, (r0, rows) in enumerate(TILES):
                    for hh in range(2):
                        mm = pe.matmul(B[2][CAP * hh:CAP * hh + CAP, :], selT[0:rows, t, CAP * hh:CAP * hh + CAP],
                                       hn[0:rows, t, 512 * hh:512 * hh + 512], start=(t == 0), stop=(t == 2),
                                       tile_position=(0, CAP * hh), skip_group_check=True)
                mm.then_inc(xe_psum, 1)

            def turn_gathered(q, it):
                pe.wait_ge(xe_out, q + 2)
                pe.wait_ge(sgt_out, it + 1)
                for c in range(4):
                    mm = pe.transpose(B[3][:, 128 * c:128 * c + 128], xe[:, 128 * c:128 * c + 128], ident)
                mm.then_inc(xet_psum, 1)

            def scatter(q, chunks):
                for c in chunks:
                    hh, col = c // 4, 128 * (c % 4)
                    p = slice(CAP * hh, CAP * hh + CAP)
                    pe.wait_ge(sc_added, q * KC + c + 1)
                    pe.matmul(B[6 + c % 2][:, 0:NTOK], ysb[p, col:col + 128], selGT[p, :], start=True, stop=True,
                              tile_position=(CAP * hh, 0)).then_inc(sc_psum, 1)

            def pe_level(l):
                q0 = l * (NEXP + 1)
                pe.wait_ge(sgt_zero, l + 1)
                gather(q0)
                turn_gathered(q0, l * NEXP)
                with pe.Fori(0, NEXP) as e:
                    it = l * NEXP + e
                    q = q0 + e
                    pe.wait_ge(b1_full, it * 32 + 32)
                    pe.wait_ge(act_done, it + 1)
                    for hh in range(2):
                        for j in range(2):
                            p = 64 * j
                            pe.matmul(B[j][CAP * hh:CAP * hh + CAP, :], ones[p:p + 1, 0:CAP],
                                      b1r[p:p + 1, hh, :], start=True, stop=False,
                                      tile_position=(p, CAP * hh), skip_group_check=True)
                    pe.wait_ge(xet_out, q + 2)
                    for k in range(KC):
                        pe.wait_ge(*moe_full(it, k))
                        w = moe_slot(k)
                        for j in range(2):
                            for hh in range(2):
                                mm = pe.matmul(B[j][CAP * hh:CAP * hh + CAP, :], xeT[:, k % 4, k // 4, :],
                                               w[:, D * hh + 512 * j:D * hh + 512 * j + 512], start=False,
                                               stop=(k == KC - 1), tile_position=(0, CAP * hh), skip_group_check=True)
                        mm.then_inc(moe_used, 1)
                    gather(q + 1)
                    pe.wait_ge(sgt_out, it + 1)
                    pe.wait_ge(ye_out, it + 1)
                    scatter(q, (0, 1))
                    turn_gathered(q + 1, it)
                    pe.wait_ge(act_done, it + 2)
                    pe.wait_ge(at_out, it + 1)
                    for c in range(4):
                        mm = pe.transpose(B[4][:, 128 * c:128 * c + 128], act_[:, 128 * c:128 * c + 128], ident)
                    mm.then_inc(at_psum, 1)
                    scatter(q, (2, 3))
                    pe.wait_ge(at_out, it + 2)
                    for k in range(KC):
                        if k % 2 == 0:
                            pe.wait_ge(*moe_full(it, KC + k // 2))
                        for hh in range(2):
                            mm = pe.matmul(B[5][CAP * hh:CAP * hh + CAP, :], actT[:, k % 4, k // 4, :],
                                           moe_slot(KC + k // 2, D)[:, k % 2, 512 * hh:512 * hh + 512], start=(k == 0),
                                           stop=(k == KC - 1), tile_position=(0, CAP * hh), skip_group_check=True)
                        if k % 2 == 1 and k < KC - 1:
                            mm.then_inc(moe_used, 1)
                        if k == 3:
                            scatter(q, (4, 5))
                    mm.then_inc(ye_psum, 1)
                    scatter(q, (6, 7))
                    pe.wait_ge(selg_ready, it + 1)
                    pe.wait_ge(xet_out, q + 3)
                    for t, (r0, rows) in enumerate(TILES):
                        mm = pe.transpose(B[3][:, r0:r0 + rows], selG[0:rows, t, :], ident[0:rows, 0:rows])
                    mm.then_inc(sgt_psum, 1)
                pe.wait_ge(ye_out, l * NEXP + NEXP + 1)
                pe.wait_ge(sgt_out, l * NEXP + NEXP + 1)
                scatter(q0 + NEXP, range(KC))

            levels(pe, pe_level)
            pe.wait_ge(yt_ready, 1)
            for t, (r0, rows) in enumerate(TILES):
                for c in range(KC):
                    mm = pe.transpose(B[2 * t + c // 4][0:rows, 128 * (c % 4):128 * (c % 4) + 128],
                                      yT[:, c, r0:r0 + rows], ident)
                mm.then_inc(yt_psum, 1)

        @block.vector
        def _(dve):
            dve.memset(xT[:, :, 0:1], 0.0).then_inc(zero_col, 1)
            dve.memset(prm[0:NPRM, :], 0.0).then_inc(prm_zero, 1)
            dve.wait_ge(nw_in, 16)
            for t, (r0, rows) in enumerate(TILES):
                dve.wait_ge(squares, t + 1)
                dve.reciprocal(rstd[0:rows, t:t + 1], rms[0:rows, t:t + 1])
                dve.drain()
                dve.scalar_tensor_tensor(out=x_sb[0:rows, t, :], in0=x_sb[0:rows, t, :],
                                         scalar=rstd[0:rows, t:t + 1], in1=nw[0:rows, :],
                                         op0=ALU.mult, op1=ALU.mult).then_inc(xn_ready, 1)
            dve.wait_ge(prm_ready, 1)
            dve.tensor_scalar(prmT[:, ONEKA:ONEKA + KC], prmT[:, PKA:PKA + KC], -1.0, 1.0, ALU.mult, ALU.add)
            for m in range(NM_RW):
                rows = min(128, C_RW - 128 * m)
                p = praw[0:rows, m % 2, :]
                dst = ((rT, kR, vR)[m // KC][:, m % KC, :] if m < 3 * KC else lo[:, m - 3 * KC, :])[0:rows, :]
                mu = prmT[0:rows, MU + m:MU + m + 1]
                dve.wait_ge(rw_raw, m + 1)
                dve.tensor_tensor(pdiff[0:rows, 1:XC], p[:, 0:XC - 1], p[:, 1:XC], ALU.subtract)
                dve.drain()
                dve.scalar_tensor_tensor(out=dst[:, 0:SEQ], in0=pdiff[0:rows, 1:SMP0], scalar=mu,
                                         in1=p[:, 1:SMP0], op0=ALU.mult, op1=ALU.add)
                smp = lambda v: v[:, SMP0:XC].rearrange("p (b u) -> p b u", b=NB)[:, :, 1:TS + 1]
                dve.scalar_tensor_tensor(out=dst[:, SEQ:NTOK].rearrange("p (b t) -> p b t", b=NB),
                                         in0=smp(pdiff[0:rows, :]), scalar=mu, in1=smp(p),
                                         op0=ALU.mult, op1=ALU.add).then_inc(rw_mixed, 1)
                dve.drain()

            def prmb(off, n=NTOK):
                return prmT[:, off:off + KC].unsqueeze(2).broadcast_to([128, KC, n])

            dve.tensor_tensor(kkn, kR, prmb(PKK), ALU.mult)
            dve.drain()
            dve.tensor_tensor(sqk, kkn, kkn, ALU.mult).then_inc(sqk_ready, 1)

            def rwkv_arrays(part):
                if part == 0:
                    dve.wait_ge(lora_out, 2 * KC)
                    dve.tensor_tensor(sqk, aR, prmb(PKA), ALU.mult)
                elif part == 1:
                    dve.tensor_tensor(sqk, sqk, prmb(ONEKA), ALU.add)
                elif part == 2:
                    dve.tensor_tensor(kR, kR, sqk, ALU.mult)
                elif part == 3:
                    dve.wait_ge(knorm, KC)
                    dve.tensor_scalar(knb, knb, 1e-12, None, ALU.max)
                elif part == 4:
                    dve.reciprocal(knb, knb)
                elif part == 5:
                    dve.tensor_tensor(kkn, kkn, knb, ALU.mult)
                else:
                    dve.tensor_tensor(aR, kkn, aR, ALU.mult).then_inc(rw_arrays, 1)
                dve.drain()

            dve.wait_ge(tables_in, 16)
            dve.wait_ge(qkw_in, 32)
            cos = const("cos").rearrange("p (t n) -> p t n", t=3)
            sin = const("sin").rearrange("p (t n) -> p t n", t=3)
            for s in range(2):
                w_lo = wqk[:, s, 0:64].unsqueeze(1).broadcast_to([128, 3, 64])
                w_hi = wqk[:, s, 64:128].unsqueeze(1).broadcast_to([128, 3, 64])
                dve.tensor_tensor(tabs[:, s, :, 0:64], w_lo, cos, ALU.mult)
                dve.tensor_tensor(tabs[:, s, :, 64:128], w_hi, cos, ALU.mult)
                dve.scalar_tensor_tensor(out=tabs[:, s, :, 128:192], in0=w_hi, scalar=-1.0, in1=sin,
                                         op0=ALU.mult, op1=ALU.mult)
                dve.tensor_tensor(tabs[:, s, :, 192:256], w_lo, sin, ALU.mult)
            dve.drain()
            for j in range(18):
                c, t = j // 3, j % 3
                rows, nh = QK_TILES[t]
                x = raw[:, j % 2, 0:nh * E].rearrange("p (h e) -> p h e", h=nh)
                y = roped[:, j % 2, 0:nh * E].rearrange("p (h e) -> p h e", h=nh)
                t1 = rt1[:, 0:nh * E].rearrange("p (h e) -> p h e", h=nh)
                t2 = rt2[:, 0:nh * E].rearrange("p (h e) -> p h e", h=nh)
                tab = tabs[:, c // 3, t, :]
                bc = lambda a, n: a.unsqueeze(1).broadcast_to([rows, nh, n])
                dve.wait_ge(proj_out, j + 1)
                dve.reciprocal(hrs[:, 0:nh], hms[:, j % 2, 0:nh])
                dve.drain()
                dve.tensor_tensor(t1, x, hrs[:, 0:nh].unsqueeze(2).broadcast_to([rows, nh, E]), ALU.mult)
                dve.drain()
                dve.tensor_tensor(t2[:, :, 0:64], t1[:, :, 64:128], bc(tab[:, 128:192], 64), ALU.mult)
                dve.tensor_tensor(t2[:, :, 64:128], t1[:, :, 0:64], bc(tab[:, 192:256], 64), ALU.mult)
                dve.drain()
                dve.tensor_tensor(t1, t1, bc(tab[:, 0:128], 128), ALU.mult)
                dve.drain()
                if j >= 2:
                    dve.wait_ge(qk_psum, j - 1)
                if k_stores_before(j):
                    dve.wait_ge(k_stored[j % 2], 16 * k_stores_before(j))
                dve.tensor_tensor(y, t1, t2, ALU.add).then_inc(rope_done, 1)
                dve.drain()
                if 3 <= j < 10:
                    rwkv_arrays(j - 3)

            SCALE = float(E) ** -0.5

            def masked(out, bank, mask):
                return dve.scalar_tensor_tensor(out=out, in0=bank, scalar=SCALE, in1=mask, op0=ALU.mult, op1=ALU.add)

            def normalise(u):
                i = u % 2
                w = NG * 128 * (i + 1)
                dve.wait_ge(s_exp, u + 1)
                dve.reciprocal(arden[:, i:i + 1], aden[:, i:i + 1])
                dve.drain()
                dve.tensor_scalar(pP[i][:, 0:w], pP[i][:, 0:w], arden[:, i:i + 1], None, ALU.mult).then_inc(p_ready, 1)

            for i in range(2):
                dve.wait_ge(k_stored[i], 16 * k_stores_before(18 + i))
            for u in range(2 * HG):
                h, i = u // 2, u % 2
                w = NG * 128 * (i + 1)
                dve.wait_ge(s_psum, u + 1)
                if u >= 2:
                    dve.wait_ge(pt_psum, u - 1)
                if i == 0:
                    masked(pP[0], B[0][:, 0:384], const("pm0"))
                else:
                    masked(pP[1][:, 0:512], B[1][:, :], const("pm1")[:, 0:512])
                    masked(pP[1][:, 512:768], B[2][:, 0:256], const("pm1")[:, 512:768])
                dve.drain()
                dve.tensor_reduce(amax[:, i:i + 1], pP[i][:, 0:w], AX.X, ALU.max)
                dve.drain()
                dve.tensor_scalar(anmx[:, i:i + 1], amax[:, i:i + 1], -1.0, None, ALU.mult).then_inc(s_read, 1)
                if u >= 1:
                    normalise(u - 1)
            normalise(2 * HG - 1)
            for w in range(NB * HG):
                dve.wait_ge(kt_psum, 2 * w + 2)
                if w >= 2:
                    dve.wait_ge(ss_head, w - 1)
                src = B[2 * (w % 2) + 1]
                dve.tensor_copy(kTb[:, w % 2, 0, :], src[:, 0:128])
                dve.tensor_copy(kTb[:, w % 2, 5:7, :], src[:, 128:384].rearrange("p (k n) -> p k n", k=2))\
                   .then_inc(kt_out_v, 1)
            dve.wait_ge(ss_head, NB * HG)
            masked(sP, B[4][:, 0:480], const("sm"))
            dve.drain()
            dve.tensor_reduce(amax[:, 0:1], sP, AX.X, ALU.max)
            dve.drain()
            dve.tensor_scalar(anmx[:, 0:1], amax[:, 0:1], -1.0, None, ALU.mult).then_inc(ss_read, 1)
            dve.wait_ge(ss_exp, 1)
            dve.reciprocal(arden[:, 0:1], aden[:, 0:1])
            dve.drain()
            dve.wait_ge(sv_psum, NB)
            dve.tensor_scalar(osm, B[7][:, 0:E], arden[:, 0:1], None, ALU.mult).then_inc(so_read, 1)

            def prepare(c):
                if c:
                    dve.wait_ge(ch_psum, made(c - 1, "P5"))
                dve.tensor_copy(tA, sW[:, :, L * c:L * c + L])
                dve.drain()
                flat = lambda v: v.rearrange("p a b -> p (a b)")
                dve.tensor_tensor_scan(flat(tB), const("keep"), flat(tA), 0.0, ALU.mult, ALU.add)
                dve.drain()
                dve.tensor_tensor(tA, tB, tA, ALU.subtract).then_inc(cum_ready, 1)

            def operands(c):
                cs = slice(L * c, L * c + L)
                dve.wait_ge(exps_ready, c + 1)
                if c:
                    dve.wait_ge(ch_psum, made(c - 1, "kT"))
                dve.tensor_tensor(bh, aR[:, :, cs], tD, ALU.mult)
                dve.tensor_tensor(kh, kR[:, :, cs], tD, ALU.mult)
                if c:
                    dve.wait_ge(ch_psum, made(c - 1, "Y"))
                dve.scalar_tensor_tensor(out=AR[:, :, 0:NR], in0=kkn[:, :, cs], scalar=-1.0, in1=tE,
                                         op0=ALU.mult, op1=ALU.mult)
                dve.tensor_tensor(AR[:, :, NR:H2], rT[:, :, cs], tC, ALU.mult).then_inc(ops_ready, 1)

            def last_decay():
                dve.tensor_copy(wl[:, :].unsqueeze(2), tC[:, :, L - 1:L])
                dve.drain()

            def take(c, op):
                dve.wait_ge(ch_psum, made(c, op))
                if op in ("MQ", "KQ"):
                    dst = MQ if op == "MQ" else KQ
                    mask = const("tri2").unsqueeze(1).broadcast_to([128, 4, H2])
                    for i in range(2):
                        ins = dve.tensor_tensor(dst[:, 4 * i:4 * i + 4, :],
                                                B[CH_BANK[op][i]][:, :].rearrange("p (a b) -> p a b", a=4), mask, ALU.mult)
                    if op == "MQ":
                        dve.drain()
                        ins = dve.tensor_tensor(PP[0], MP[0], const("eye2").unsqueeze(1).broadcast_to([128, KC, NR]), ALU.add)
                elif op == "N":
                    ins = dve.tensor_tensor(Nn, bank(op), const("tril").unsqueeze(1).broadcast_to([128, KC, NR]), ALU.mult)
                elif op[0] == "N":
                    ins = dve.tensor_copy(NP[int(op[1])], bank(op))
                elif op[0] == "P":
                    k = int(op[1])
                    ins = dve.tensor_tensor(PP[k], PP[k - 1], bank(op), ALU.add)
                elif op == "U":
                    ins = dve.tensor_copy(Uu, bank(op))
                else:
                    dve.tensor_tensor(ST, ST, bank(op), ALU.add)
                    dve.drain()
                    ins = dve.tensor_tensor(ST, ST, wl[:, :].unsqueeze(2).broadcast_to([128, KC, NR]), ALU.mult)
                ins.then_inc(ch_dve, 1)
                dve.drain()

            def vec_k(a, t):
                return vec[:, TS * a + t, :].unsqueeze(1).broadcast_to([128, 32, NR])

            def sample_part(n, part):
                hf, t = n // TS, n % TS
                if part == 0:
                    if n == 0:
                        dve.wait_ge(vec_in, 16 * NB)
                    if t == 0:
                        dve.wait_ge(sh_load, 16 * (hf + 1))
                    dve.tensor_tensor(stA, Sh, vec_k(4, t), ALU.mult).then_inc(st_a, 1)
                elif part == 1:
                    dve.tensor_reduce(sa_, stA, AX.X, ALU.add)
                elif part == 2:
                    dve.tensor_tensor(stA, sa_.unsqueeze(2).broadcast_to([128, 32, NR]), vec_k(5, t), ALU.mult)
                elif part == 3:
                    dve.wait_ge(st_p, n + 1)
                    dve.tensor_tensor(Sh, Sh, stA, ALU.add)
                elif part == 4:
                    dve.tensor_tensor(stA, Sh, vec_k(0, t), ALU.mult)
                else:
                    dve.tensor_reduce(ysm[:, t, 32 * hf:32 * hf + 32], stA, AX.X, ALU.add).then_inc(st_done, 1)
                dve.drain()

            dve.wait_ge(so_out, 1)
            dve.wait_ge(v_stored, 128)
            after = [(0, i) for i in range(7, 15)] + [(c, i) for c in range(1, NCH) for i in range(1, 15)]
            half = 6 * TS
            part_after = dict(zip(after, [*range(half), None, None, *range(half, 2 * half)]))
            dve.memset(ST, 0.0).then_inc(st_zero, 1)
            prepare(0)
            operands(0)
            last_decay()
            for c in range(NCH):
                for i, op in enumerate(CH_DVE):
                    if op == "S" and c + 1 < NCH:
                        operands(c + 1)
                    take(c, op)
                    if op == "P5" and c + 1 < NCH:
                        prepare(c + 1)
                    part = part_after.get((c, i))
                    if part is not None:
                        sample_part(part // 6, part % 6)
                if c + 1 < NCH:
                    last_decay()

            dve.wait_ge(pst_saved, 32)
            dve.wait_ge(ys_out, 1)
            dve.tensor_tensor(gpr, rT, kR, ALU.mult)
            dve.drain()
            dve.tensor_tensor(gpr, gpr, prmb(PRK), ALU.mult).then_inc(bon_ready, 1)
            for hc in range(KC):
                dve.wait_ge(gnm_psum, hc + 1)
                dve.scalar_tensor_tensor(out=kkn[:, hc, :], in0=B[4 + hc % 2][:, 0:NTOK], scalar=-1.0 / NR,
                                         in1=kkn[:, hc, :], op0=ALU.mult, op1=ALU.add).then_inc(gn_centred, 1)
            dve.wait_ge(gn_rs, KC)
            dve.reciprocal(grs, grs)
            dve.drain()
            dve.tensor_tensor(kkn, kkn, grs, ALU.mult)
            dve.drain()
            dve.tensor_tensor(kkn, kkn, prmb(LNW), ALU.mult)
            dve.drain()
            dve.tensor_tensor(kkn, kkn, prmb(LNB), ALU.add)
            for hc in range(KC):
                dve.wait_ge(bon_psum, hc + 1)
                dve.tensor_tensor(gsq[:, hc, :], B[4 + hc % 2][:, 0:NTOK], vR[:, hc, :], ALU.mult).then_inc(bon_out, 1)
            dve.drain()
            dve.tensor_tensor(kkn, kkn, gsq, ALU.add)
            dve.drain()
            for hc in range(KC):
                dve.wait_ge(gg_psum, hc + 1)
                dve.tensor_tensor(kkn[:, hc, :], kkn[:, hc, :], B[6 + hc % 2][:, 0:NTOK], ALU.mult).then_inc(y_ready, 1)
            for m in range(KC):
                dve.wait_ge(br_psum, 2 * m + 2)
                dve.tensor_tensor(mT[:, m, :], gT[:, m, :], B[2 * (m % 2)][:, 0:NTOK], ALU.mult)
                dve.tensor_tensor(gT[:, KC + m, :], gT[:, KC + m, :], B[2 * (m % 2) + 1][:, 0:NTOK], ALU.mult)
                dve.drain()
                dve.tensor_tensor(mT[:, m, :], mT[:, m, :], gT[:, KC + m, :], ALU.add).then_inc(merged, 1)
            dve.wait_ge(rest_in, 16 * 6)
            for j in range(4):
                t, cs = j // 2, slice(512 * (j % 2), 512 * (j % 2) + 512)
                dve.wait_ge(wo_psum, j + 1)
                dve.tensor_tensor(acc[:, t, cs], acc[:, t, cs], B[4 + j][:, :], ALU.add).then_inc(h_ready, 1)
            dve.wait_ge(wo_psum, 5)
            for g in range(4):
                cs = slice(256 * g, 256 * g + 256)
                ins = dve.tensor_tensor(acc[0:NSMP, 2, cs], acc[0:NSMP, 2, cs],
                                        B[4][NSMP * g:NSMP * g + NSMP, 0:256], ALU.add)
            ins.then_inc(h_ready, 1)
            for t, (r0, rows) in enumerate(TILES):
                dve.wait_ge(h_rms, t + 1)
                dve.reciprocal(rstd[0:rows, t:t + 1], rms[0:rows, t:t + 1])
                dve.drain()
                dve.scalar_tensor_tensor(out=hn[0:rows, t, :], in0=acc[0:rows, t, :], scalar=rstd[0:rows, t:t + 1],
                                         in1=fw[0:rows, :], op0=ALU.mult, op1=ALU.mult).then_inc(hn_ready, 1)
            dve.memset(posm, -1.0)
            dve.memset(idx4, 0.0)
            dve.memset(g4, 0.0)
            dve.wait_ge(lg_psum, 1)
            for t, (r0, rows) in enumerate(TILES):
                dve.tensor_tensor(lg[0:rows, t, :], B[6][0:rows, 32 * t:32 * t + NEXP], rb[0:rows, :], ALU.add)
            dve.drain()
            for t, (r0, rows) in enumerate(TILES):
                dve.max(m8[0:rows, t, :], lg[0:rows, t, :])
            dve.drain()
            for t, (r0, rows) in enumerate(TILES):
                dve.tensor_scalar(nm8[0:rows, t:t + 1], m8[0:rows, t, 0:1], -1.0, None, ALU.mult).then_inc(lg_max, 1)
                dve.max_index(idx[0:rows, t, :], m8[0:rows, t, :], lg[0:rows, t, :])
            dve.drain()
            for t, (r0, rows) in enumerate(TILES):
                dve.tensor_copy(idx4[0:rows, t, :], idx[0:rows, t, 0:4])
            dve.wait_ge(lg_exp, 3)
            for t, (r0, rows) in enumerate(TILES):
                dve.reciprocal(nm8[0:rows, 4 + t:5 + t], nm8[0:rows, 4 + t:5 + t])
            dve.drain()
            for t, (r0, rows) in enumerate(TILES):
                dve.tensor_scalar(g4[0:rows, t, :], g4[0:rows, t, :], nm8[0:rows, 4 + t:5 + t], None, ALU.mult)
            wide = lambda v: v.rearrange("p t j -> p (t j)").unsqueeze(2).broadcast_to([128, 12, NEXP])
            over = lambda v: v.rearrange("p (t j) n -> p t n j", j=4)
            dve.tensor_tensor(chosen, const("iota32").unsqueeze(1).broadcast_to([128, 12, NEXP]), wide(idx4), ALU.is_equal)
            dve.drain()
            dve.tensor_tensor(gated, chosen, wide(g4), ALU.mult)
            dve.tensor_reduce(mk, over(chosen), AX.X, ALU.add).then_inc(mk_ready, 1)
            dve.drain()
            dve.tensor_reduce(gsel, over(gated), AX.X, ALU.add).then_inc(mk_ready, 1)
            dve.drain()
            dve.wait_ge(pos_psum, 1)
            for t, (r0, rows) in enumerate(TILES):
                dve.tensor_tensor(posm[0:rows, t, 0:NEXP], B[7][0:rows, 32 * t:32 * t + NEXP], mk[0:rows, t, :], ALU.mult)
            dve.tensor_reduce(most[:, 0:1], B[7][:, 96:96 + NEXP], AX.X, ALU.max)
            dve.drain()
            for t, (r0, rows) in enumerate(TILES):
                dve.tensor_scalar(posm[0:rows, t, 0:NEXP], posm[0:rows, t, 0:NEXP], -1.0, None, ALU.add)
            dve.tensor_copy(most_i[:, 0:1], most[:, 0:1]).then_inc(routed, 1)
            dve.drain()

            dve.sem_inc(act_done, 1)
            dve.sem_inc(sc_added, 2)
            iota64 = const("iota64")

            def select(q, e):
                for t, (r0, rows) in enumerate(TILES):
                    ins = dve.tensor_scalar(selT[0:rows, t, :], iota64[0:rows, :], posm[0:rows, t, e], None, ALU.is_equal)
                ins.then_inc(sel_ready, 1)

            def dve_level(l):
                q0 = l * (NEXP + 1)
                if not isinstance(l, int):
                    dve.wait_ge(xe_psum, q0)
                    for t, (r0, rows) in enumerate(TILES):
                        dve.tensor_scalar(posm[0:rows, t, :], posm[0:rows, t, :], -float(CAP), None, ALU.add)
                    dve.drain()
                    dve.wait_ge(sc_psum, q0 * KC)
                else:
                    dve.memset(ysb, 0.0)
                    dve.drain()
                dve.memset(selGT, 0.0).then_inc(sgt_zero, 1)
                select(q0, slice(0, 1))
                with dve.Fori(0, NEXP) as e:
                    it = l * NEXP + e
                    q = q0 + e
                    dve.wait_ge(xe_psum, q + 1)
                    select(q + 1, bass.ds(e + 1, 1))
                    dve.wait_ge(sgt_psum, it + 1)
                    for t, (r0, rows) in enumerate(TILES):
                        ins = dve.tensor_scalar(selG[0:rows, t, :], iota64[0:rows, :], posm[0:rows, t, bass.ds(e, 1)],
                                                gsel[0:rows, t, bass.ds(e, 1)], ALU.is_equal, ALU.mult)
                    ins.then_inc(selg_ready, 1)
                    dve.wait_ge(moe_used, it * (NL - 1) + KC)
                    for j in range(2):
                        pair = B[j][:, :].rearrange("p (n two) -> p n two", two=2)
                        cs = slice(256 * j, 256 * j + 256)
                        ins = dve.tensor_scalar(glu[:, cs].unsqueeze(2), pair[:, :, 0:1], 7.0, None, ALU.min)
                    ins.then_inc(glu_min, 1)
                    for j in range(2):
                        pair = B[j][:, :].rearrange("p (n two) -> p n two", two=2)
                        cs = slice(256 * j, 256 * j + 256)
                        dve.tensor_scalar(lin[:, cs].unsqueeze(2), pair[:, :, 1:2], 7.0, -7.0, ALU.min, ALU.max)
                    dve.drain()
                    dve.scalar_tensor_tensor(out=lin, in0=lin, scalar=1.0, in1=glu, op0=ALU.add, op1=ALU.mult)
                    dve.drain()
                    dve.wait_ge(sg_ready, it + 2)
                    dve.tensor_tensor(act_, lin, sgm, ALU.mult).then_inc(act_done, 1)
                    for c in range(KC):
                        add(q, c)
                for c in range(KC):
                    add(q0 + NEXP, c)

            def add(q, c):
                dve.wait_ge(sc_psum, q * KC + c + 1)
                dve.tensor_tensor(yT[:, c, :], yT[:, c, :], B[6 + c % 2][:, 0:NTOK], ALU.add).then_inc(sc_added, 1)

            levels(dve, dve_level)
            dve.drain().then_inc(yt_ready, 1)
            for t, (r0, rows) in enumerate(TILES):
                dve.wait_ge(yt_psum, t + 1)
                for c in range(2):
                    cs = slice(512 * c, 512 * c + 512)
                    ins = dve.tensor_tensor(acc[0:rows, t, cs], acc[0:rows, t, cs], B[2 * t + c][0:rows, :], ALU.add)
                ins.then_inc(y_done, 1)

        @block.sync
        def _(sp):
            sp.dma_start(C[:, 0:NFIRST], consts[:, 0:NFIRST]).then_inc(c_in, 16)
            sp.dma_start(x_sb[:, 0, :], A["x_prompt"][0, 0:128, :]).then_inc(x_in, 16)
            sp.dma_start(x_sb[:, 1, :], A["x_prompt"][0, 128:256, :]).then_inc(x_in, 16)
            sp.dma_start(x_sb[0:NSMP, 2, :], A["x_sample"].rearrange("b t d -> (b t) d")).then_inc(x_in, 16)
            sp.dma_start(nw, row(A["attn_norm_w"], 128)).then_inc(nw_in, 16)
            sp.dma_start(xsh[0:NB, :], A["state_shift"][0]).then_inc(sh_in, 16)
            sp.dma_start(C[:, NFIRST:], consts[:, NFIRST:]).then_inc(tables_in, 16)
            sp.dma_start(wqk[:, 0, :], row(A["q_norm_w"], 128)).then_inc(qkw_in, 16)
            sp.dma_start(wqk[:, 1, :], row(A["k_norm_w"], 128)).then_inc(qkw_in, 16)
            sp.wait_ge(prm_zero, 1)
            full_mu = C_RW // 128
            sp.dma_start(prm[0:full_mu, :], A["rw_mu"][0, 0:128 * full_mu].rearrange("(k n) -> k n", n=128)).then_inc(prm_in, 16)
            sp.dma_start(prm[full_mu:NM_RW, 0:C_RW - 128 * full_mu], A["rw_mu"][0:1, 128 * full_mu:C_RW]).then_inc(prm_in, 16)
            for i, name in enumerate(("rw_w0", "rw_a0", "rw_kk", "rw_ka", "rw_lnx_w", "rw_lnx_b")):
                at = (W0, A0, PKK, PKA, LNW, LNB)[i]
                sp.dma_start(prm[at:at + KC, :], A[name][0].rearrange("(k n) -> k n", n=128)).then_inc(prm_in, 16)
            sp.dma_start(prm[PRK:PRK + KC, :], A["rw_rk"][0].rearrange("(k a) n -> k (a n)", a=2)).then_inc(prm_in, 16)
            sp.dma_start(w2a2[0:LORA, :], A["rw_w2"][0]).then_inc(w2a2_in, 16)
            sp.dma_start(w2a2[LORA:2 * LORA, :], A["rw_a2"][0]).then_inc(w2a2_in, 16)
            def move_caches():
                sp.wait_ge(vec_in, 16 * NB)
                sp.wait_ge(sh_load, 16)
                for gi in range(NG):
                    src, dst, w = A[f"cache_kv_w{WIN[gi][0]}"], O[9 + gi], CACHE[gi]
                    for b in range(NB):
                        stored(sp.dma_start(dst[0, b:b + 1, 0:w - TS].rearrange("b w a h e -> b (w a h e)"),
                                            src[0, b:b + 1, TS:w].rearrange("b w a h e -> b (w a h e)")))

            def load_rest():
                sp.wait_ge(ch_act, len(CH_ACT) * NCH + 1)
                sp.wait_ge(ys_out, 1)
                sp.wait_ge(pst_saved, 32)
                sp.dma_start(g2w[:, 0, :], A["rw_g2"][0, 0:128, :]).then_inc(g2_in, 16)
                sp.dma_start(g2w[0:32, 1, :], A["rw_g2"][0, 128:GLORA, :]).then_inc(g2_in, 16)
                sp.dma_start(acc[:, 0, :], A["x_prompt"][0, 0:128, :]).then_inc(rest_in, 16)
                sp.dma_start(acc[:, 1, :], A["x_prompt"][0, 128:256, :]).then_inc(rest_in, 16)
                sp.dma_start(acc[0:NSMP, 2, :], A["x_sample"].rearrange("b t d -> (b t) d")).then_inc(rest_in, 16)
                sp.dma_start(fw, row(A["ffn_norm_w"], 128)).then_inc(rest_in, 16)
                sp.dma_start(rwt, A["router_w"][0].rearrange("(k p) n -> p k n", p=128)).then_inc(rest_in, 16)
                sp.dma_start(rb, row(A["router_b"], 128)).then_inc(rest_in, 16)

            for n, (parts, _) in enumerate(loads):
                if n == N_BR + 2:
                    load_rest()
                if n == N_GATE + NSLOT:
                    move_caches()
                if n >= NSLOT:
                    sp.wait_ge(*loads[n - NSLOT][1])
                for dst, src in parts:
                    sp.dma_start(dst, src).then_inc(slot_full[n % NSLOT], 16)
            def load_expert(e, s):
                src = w1_v[:, e, s, :] if s < KC else w2_v[:, e, 2 * (s - KC):2 * (s - KC) + 2, :]
                dst = moe_slot(s) if s < KC else moe_slot(s, D)
                sp.dma_start(dst.unsqueeze(1), src).then_inc(w_full[s], 16)

            def load_b1(e):
                src = A["moe_b1"][0, e, :].rearrange("a (h j n) -> a j h n", h=2, j=2)
                for j in range(2):
                    sp.dma_start(b1r[64 * j:64 * j + 1], src[:, j]).then_inc(b1_full, 16)

            def reuse(it, s_):
                if s_ < NL - 1:
                    sp.wait_ge(moe_used, it * (NL - 1) + (s_ + 1))
                else:
                    sp.wait_ge(ye_psum, it + 1)

            def sp_level(l):
                i0 = l * NEXP
                for s_ in range(NL):
                    if isinstance(l, int):
                        if s_ == 0:
                            sp.wait_ge(y_ready, KC)
                            for i in range(4):
                                sp.dma_start(w_o[i], w_out[:, 2 * i:2 * i + 2, :]).then_inc(w_o_in, 16)
                        elif s_ == 2:
                            sp.wait_ge(br_psum, 2 * KC)
                        elif s_ == 9:
                            sp.wait_ge(wo_psum, 5)
                    else:
                        reuse(i0 - 1, s_)
                    load_expert(slice(0, 1), s_)
                if isinstance(l, int):
                    sp.wait_ge(hn_ready, 3)
                    sp.dma_start(b2w[0:NEXP, :], A["moe_b2"][0]).then_inc(b2_in, 16)
                load_b1(slice(0, 1))
                with sp.Fori(0, NEXP - 1) as e:
                    for s_ in range(NL):
                        reuse(i0 + e, s_)
                        load_expert(bass.ds(e + 1, 1), s_)
                        if s_ == 0:
                            load_b1(bass.ds(e + 1, 1))

            levels(sp, sp_level)
            for t in range(2):
                sp.wait_ge(y_done, t + 1)
                sp.dma_start(O[0][0, 128 * t:128 * t + 128, :], acc[:, t, :]).then_inc(y_saved, 16)
            sp.wait_ge(y_done, 3)
            sp.dma_start(O[1].rearrange("b t d -> (b t) d"), acc[0:NSMP, 2, :]).then_inc(y_saved, 16)
            sp.wait_ge(y_saved, 48)
            sp.wait_ge(xn_stored, 32)
            sp.wait_ge(v_stored, 128)
            sp.wait_ge(sh_saved, 32)
            sp.wait_ge(pst_saved, 32)
            sp.wait_ge(out_dma, 16 * n_out[0])
            for i in range(2):
                sp.wait_ge(k_stored[i], 16 * k_stores_before(18 + i))


def kernel(**inputs):
    import numpy as _np
    import concourse.bacc as _bacc
    from concourse.bass_utils import run_bass_kernel_spmd as _run

    nc = _bacc.Bacc("TRN2", target_bir_lowering=False, num_devices=1)
    arrays, A = {}, {}
    for name in INS:
        a = _np.ascontiguousarray(inputs[name])
        arrays[f"in_{name}"] = a
        A[name] = nc.dram_tensor(f"in_{name}", a.shape, F32, kind="ExternalInput").ap()
    c = host_constants()
    arrays["in_consts"] = c
    consts = nc.dram_tensor("in_consts", c.shape, F32, kind="ExternalInput").ap()
    O = [nc.dram_tensor(f"out_{i}", s, F32, kind="ExternalOutput").ap() for i, s in enumerate(OUTS)]
    build(nc, A, consts, O)
    r = _run(nc, [arrays], core_ids=[0])
    return tuple(r.results[0][f"out_{i}"] for i in range(len(OUTS)))
```
